# Optimizing a Trainium2 kernel written in Bass

```python
import jax, jax.numpy as jnp
from jax import lax
import numpy as np

D_MODEL = 1024
BATCH = 1
SEQ = 512
DEPTH = 2

CTX_LEN = 256
GRID_W = 64
BLOCK = 128
WINDOW = 128
ROPE_BASE = 10000.0
EPS = 1e-6
N_MOD = 6
D_FF = 4 * D_MODEL

A_HEADS = 4
A_HEAD_DIM = D_MODEL // 8
A_WIDTH = A_HEADS * A_HEAD_DIM
A_GATES = 4 * A_HEADS
B_HEADS = 8
B_KV_HEADS = 2
B_HEAD_DIM = D_MODEL // 16
B_WIDTH = B_HEADS * B_HEAD_DIM
B_KV_WIDTH = B_KV_HEADS * B_HEAD_DIM
AB_IN = 4 * A_WIDTH + A_GATES + B_WIDTH + 2 * B_KV_WIDTH
AB_OUT = A_WIDTH + B_WIDTH
C_HEADS = 8
C_KV_HEADS = 2
C_HEAD_DIM = D_MODEL // 8
C_WIDTH = C_HEADS * C_HEAD_DIM
C_KV_WIDTH = C_KV_HEADS * C_HEAD_DIM
C_IN = C_WIDTH + 2 * C_KV_WIDTH


def rms_norm(x, g):
    xf = x.astype(jnp.float32)
    y = xf * lax.rsqrt(jnp.mean(xf * xf, axis=-1, keepdims=True) + EPS)
    return (y * g.astype(jnp.float32)).astype(x.dtype)

def modulate(x, g, mod, i):
    return rms_norm(x, g) * (1 + mod[:, :, i + 1]) + mod[:, :, i]

def sq_relu_mlp(h, w1, w2):
    return jnp.square(jax.nn.relu(h @ w1)) @ w2

def axial_rope_tables(n_tokens, head_dim):
    rows = n_tokens // GRID_W
    row = jnp.broadcast_to(jnp.arange(rows)[:, None], (rows, GRID_W)).reshape(n_tokens).astype(jnp.float32)
    col = jnp.broadcast_to(jnp.arange(GRID_W)[None, :], (rows, GRID_W)).reshape(n_tokens).astype(jnp.float32)
    pairs_per_axis = head_dim // 4
    inv_freq = ROPE_BASE ** (-jnp.arange(pairs_per_axis, dtype=jnp.float32) / pairs_per_axis)
    ang = jnp.concatenate([row[:, None] * inv_freq, col[:, None] * inv_freq], axis=-1)
    return jnp.cos(ang), jnp.sin(ang)

def apply_rope(x, cos, sin):
    half = x.shape[-1] // 2
    xf = x.astype(jnp.float32)
    x1, x2 = xf[..., :half], xf[..., half:]
    cs, sn = cos[:, None, :], sin[:, None, :]
    return jnp.concatenate([x1 * cs - x2 * sn, x2 * cs + x1 * sn], axis=-1).astype(x.dtype)

def gqa_attend(q, k, v, sink=None):
    b, tq, hq, d = q.shape
    hkv = k.shape[2]
    g = hq // hkv
    s = jnp.einsum('bqhgd,bkhd->bhgqk', q.reshape(b, tq, hkv, g, d), k).astype(jnp.float32) * d ** -0.5
    if sink is None:
        p = jax.nn.softmax(s, axis=-1)
    else:
        s_sink = jnp.broadcast_to(sink.astype(jnp.float32).reshape(1, hkv, g, 1, 1), s.shape[:-1] + (1,))
        p = jax.nn.softmax(jnp.concatenate([s, s_sink], axis=-1), axis=-1)[..., :-1]
    o = jnp.einsum('bhgqk,bkhd->bqhgd', p.astype(v.dtype), v)
    return o.reshape(b, tq, hq * d)

def banded_window_attention(q, k, v, k_ctx, v_ctx, sink):
    b, t, hq, d = q.shape
    hkv = k.shape[2]
    g = hq // hkv
    nb = t // BLOCK
    n_ctx = k_ctx.shape[1]
    nw = 3 * BLOCK
    scale = d ** -0.5
    qb = jnp.moveaxis(q.reshape(b, nb, BLOCK, hkv, g, d), 1, 0)

    def band(a):
        a = jnp.pad(a, ((0, 0), (BLOCK, BLOCK), (0, 0), (0, 0))).reshape(b, nb + 2, BLOCK, hkv, d)
        a = jnp.concatenate([a[:, :-2], a[:, 1:-1], a[:, 2:]], axis=2)
        return jnp.moveaxis(a, 1, 0)

    kw, vw = band(k), band(v)
    qpos = jnp.arange(nb)[:, None, None] * BLOCK + jnp.arange(BLOCK)[None, :, None]
    kpos = (jnp.arange(nb)[:, None, None] - 1) * BLOCK + jnp.arange(nw)[None, None, :]
    valid = (jnp.abs(kpos - qpos) <= WINDOW) & (kpos >= 0) & (kpos < t)
    sink_l = sink.astype(jnp.float32).reshape(1, hkv, g, 1, 1)

    def one_block(args):
        qn, kn, vn, valid_n = args
        s_win = jnp.einsum('bqhgd,bkhd->bhgqk', qn, kn).astype(jnp.float32) * scale
        s_win = jnp.where(valid_n, s_win, -jnp.inf)
        s_ctx = jnp.einsum('bqhgd,bchd->bhgqc', qn, k_ctx).astype(jnp.float32) * scale
        s_sink = jnp.broadcast_to(sink_l, s_win.shape[:-1] + (1,))
        p = jax.nn.softmax(jnp.concatenate([s_win, s_ctx, s_sink], axis=-1), axis=-1).astype(v.dtype)
        o = (jnp.einsum('bhgqk,bkhd->bqhgd', p[..., :nw], vn)
             + jnp.einsum('bhgqc,bchd->bqhgd', p[..., nw:nw + n_ctx], v_ctx))
        return o.reshape(b, BLOCK, hq * d)

    o = lax.map(one_block, (qb, kw, vw, valid))
    return jnp.moveaxis(o, 0, 1).reshape(b, t, hq * d)

def mlstm_dir(q, k, v, log_i, log_f, state):
    n_chunks = q.shape[2] // BLOCK

    def to_chunks(a):
        a = a.reshape(a.shape[:2] + (n_chunks, BLOCK) + a.shape[3:])
        return jnp.moveaxis(a, 2, 0)

    lower = jnp.tril(jnp.ones((BLOCK, BLOCK), dtype=bool))

    def step(carry, inp):
        c_mat, n_vec, m = carry
        qc, kc, vc, ic, fc = inp
        bcum = jnp.cumsum(fc, axis=-1)
        d_log = jnp.where(lower, bcum[..., :, None] - bcum[..., None, :] + ic[..., None, :], -jnp.inf)
        inter_log = bcum + m[..., None]
        m_t = jnp.maximum(inter_log, jnp.max(d_log, axis=-1))
        inter_w = jnp.exp(inter_log - m_t)
        s = jnp.einsum('bhtd,bhsd->bhts', qc, kc) * jnp.exp(d_log - m_t[..., None])
        num = inter_w[..., None] * jnp.einsum('bhtd,bhde->bhte', qc, c_mat) + jnp.einsum('bhts,bhse->bhte', s, vc)
        den = inter_w * jnp.einsum('bhtd,bhd->bht', qc, n_vec) + jnp.sum(s, axis=-1)
        h = num / jnp.maximum(jnp.abs(den), jnp.exp(-m_t))[..., None]
        b_last = bcum[..., -1]
        w_log = b_last[..., None] - bcum + ic
        m_new = jnp.maximum(b_last + m, jnp.max(w_log, axis=-1))
        carry_w = jnp.exp(b_last + m - m_new)
        w = jnp.exp(w_log - m_new[..., None])
        c_new = carry_w[..., None, None] * c_mat + jnp.einsum('bhs,bhsd,bhse->bhde', w, kc, vc)
        n_new = carry_w[..., None] * n_vec + jnp.einsum('bhs,bhsd->bhd', w, kc)
        return (c_new, n_new, m_new), h

    state, h = lax.scan(step, state, (to_chunks(q), to_chunks(k), to_chunks(v), to_chunks(log_i), to_chunks(log_f)))
    h = jnp.moveaxis(h, 0, 2)
    return h.reshape(h.shape[:2] + (-1, h.shape[-1])), state

def mlstm_bidir(q, k, v, gates, state_f, state_b):
    li_f, lf_f, li_b, lf_b = gates
    h_f, st_f = mlstm_dir(q, k, v, li_f, lf_f, state_f)
    flip = lambda a: jnp.flip(a, axis=2)
    h_b, st_b = mlstm_dir(flip(q), flip(k), flip(v), flip(li_b), flip(lf_b), state_b)
    return h_f + flip(h_b), st_f, st_b

def ab_mixer(h_ctx, h_lat, w_in, gate_b, a_norm_g, q_norm_g, k_norm_g, sink, w_out, need_ctx):
    batch = h_lat.shape[0]
    sizes = [A_WIDTH] * 4 + [A_GATES, B_WIDTH, B_KV_WIDTH]
    bounds = [int(s) for s in np.cumsum(sizes)]

    def project(h):
        t = h.shape[1]
        qa, ka, va, oa, ga, qb, kb, vb = jnp.split(h @ w_in, bounds, axis=-1)
        heads_a = lambda a: a.reshape(batch, t, A_HEADS, A_HEAD_DIM).transpose(0, 2, 1, 3).astype(jnp.float32)
        qa, ka, va = heads_a(qa), heads_a(ka) * A_HEAD_DIM ** -0.5, heads_a(va)
        g = (ga + gate_b).astype(jnp.float32).reshape(batch, t, 4, A_HEADS).transpose(2, 0, 3, 1)
        gates = (g[0], jax.nn.log_sigmoid(g[1]), g[2], jax.nn.log_sigmoid(g[3]))
        qb = rms_norm(qb.reshape(batch, t, B_HEADS, B_HEAD_DIM), q_norm_g)
        kb = rms_norm(kb.reshape(batch, t, B_KV_HEADS, B_HEAD_DIM), k_norm_g)
        vb = vb.reshape(batch, t, B_KV_HEADS, B_HEAD_DIM)
        return (qa, ka, va, gates), oa, (qb, kb, vb)

    def mlstm_out(h, oa):
        h = rms_norm(h.transpose(0, 2, 1, 3), a_norm_g.reshape(A_HEADS, A_HEAD_DIM))
        return (h.reshape(h.shape[0], h.shape[1], A_WIDTH) * jax.nn.sigmoid(oa)).astype(oa.dtype)

    a_c, oa_c, (qb_c, kb_c, vb_c) = project(h_ctx)
    a_l, oa_l, (qb_l, kb_l, vb_l) = project(h_lat)
    zero = (jnp.zeros((batch, A_HEADS, A_HEAD_DIM, A_HEAD_DIM), jnp.float32),
            jnp.zeros((batch, A_HEADS, A_HEAD_DIM), jnp.float32),
            jnp.zeros((batch, A_HEADS), jnp.float32))
    ha_c, st_f, st_b = mlstm_bidir(*a_c, zero, zero)
    ha_l, _, _ = mlstm_bidir(*a_l, st_f, st_b)
    cos, sin = axial_rope_tables(h_lat.shape[1], B_HEAD_DIM)
    qb_l, kb_l = apply_rope(qb_l, cos, sin), apply_rope(kb_l, cos, sin)
    ob_l = banded_window_attention(qb_l, kb_l, vb_l, kb_c, vb_c, sink)
    y_lat = jnp.concatenate([mlstm_out(ha_l, oa_l), ob_l.astype(oa_l.dtype)], axis=-1) @ w_out
    y_ctx = None
    if need_ctx:
        ob_c = gqa_attend(qb_c, kb_c, vb_c, sink)
        y_ctx = jnp.concatenate([mlstm_out(ha_c, oa_c), ob_c.astype(oa_c.dtype)], axis=-1) @ w_out
    return y_ctx, y_lat

def c_mixer(h_ctx, h_lat, w_in, q_norm_g, k_norm_g, w_out, need_ctx):
    def project(h):
        b, t, _ = h.shape
        q, k, v = jnp.split(h @ w_in, [C_WIDTH, C_WIDTH + C_KV_WIDTH], axis=-1)
        q = rms_norm(q.reshape(b, t, C_HEADS, C_HEAD_DIM), q_norm_g)
        k = rms_norm(k.reshape(b, t, C_KV_HEADS, C_HEAD_DIM), k_norm_g)
        return q, k, v.reshape(b, t, C_KV_HEADS, C_HEAD_DIM)

    q_c, k_c, v_c = project(h_ctx)
    q_l, k_l, v_l = project(h_lat)
    b, t = h_lat.shape[:2]
    cos, sin = axial_rope_tables(t, C_HEAD_DIM)
    q_l, k_l = apply_rope(q_l, cos, sin), apply_rope(k_l, cos, sin)
    k_all = jnp.concatenate([k_c, k_l], axis=1)
    v_all = jnp.concatenate([v_c, v_l], axis=1)
    q_blocks = jnp.moveaxis(q_l.reshape(b, t // BLOCK, BLOCK, C_HEADS, C_HEAD_DIM), 1, 0)
    o = lax.map(lambda qb: gqa_attend(qb, k_all, v_all), q_blocks)
    y_lat = jnp.moveaxis(o, 0, 1).reshape(b, t, C_WIDTH) @ w_out
    y_ctx = gqa_attend(q_c, k_c, v_c) @ w_out if need_ctx else None
    return y_ctx, y_lat

def first_inputs(seed: int = 0) -> dict:
    key = jax.random.key(seed)
    ks = jax.random.split(key, 24)
    n_even = (DEPTH + 1) // 2
    n_odd = DEPTH // 2
    f32 = jnp.float32
    nrm = lambda k, shape, scale: jax.random.normal(k, shape, f32) * scale
    gain = lambda k, shape: 1.0 + 0.05 * jax.random.normal(k, shape, f32)
    gate_b = jnp.concatenate([
        nrm(ks[9], (n_even, A_HEADS), 0.1),
        jax.random.uniform(ks[10], (n_even, A_HEADS), f32, 3.0, 6.0),
        nrm(ks[11], (n_even, A_HEADS), 0.1),
        jax.random.uniform(ks[12], (n_even, A_HEADS), f32, 3.0, 6.0)], axis=-1)
    return {
        'x': nrm(ks[0], (BATCH, SEQ, D_MODEL), 1.0),
        'c': nrm(ks[1], (BATCH, D_MODEL), 1.0),
        'ctx': nrm(ks[2], (BATCH, CTX_LEN, D_MODEL), 1.0),
        'c_ctx': nrm(ks[3], (D_MODEL,), 1.0),
        'ada_w': nrm(ks[4], (DEPTH, D_MODEL, N_MOD * D_MODEL), 0.5 * D_MODEL ** -0.5),
        'ada_b': nrm(ks[5], (DEPTH, N_MOD * D_MODEL), 0.02),
        'norm1_g': gain(ks[6], (DEPTH, D_MODEL)),
        'norm2_g': gain(ks[7], (DEPTH, D_MODEL)),
        'ab_w_in': nrm(ks[8], (n_even, D_MODEL, AB_IN), D_MODEL ** -0.5),
        'ab_gate_b': gate_b,
        'mlstm_norm_g': gain(ks[13], (n_even, A_WIDTH)),
        'swa_q_norm_g': gain(ks[14], (n_even, B_HEAD_DIM)),
        'swa_k_norm_g': gain(ks[15], (n_even, B_HEAD_DIM)),
        'swa_sink': nrm(ks[16], (n_even, B_HEADS), 0.5),
        'ab_w_out': nrm(ks[17], (n_even, AB_OUT, D_MODEL), AB_OUT ** -0.5),
        'c_w_in': nrm(ks[18], (n_odd, D_MODEL, C_IN), D_MODEL ** -0.5),
        'c_q_norm_g': gain(ks[19], (n_odd, C_HEAD_DIM)),
        'c_k_norm_g': gain(ks[20], (n_odd, C_HEAD_DIM)),
        'c_w_out': nrm(ks[21], (n_odd, C_WIDTH, D_MODEL), C_WIDTH ** -0.5),
        'mlp_w1': nrm(ks[22], (DEPTH, D_MODEL, D_FF), D_MODEL ** -0.5),
        'mlp_w2': nrm(ks[23], (DEPTH, D_FF, D_MODEL), D_FF ** -0.5),
    }

def first_block(x, c, ctx, c_ctx, ada_w, ada_b, norm1_g, norm2_g, ab_w_in, ab_gate_b, mlstm_norm_g,
              swa_q_norm_g, swa_k_norm_g, swa_sink, ab_w_out, c_w_in, c_q_norm_g, c_k_norm_g, c_w_out,
              mlp_w1, mlp_w2):
    batch = x.shape[0]
    for layer in range(DEPTH):
        last = layer == DEPTH - 1
        mod_l = (jax.nn.silu(c) @ ada_w[layer] + ada_b[layer]).reshape(batch, 1, N_MOD, D_MODEL)
        mod_c = (jax.nn.silu(c_ctx) @ ada_w[layer] + ada_b[layer]).reshape(1, 1, N_MOD, D_MODEL)
        h_l = modulate(x, norm1_g[layer], mod_l, 0)
        h_c = modulate(ctx, norm1_g[layer], mod_c, 0)
        j = layer // 2
        if layer % 2 == 0:
            y_c, y_l = ab_mixer(h_c, h_l, ab_w_in[j], ab_gate_b[j], mlstm_norm_g[j], swa_q_norm_g[j],
                                swa_k_norm_g[j], swa_sink[j], ab_w_out[j], not last)
        else:
            y_c, y_l = c_mixer(h_c, h_l, c_w_in[j], c_q_norm_g[j], c_k_norm_g[j], c_w_out[j], not last)
        x = x + mod_l[:, :, 2] * y_l
        x = x + mod_l[:, :, 5] * sq_relu_mlp(modulate(x, norm2_g[layer], mod_l, 3), mlp_w1[layer], mlp_w2[layer])
        if not last:
            ctx = ctx + mod_c[:, :, 2] * y_c
            ctx = ctx + mod_c[:, :, 5] * sq_relu_mlp(modulate(ctx, norm2_g[layer], mod_c, 3), mlp_w1[layer], mlp_w2[layer])
    return x


D_MIX = D_MODEL
HEAD_DIM = 64
A_WIDTH_2 = A_HEADS * HEAD_DIM
A_CHUNK = 128
B_DK = 64
B_DV = 64
B_WIDTH_2 = B_HEADS * B_DV
B_CONV = 4
B_CHUNK = 64
C_HEADS_2 = 4
C_DK = 32
C_DV = 64
C_KEY = C_HEADS_2 * C_DK
C_WIDTH_2 = C_HEADS_2 * C_DV
C_RANK = 16
C_TAU = 16.0
C_CHUNK = 64
D_FF_2 = 2816
ALPHA = (2.0 * DEPTH) ** 0.25
BETA_INIT = (8.0 * DEPTH) ** -0.25
EPS_2 = 1e-5
SPLITS = (A_WIDTH_2, A_WIDTH_2,
          3 * B_WIDTH_2, B_WIDTH_2, B_HEADS, B_HEADS,
          C_KEY, C_KEY, C_WIDTH_2, C_WIDTH_2, C_RANK)
D_IN = sum(SPLITS)


def layer_norm(x, g, b):
    xf = x.astype(jnp.float32)
    mu = jnp.mean(xf, -1, keepdims=True)
    var = jnp.mean(jnp.square(xf - mu), -1, keepdims=True)
    return ((xf - mu) * lax.rsqrt(var + EPS_2) * g + b).astype(x.dtype)

def rms_norm_2(x, g):
    xf = x.astype(jnp.float32)
    return (xf * lax.rsqrt(jnp.mean(xf * xf, -1, keepdims=True) + EPS_2) * g).astype(x.dtype)

def l2_norm(x):
    xf = x.astype(jnp.float32)
    return (xf * lax.rsqrt(jnp.sum(xf * xf, -1, keepdims=True) + 1e-6)).astype(x.dtype)

def swiglu_half(x, w1, w3, w2):
    return 0.5 * ((jax.nn.silu(x @ w1) * (x @ w3)) @ w2)

def to_chunks(x, c):
    b_, t, h, d = x.shape
    return x.reshape(b_, t // c, c, h, d).transpose(0, 3, 1, 2, 4)

def gates_to_chunks(x, c):
    b_, t, h = x.shape
    return x.reshape(b_, t // c, c, h).transpose(0, 3, 1, 2)

def from_chunks(x):
    b_, h, n, c, d = x.shape
    return x.transpose(0, 2, 3, 1, 4).reshape(b_, n * c, h, d)

def causal_short_conv(x, w):
    k = w.shape[0]
    t = x.shape[1]
    xp = jnp.pad(x, ((0, 0), (k - 1, 0), (0, 0)))
    y = w[0] * xp[:, 0:t]
    for i in range(1, k):
        y = y + w[i] * xp[:, i:i + t]
    return y

def spatial_gating(u, v, ln_g, ln_b, w_s, b_s):
    b_, t, _ = v.shape
    n = t // A_CHUNK
    v = layer_norm(v, ln_g, ln_b).reshape(b_, n, A_CHUNK, A_HEADS, HEAD_DIM)
    mask = jnp.tril(jnp.ones((A_CHUNK, A_CHUNK), dtype=bool))
    w = jnp.where(mask, w_s, 0.0)
    z = jnp.einsum('hij,bnjhd->bnihd', w, v) + b_s.T[:, :, None]
    return u * z.reshape(b_, t, A_WIDTH_2)

def gated_delta_rule(q, k, v, log_g, beta):
    out_dtype = v.dtype
    q, k, v, log_g, beta = (t_.astype(jnp.float32) for t_ in (q, k, v, log_g, beta))
    c = q.shape[3]
    b_, h, _, _, dk = q.shape
    dv = v.shape[-1]
    incl = jnp.tril(jnp.ones((c, c), dtype=bool))
    strict = jnp.tril(jnp.ones((c, c), dtype=bool), -1)
    gam = jnp.cumsum(log_g, axis=-1)
    decay = jnp.exp(jnp.where(incl, gam[..., :, None] - gam[..., None, :], -jnp.inf))
    kk = jnp.einsum('bhnid,bhnjd->bhnij', k, k)
    lower = jnp.where(strict, beta[..., :, None] * kk * decay, 0.0)
    eye = jnp.eye(c, dtype=jnp.float32)
    rhs = jnp.concatenate([beta[..., None] * v, (beta * jnp.exp(gam))[..., None] * k], axis=-1)
    sol = lax.linalg.triangular_solve(eye + lower, rhs, left_side=True, lower=True, unit_diagonal=True)
    u_base, w_state = sol[..., :dv], sol[..., dv:]
    p_intra = jnp.einsum('bhnid,bhnjd->bhnij', q, k) * decay
    q_dec = q * jnp.exp(gam)[..., None]
    k_dec = k * jnp.exp(gam[..., -1:] - gam)[..., None]
    g_tot = jnp.exp(gam[..., -1])

    def step(s, inp):
        u_b, w_c, p_c, qd, kd, gt = inp
        u = u_b - jnp.einsum('bhck,bhkv->bhcv', w_c, s)
        o = jnp.einsum('bhck,bhkv->bhcv', qd, s) + jnp.einsum('bhij,bhjv->bhiv', p_c, u)
        s = gt[..., None, None] * s + jnp.einsum('bhck,bhcv->bhkv', kd, u)
        return s, o

    s0 = jnp.zeros((b_, h, dk, dv), jnp.float32)
    xs = tuple(jnp.moveaxis(t_, 2, 0) for t_ in (u_base, w_state, p_intra, q_dec, k_dec, g_tot))
    _, o = lax.scan(step, s0, xs)
    return jnp.moveaxis(o, 0, 2).astype(out_dtype)

def gated_deltanet(qkv, z, beta_logit, decay_logit, conv_w, a_log, dt_bias, norm_g):
    b_, t, _ = qkv.shape
    qkv = jax.nn.silu(causal_short_conv(qkv, conv_w))
    q, k, v = jnp.split(qkv, 3, axis=-1)
    q = l2_norm(q.reshape(b_, t, B_HEADS, B_DK)) * (B_DK ** -0.5)
    k = l2_norm(k.reshape(b_, t, B_HEADS, B_DK))
    v = v.reshape(b_, t, B_HEADS, B_DV)
    beta = jax.nn.sigmoid(beta_logit.astype(jnp.float32))
    log_g = -jnp.exp(a_log) * jax.nn.softplus(decay_logit.astype(jnp.float32) + dt_bias)
    o = gated_delta_rule(to_chunks(q, B_CHUNK), to_chunks(k, B_CHUNK), to_chunks(v, B_CHUNK),
                         gates_to_chunks(log_g, B_CHUNK), gates_to_chunks(beta, B_CHUNK))
    o = from_chunks(o)
    o = rms_norm_2(o, norm_g) * jax.nn.silu(z.reshape(b_, t, B_HEADS, B_DV))
    return o.reshape(b_, t, B_WIDTH_2)

def gla_chunked(q, k, v, log_a):
    out_dtype = v.dtype
    q, k, v, log_a = (t_.astype(jnp.float32) for t_ in (q, k, v, log_a))
    c = q.shape[3]
    b_, h, _, _, dk = q.shape
    dv = v.shape[-1]
    incl = jnp.tril(jnp.ones((c, c), dtype=bool))
    bcum = jnp.cumsum(log_a, axis=3)
    q_dec = q * jnp.exp(bcum)
    p_intra = jnp.where(incl, jnp.einsum('bhnid,bhnjd->bhnij', q_dec, k * jnp.exp(-bcum)), 0.0)
    o_intra = jnp.einsum('bhnij,bhnjv->bhniv', p_intra, v)
    k_dec = k * jnp.exp(bcum[..., -1:, :] - bcum)
    g_tot = jnp.exp(bcum[..., -1, :])

    def step(s, inp):
        o_i, qd, kd, vc, gt = inp
        o = o_i + jnp.einsum('bhck,bhkv->bhcv', qd, s)
        s = gt[..., :, None] * s + jnp.einsum('bhck,bhcv->bhkv', kd, vc)
        return s, o

    s0 = jnp.zeros((b_, h, dk, dv), jnp.float32)
    xs = tuple(jnp.moveaxis(t_, 2, 0) for t_ in (o_intra, q_dec, k_dec, v, g_tot))
    _, o = lax.scan(step, s0, xs)
    return jnp.moveaxis(o, 0, 2).astype(out_dtype)

def gla(q, k, v, r, g_low, gate_up, gate_b, norm_g):
    b_, t, _ = q.shape
    log_a = jax.nn.log_sigmoid((g_low @ gate_up + gate_b).astype(jnp.float32)) / C_TAU
    q = q.reshape(b_, t, C_HEADS_2, C_DK) * (C_DK ** -0.5)
    k = k.reshape(b_, t, C_HEADS_2, C_DK)
    v = v.reshape(b_, t, C_HEADS_2, C_DV)
    log_a = log_a.reshape(b_, t, C_HEADS_2, C_DK)
    o = gla_chunked(to_chunks(q, C_CHUNK), to_chunks(k, C_CHUNK), to_chunks(v, C_CHUNK),
                    to_chunks(log_a, C_CHUNK))
    o = rms_norm_2(from_chunks(o), norm_g) * jax.nn.silu(r.reshape(b_, t, C_HEADS_2, C_DV))
    return o.reshape(b_, t, C_WIDTH_2)

def second_inputs(seed: int = 0) -> dict:
    key = jax.random.key(seed)
    ks = jax.random.split(key, 40)
    L = DEPTH
    f32 = jnp.float32

    def nrm(i, shape, scale):
        return jax.random.normal(ks[i], shape, f32) * scale

    def gain(i, shape):
        return 1.0 + 0.1 * jax.random.normal(ks[i], shape, f32)

    a_val = jax.random.uniform(ks[17], (L, B_HEADS), f32, 1.0, 16.0)
    dt = jnp.exp(jax.random.uniform(ks[18], (L, B_HEADS), f32, np.log(1e-3), np.log(1e-1)))
    return {
        "x": jax.random.normal(ks[0], (BATCH, SEQ, D_MODEL), f32),
        "ffn1_w1": nrm(1, (L, D_MODEL, D_FF_2), D_MODEL ** -0.5),
        "ffn1_w3": nrm(2, (L, D_MODEL, D_FF_2), D_MODEL ** -0.5),
        "ffn1_w2": nrm(3, (L, D_FF_2, D_MODEL), BETA_INIT * D_FF_2 ** -0.5),
        "ln1_g": gain(4, (L, D_MODEL)),
        "ln1_b": nrm(5, (L, D_MODEL), 0.02),
        "w_in": nrm(6, (L, D_MODEL, D_IN), D_MODEL ** -0.5),
        "sgu_ln_g": gain(7, (L, A_WIDTH_2)),
        "sgu_ln_b": nrm(8, (L, A_WIDTH_2), 0.02),
        "sgu_w": nrm(9, (L, A_HEADS, A_CHUNK, A_CHUNK), 0.5 * A_CHUNK ** -0.5),
        "sgu_b": gain(10, (L, A_HEADS, A_CHUNK)),
        "gdn_conv_w": nrm(11, (L, B_CONV, 3 * B_WIDTH_2), 0.5),
        "gdn_a_log": jnp.log(a_val),
        "gdn_dt_bias": dt + jnp.log(-jnp.expm1(-dt)),
        "gdn_norm_g": gain(12, (L, B_DV)),
        "gla_gate_up": nrm(13, (L, C_RANK, C_KEY), C_RANK ** -0.5),
        "gla_gate_b": nrm(14, (L, C_KEY), 0.1),
        "gla_norm_g": gain(15, (L, C_DV)),
        "w_out": nrm(16, (L, D_MIX, D_MODEL), BETA_INIT * D_MIX ** -0.5),
        "ln2_g": gain(19, (L, D_MODEL)),
        "ln2_b": nrm(20, (L, D_MODEL), 0.02),
        "ffn2_w1": nrm(21, (L, D_MODEL, D_FF_2), D_MODEL ** -0.5),
        "ffn2_w3": nrm(22, (L, D_MODEL, D_FF_2), D_MODEL ** -0.5),
        "ffn2_w2": nrm(23, (L, D_FF_2, D_MODEL), BETA_INIT * D_FF_2 ** -0.5),
        "ln3_g": gain(24, (L, D_MODEL)),
        "ln3_b": nrm(25, (L, D_MODEL), 0.02),
    }

def second_block(x, ffn1_w1, ffn1_w3, ffn1_w2, ln1_g, ln1_b, w_in, sgu_ln_g, sgu_ln_b, sgu_w, sgu_b,
              gdn_conv_w, gdn_a_log, gdn_dt_bias, gdn_norm_g, gla_gate_up, gla_gate_b, gla_norm_g,
              w_out, ln2_g, ln2_b, ffn2_w1, ffn2_w3, ffn2_w2, ln3_g, ln3_b):
    split_at = [int(s) for s in np.cumsum(SPLITS)[:-1]]
    for l in range(DEPTH):
        x = layer_norm(ALPHA * x + swiglu_half(x, ffn1_w1[l], ffn1_w3[l], ffn1_w2[l]), ln1_g[l], ln1_b[l])
        h = x @ w_in[l]
        (a_u, a_v, b_qkv, b_z, b_beta, b_decay,
         c_q, c_k, c_v, c_r, c_g) = jnp.split(h, split_at, axis=-1)
        out_a = spatial_gating(jax.nn.gelu(a_u), jax.nn.gelu(a_v), sgu_ln_g[l], sgu_ln_b[l], sgu_w[l], sgu_b[l])
        out_b = gated_deltanet(b_qkv, b_z, b_beta, b_decay, gdn_conv_w[l], gdn_a_log[l], gdn_dt_bias[l], gdn_norm_g[l])
        out_c = gla(c_q, c_k, c_v, c_r, c_g, gla_gate_up[l], gla_gate_b[l], gla_norm_g[l])
        mix = jnp.concatenate([out_a, out_b, out_c], axis=-1) @ w_out[l]
        x = layer_norm(ALPHA * x + mix, ln2_g[l], ln2_b[l])
        x = layer_norm(ALPHA * x + swiglu_half(x, ffn2_w1[l], ffn2_w3[l], ffn2_w2[l]), ln3_g[l], ln3_b[l])
    return x


def setup_inputs(seed=0):
    out = dict(first_inputs(seed))
    for name, value in second_inputs(seed + 1).items():
        if name != "x":
            out[name + "_2"] = value
    return out


def reference(
    x, c, ctx, c_ctx, ada_w, ada_b, norm1_g, norm2_g, ab_w_in, ab_gate_b, mlstm_norm_g,
    swa_q_norm_g, swa_k_norm_g, swa_sink, ab_w_out, c_w_in, c_q_norm_g, c_k_norm_g, c_w_out,
    mlp_w1, mlp_w2, ffn1_w1_2, ffn1_w3_2, ffn1_w2_2, ln1_g_2, ln1_b_2, w_in_2, sgu_ln_g_2,
    sgu_ln_b_2, sgu_w_2, sgu_b_2, gdn_conv_w_2, gdn_a_log_2, gdn_dt_bias_2, gdn_norm_g_2,
    gla_gate_up_2, gla_gate_b_2, gla_norm_g_2, w_out_2, ln2_g_2, ln2_b_2, ffn2_w1_2, ffn2_w3_2,
    ffn2_w2_2, ln3_g_2, ln3_b_2,
):
    x = first_block(
        x, c, ctx, c_ctx, ada_w, ada_b, norm1_g, norm2_g, ab_w_in, ab_gate_b, mlstm_norm_g,
        swa_q_norm_g, swa_k_norm_g, swa_sink, ab_w_out, c_w_in, c_q_norm_g, c_k_norm_g, c_w_out,
        mlp_w1, mlp_w2,
    )
    return second_block(
        x, ffn1_w1_2, ffn1_w3_2, ffn1_w2_2, ln1_g_2, ln1_b_2, w_in_2, sgu_ln_g_2, sgu_ln_b_2,
        sgu_w_2, sgu_b_2, gdn_conv_w_2, gdn_a_log_2, gdn_dt_bias_2, gdn_norm_g_2, gla_gate_up_2,
        gla_gate_b_2, gla_norm_g_2, w_out_2, ln2_g_2, ln2_b_2, ffn2_w1_2, ffn2_w3_2, ffn2_w2_2,
        ln3_g_2, ln3_b_2,
    )


_drawn_inputs = setup_inputs


def setup_inputs(seed=0):
    import zlib

    import numpy as np

    out = dict(_drawn_inputs(seed))
    spreads = {}
    factors = {'norm1_g': 3.129,
     'mlstm_norm_g': 8.0,
     'swa_q_norm_g': 8.0,
     'swa_k_norm_g': 8.0,
     'swa_sink': 8.0,
     'c_q_norm_g': 8.0,
     'c_k_norm_g': 8.0,
     'sgu_ln_g_2': 8.0,
     'sgu_ln_b_2': 57.543,
     'sgu_b_2': 3.502,
     'gdn_norm_g_2': 2.838,
     'gla_gate_b_2': 8.0,
     'gla_norm_g_2': 5.131}
    for name, (base, spread) in spreads.items():
        noise = np.random.default_rng([zlib.crc32(name.encode()), seed]).standard_normal(out[name].shape)
        drawn = base * np.exp(spread * noise) if base else spread * noise
        out[name] = __import__('jax').numpy.asarray(drawn.astype(out[name].dtype))
    for name, factor in factors.items():
        out[name] = (out[name] * factor).astype(out[name].dtype)
    return out
```

```python
from contextlib import ExitStack

import numpy as np

import concourse.bass as bass
from concourse import mybir

F32 = mybir.dt.float32
ALU = mybir.AluOpType
ACT = mybir.ActivationFunctionType
AX = mybir.AxisListType.X

P = 128
D = 1024
KD = D // P
CTX = 256
SEQ = 512
TOK = CTX + SEQ
NT = TOK // P
NCT = CTX // P
NLT = SEQ // P
FF1 = 4 * D
FF2 = 2816
EPS1, EPS2, EPSL = 1e-6, 1e-5, 1e-6
ALPHA = 4.0 ** 0.25
NEG = -1e30
ALL = [(0, 384), (384, 768)]
LAT = [(256, 768)]
SLAB = 16
RING = 4

VECS = [("c", 8), ("c_ctx", 8), ("ada_b", 96), ("norm1_g", 16), ("norm2_g", 16), ("mlstm_g", 4),
        ("swa_q", 1), ("swa_k", 1), ("c_q", 1), ("c_k", 1), ("sink", 8), ("gb_i", 1), ("gb_f", 1),
        ("ln1_g", 16), ("ln1_b", 16), ("ln2_g", 16), ("ln2_b", 16), ("ln3_g", 16), ("ln3_b", 16),
        ("sgu_g", 4), ("sgu_b", 4), ("conv", 96), ("a_log", 2), ("dt_b", 2), ("gdn_g", 2),
        ("gla_gb", 2), ("gla_g", 2), ("eps1", 1), ("eps2", 1), ("epsl", 1), ("one", 1)]
VOFF = {}
_o = 0
for _n, _w in VECS:
    VOFF[_n] = (_o, _w)
    _o += _w
NVEC = _o

SHARED = [("ident", 128), ("ones", 128), ("blk64", 128), ("neg_ge", 128), ("neg_le", 128)]
FIRST = [("rot64", 128), ("rot128", 128), ("dup0", 128), ("dup1", 128), ("self", 512), ("selb", 512),
         ("cos64", 512), ("sin64", 512), ("cos128", 512), ("sin128", 512)]
SECOND = [("pos_lt", 128), ("m_ge", 128), ("sel", 1024), ("selp", 512), ("m_gla", 128), ("bd_gla", 256),
          ("rs128", 512), ("rs64", 512), ("lev", 896), ("levt", 896)]


def offsets(names):
    at, out = 0, {}
    for name, cols in names:
        out[name] = at
        at += cols
    return out, at


SHARED_AT, N_SHARED = offsets(SHARED)
FIRST_AT, N_FIRST = offsets(FIRST)
SECOND_AT, N_SECOND = offsets(SECOND)


def consts():
    r, c = np.arange(P)[:, None], np.arange(P)[None, :]
    a = {}
    a["ident"] = (r == c)
    a["ones"] = np.ones((P, P))
    a["blk64"] = (r // 64 == c // 64)

    def rot(n):
        h = n // 2
        return np.where((c % n < h) & (r == c + h), -1.0, 0.0) + np.where((c % n >= h) & (r == c - h), 1.0, 0.0)

    a["rot64"], a["rot128"] = rot(64), rot(128)
    a["dup0"], a["dup1"] = (r == c % 64), (r == 64 + c % 64)
    a["neg_ge"] = np.where(c >= r, 0.0, NEG)
    a["neg_le"] = np.where(c <= r, 0.0, NEG)
    a["pos_lt"] = np.where(c < r, 0.0, -NEG)
    a["m_ge"] = (c >= r)
    for name, base, heads in (("self", 0, 4), ("selb", 32, 4), ("sel", 0, 8)):
        a[name] = np.concatenate([np.broadcast_to(r == base + h, (P, P)) for h in range(heads)], 1)
    a["selp"] = np.concatenate([(r == 2 * p + c // 64) for p in range(4)], 1)
    a["m_gla"] = (c >= r) & (c // 64 == r // 64)
    a["bd_gla"] = (r // 32 == np.arange(256)[None, :] // 64)
    t = np.arange(512)[None, :]
    a["rs128"] = np.broadcast_to(t % 128 != 0, (P, 512))
    a["rs64"] = np.broadcast_to(t % 64 != 0, (P, 512))
    lev = [((r // (2 * b) == c // (2 * b)) & (r % (2 * b) >= b) & (c % (2 * b) < b)) for b in (1, 2, 4, 8, 16, 32, 64)]
    a["lev"] = np.concatenate(lev, 1)
    a["levt"] = np.concatenate([m.T for m in lev], 1)
    a["cos64"], a["sin64"] = rope_tables(64)
    a["cos128"], a["sin128"] = rope_tables(128)
    return [np.concatenate([np.asarray(a[n], np.float32) for n, _ in group], 1) for group in (SHARED, FIRST, SECOND)]


def rope_tables(head_dim):
    t = np.arange(SEQ)
    row, col = (t // 64).astype(np.float32), (t % 64).astype(np.float32)
    pairs = head_dim // 4
    inv = (np.float32(10000.0) ** (-np.arange(pairs, dtype=np.float32) / np.float32(pairs))).astype(np.float32)
    ang = np.concatenate([inv[:, None] * row[None], inv[:, None] * col[None]], 0)
    reps = P // ang.shape[0]
    return np.tile(np.cos(ang), (reps, 1)).astype(np.float32), np.tile(np.sin(ang), (reps, 1)).astype(np.float32)


def ftiles(w, cols, kt=KD):
    return [(w, k, c, P) for c in range(cols[0], cols[1], P) for k in range(kt)]


def ttiles(w, cols, kt=KD):
    return [(w, k, c, P) for k in range(kt) for c in range(cols[0], cols[1], P)]


def stream():
    s = ftiles("ada0", (0, 6144)) + ftiles("ada1", (0, 6144))
    s += ftiles("ab", (0, 1024)) + ftiles("ab", (1536, 2048)) + ftiles("ab", (2064, 2576)) + ftiles("ab", (2576, 2704))
    s += ftiles("gi", (0, P)) + ftiles("gf", (0, P))
    s += ttiles("ab", (1024, 1280)) + ttiles("ab", (1280, 1536)) + ttiles("ab", (2704, 2832))
    s += ftiles("abo", (0, D)) + ftiles("m1_0", (0, FF1)) + ftiles("m2_0", (0, D), FF1 // P)
    s += ftiles("cw", (0, 1280)) + ttiles("cw", (1280, 1536)) + ftiles("co", (0, D))
    s += ftiles("m1_1", (0, FF1)) + ftiles("m2_1", (0, D), FF1 // P)
    for l in range(2):
        for f in ("f", None, "g"):
            if f is None:
                w = f"in{l}"
                s += ftiles(w, (0, 512)) + ftiles(w, (512, 2048)) + ftiles(w, (2048, 2560))
                s += ftiles(f"be{l}", (0, P)) + ftiles(f"de{l}", (0, P))
                s += ftiles(w, (2576, 2832)) + ftiles(w, (3088, 3344)) + ftiles(f"gl{l}", (0, P))
                s += ttiles(w, (2832, 3088)) + ftiles(f"out{l}", (0, D))
            else:
                for c in range(0, FF2, P):
                    s += ftiles(f"{f}1_{l}", (c, c + P)) + ftiles(f"{f}3_{l}", (c, c + P))
                s += ftiles(f"{f}2_{l}", (0, D), FF2 // P)
    return s


N_SLABS = -(-len(stream()) // SLAB)


class Signal:

    def __init__(self, sem):
        self.sem = sem
        self.seen = {}

    def at(self, who, k):
        return self.seen.get(who, 0) + k + 1

    def advance(self, who, n):
        self.seen[who] = self.seen.get(who, 0) + n

    def next(self, who, step=1):
        self.seen[who] = self.seen.get(who, 0) + step
        return self.seen[who]


class Out:

    def __init__(self, bank, ready, who, freed, reuse):
        self.bank, self.ready, self.who, self.freed, self.reuse = bank, ready, who, freed, reuse


class Banks:

    def __init__(self):
        self.n, self.done, self.user = 0, {"act": 0, "dve": 0}, [None] * 8

    def take(self, who):
        bank = self.n % 8
        self.n += 1
        self.done[who] += 1
        out = Out(bank, self.n, who, self.done[who], self.user[bank])
        self.user[bank] = (who, self.done[who])
        return out


def program(nc, xT_d, vec_d, shared_d, first_d, second_d, gup_d, sguw_d, sgub_d, w_d, out_d):
    with ExitStack() as ctx:
        def sb(name, cols):
            return ctx.enter_context(nc.sbuf_tensor(name, [P, cols], F32))

        def signal(name):
            return Signal(ctx.enter_context(nc.semaphore(name)))

        X = ctx.enter_context(nc.sbuf_tensor("X", [P, KD, TOK], F32))
        H = ctx.enter_context(nc.sbuf_tensor("H", [P, KD, TOK], F32))
        ring = ctx.enter_context(nc.sbuf_tensor("ring", [P, RING, SLAB, P], F32))
        ARENA = 24576
        arena = sb("arena", ARENA)
        vec = sb("vec", NVEC)
        con = sb("con", N_SHARED)
        con2 = sb("con2", max(N_FIRST, N_SECOND))
        mods = ctx.enter_context(nc.sbuf_tensor("mods", [P, 2, 2, 48], F32))
        amul = ctx.enter_context(nc.sbuf_tensor("amul", [P, 2, 2, 2, 8], F32))
        cs = ctx.enter_context(nc.sbuf_tensor("cs", [P, 8, 2], F32))
        small = sb("small", 160)
        PS = ctx.enter_context(nc.psum_tensor("PS", [P, 8, 512], F32))

        def V(name, i=0, n=1):
            return vec[:, VOFF[name][0] + i:VOFF[name][0] + i + n]

        def C(name, i=0, n=P):
            if name in SHARED_AT:
                return con[:, SHARED_AT[name] + i:SHARED_AT[name] + i + n]
            at = FIRST_AT[name] if name in FIRST_AT else SECOND_AT[name]
            return con2[:, at + i:at + i + n]

        def area(at, *dims):
            n = int(np.prod(dims))
            assert at + n <= ARENA, (at, n)
            a = arena[:, at:at + n]
            if len(dims) == 2:
                return a.rearrange("p (a b) -> p a b", a=dims[0])
            if len(dims) == 3:
                return a.rearrange("p (a b c) -> p a b c", a=dims[0], b=dims[1])
            return a

        loaded = signal("inputs_loaded")
        rope_loaded = signal("rope_loaded")
        small_loaded = signal("sgu_loaded")
        slab_loaded = [signal(f"slab_loaded{i}") for i in range(RING)]
        slab_used = signal("slab_used")
        mm_done = signal("product_ready")
        evac = {"act": signal("evacuated_by_act"), "dve": signal("evacuated_by_dve")}
        stage = signal("stage_done")
        stored = signal("stored")
        act_step = signal("act_step")
        dve_step = signal("dve_step")
        silu_c = signal("silu_c_ready")
        ada_done = signal("ada_products_ready")
        sq_ready = signal("squares_ready")
        sum_ready = signal("sums_ready")
        mean_sums = signal("mean_sums_ready")
        std_ready = signal("std_ready")
        norm_ready = signal("normed_ready")
        mean_used = signal("mean_used")

        def a_link(act, ins):
            ins.then_inc(act_step.sem, 1)
            act.wait_ge(act_step.sem, act_step.next("act"))

        def v_link(dve, ins):
            ins.then_inc(dve_step.sem, 1)
            dve.wait_ge(dve_step.sem, dve_step.next("dve"))

        def end_stage(eng, who):
            eng.drain().then_inc(stage.sem, 1)
            eng.wait_ge(stage.sem, stage.next(who, 3))

        class Weights:
            at = 0
            used = []

        def used_up(ins):
            ins.then_inc(slab_used.sem, 1)
            Weights.used.append((slab_used, slab_used.next("pe")))

        def tiles_of(pe, n):
            slab, pos = divmod(Weights.at, SLAB)
            assert pos + n <= SLAB
            if pos == 0:
                pe.wait_ge(slab_loaded[slab % RING].sem, 16 * (slab // RING + 1))
            Weights.at += n
            return ring[:, slab % RING, pos:pos + n, :], Weights.at % SLAB == 0

        def gemm_pe(pe, tiles):
            for t in tiles:
                for o in t["outs"]:
                    if o.reuse:
                        pe.wait_ge(evac[o.reuse[0]].sem, o.reuse[1])
                kt = t["kt"]
                for k in range(kt):
                    w, last_of_slab = tiles_of(pe, t["n"])
                    for o, (lo, hi) in zip(t["outs"], t["segs"]):
                        if t["mode"] == "F":
                            ins = pe.matmul(PS[:, o.bank, 0:hi - lo], w[:, 0, :], t["rhs"](k, lo, hi),
                                            start=(k == 0), stop=(k == kt - 1))
                        else:
                            ins = pe.matmul(PS[:, o.bank, 0:t["n"] * P], t["rhs"](k, lo, hi),
                                            w.rearrange("p a b -> p (a b)"), start=(k == 0), stop=(k == kt - 1))
                        if k == kt - 1:
                            ins.then_inc(mm_done.sem, 1)
                    if last_of_slab:
                        if k == kt - 1:
                            Weights.used.append((mm_done, t["outs"][-1].ready))
                        else:
                            used_up(ins)

        def gemm_evac(eng, who, tiles):
            for t in tiles:
                for o, (lo, hi) in zip(t["outs"], t["segs"]):
                    if o.who == who:
                        eng.wait_ge(mm_done.sem, o.ready)
                        width = hi - lo if t["mode"] == "F" else t["n"] * P
                        t["ev"](eng, PS[:, o.bank, 0:width], lo, hi).then_inc(evac[who].sem, 1)

        banks = Banks()

        def ftile(rhs, segs, who, ev, kt=KD):
            return dict(mode="F", n=1, kt=kt, segs=segs, rhs=rhs, ev=ev, outs=[banks.take(who) for _ in segs])

        def ttile(rhs, toks, n, who, ev):
            return dict(mode="T", n=n, kt=KD, segs=[(P * t, P * t + P) for t in toks], rhs=rhs, ev=ev,
                        outs=[banks.take(who) for _ in toks])

        def x_h(k, lo, hi):
            return H[:, k, lo:hi]

        def copy_act(dst, scale=1.0):
            def ev(eng, ps, lo, hi):
                return nc.scalar.activation(dst(lo, hi), ps, ACT.Copy, scale=scale)
            return ev

        def copy_dve(dst):
            def ev(eng, ps, lo, hi):
                return nc.vector.tensor_copy(dst(lo, hi), ps)
            return ev

        def streams(lo, hi):
            return [(s, max(lo, a), min(hi, b)) for s, a, b in ((1, 0, CTX), (0, CTX, TOK)) if max(lo, a) < min(hi, b)]

        rstd = sb("rstd", 512)
        mean = sb("mean", 512)

        def norm_act(act, segs, eps, centred, affine):
            for lo, hi in segs:
                if centred:
                    act.wait_ge(mean_used.sem, mean_used.next("act"))
                for k in range(KD):
                    src = H if centred else X
                    dst = tmp_sq
                    ins = nc.scalar.activation(dst[:, k, lo:hi], src[:, k, lo:hi], ACT.Square)
                ins.then_inc(sq_ready.sem, 1)
                act.wait_ge(sum_ready.sem, sum_ready.next("act"))
                nc.scalar.activation(rstd[:, 0:hi - lo], PS[:, 0, 0:hi - lo], ACT.Sqrt, bias=V(eps),
                                     scale=1.0 / D).then_inc(std_ready.sem, 1)
                for k in range(KD):
                    act.wait_ge(norm_ready.sem, norm_ready.next("act"))
                    affine(act, k, lo, hi)

        def norm_pe(pe, segs, centred):
            for lo, hi in segs:
                if centred:
                    for k in range(KD):
                        ins = pe.matmul(PS[:, 1, 0:hi - lo], C("ones"), X[:, k, lo:hi], start=(k == 0), stop=(k == KD - 1))
                    ins.then_inc(mean_sums.sem, 1)
                pe.wait_ge(sq_ready.sem, sq_ready.next("pe"))
                for k in range(KD):
                    ins = pe.matmul(PS[:, 0, 0:hi - lo], C("ones"), tmp_sq[:, k, lo:hi], start=(k == 0), stop=(k == KD - 1))
                ins.then_inc(sum_ready.sem, 1)

        def norm_dve(dve, segs, centred):
            for lo, hi in segs:
                src = X
                if centred:
                    dve.wait_ge(mean_sums.sem, mean_sums.next("dve"))
                    v_link(dve, nc.vector.tensor_scalar(mean[:, 0:hi - lo], PS[:, 1, 0:hi - lo], 1.0 / D, None, ALU.mult))
                    for k in range(KD):
                        ins = nc.vector.tensor_tensor(H[:, k, lo:hi], X[:, k, lo:hi], mean[:, 0:hi - lo], ALU.subtract)
                    ins.then_inc(mean_used.sem, 1)
                    src = H
                dve.wait_ge(std_ready.sem, std_ready.next("dve"))
                v_link(dve, nc.vector.reciprocal(rstd[:, 0:hi - lo], rstd[:, 0:hi - lo]))
                for k in range(KD):
                    nc.vector.tensor_tensor(H[:, k, lo:hi], src[:, k, lo:hi], rstd[:, 0:hi - lo],
                                            ALU.mult).then_inc(norm_ready.sem, 1)

        tmp_sq = area(0, KD, TOK)

        def modulate(l, n):
            def affine(act, k, lo, hi):
                for s, a, b in streams(lo, hi):
                    nc.scalar.activation(H[:, k, a:b], H[:, k, a:b], ACT.Identity, bias=mods[:, l, s, 24 * n + k:24 * n + k + 1],
                                         scale=amul[:, l, s, n, k:k + 1])
            return affine

        def layer_norm_affine(name, l):
            def affine(act, k, lo, hi):
                nc.scalar.activation(X[:, k, lo:hi], H[:, k, lo:hi], ACT.Identity, bias=V(name + "_b", 8 * l + k),
                                     scale=V(name + "_g", 8 * l + k))
            return affine

        def ada_act(act):
            act.wait_ge(loaded.sem, 64)
            nc.scalar.activation(cs[:, :, 0], V("c", 0, 8), ACT.Silu)
            nc.scalar.activation(cs[:, :, 1], V("c_ctx", 0, 8), ACT.Silu).then_inc(silu_c.sem, 1)

        def ada_pe(pe):
            pe.wait_ge(loaded.sem, 64)
            pe.wait_ge(silu_c.sem, 1)
            for l in range(2):
                for m in range(48):
                    for k in range(KD):
                        w, last_of_slab = tiles_of(pe, 1)
                        ins = pe.matmul(PS[:, l, 2 * m:2 * m + 2], w[:, 0, :], cs[:, k, :], start=(k == 0), stop=(k == KD - 1))
                        if last_of_slab:
                            used_up(ins)
            pe.drain().then_inc(ada_done.sem, 1)

        def ada_dve(dve):
            dve.wait_ge(loaded.sem, 64)
            dve.wait_ge(ada_done.sem, 1)
            for l in range(2):
                for s in range(2):
                    v_link(dve, nc.vector.tensor_tensor(mods[:, l, s, :], PS[:, l, 0:96].rearrange("p (m s) -> p m s", s=2)[:, :, s],
                                                        V("ada_b", 48 * l, 48), ALU.add))
                    for n in range(2):
                        g = V("norm1_g" if n == 0 else "norm2_g", 8 * l, 8)
                        nc.vector.scalar_tensor_tensor(out=amul[:, l, s, n, :], in0=mods[:, l, s, 24 * n + 8:24 * n + 16],
                                                       scalar=1.0, in1=g, op0=ALU.add, op1=ALU.mult)

        hn_sq, hn_sum = signal("head_squares_ready"), signal("head_sums_ready")
        hn_std, hn_done = signal("head_std_ready"), signal("head_normed")
        HR = 4

        def head_norm(items, at):
            sq = [area(at + 512 * i, 512) for i in range(HR)]
            rs = [area(at + 512 * (HR + i), 512) for i in range(HR)]

            def width(it):
                return it[0].shape[-1]

            def act_fn(act):
                for i in range(len(items) + 1):
                    if i < len(items):
                        nc.scalar.activation(sq[i % HR][:, 0:width(items[i])], items[i][0], ACT.Square).then_inc(hn_sq.sem, 1)
                    if i >= 1:
                        j, it = i - 1, items[i - 1]
                        act.wait_ge(hn_sum.sem, hn_sum.at("act", j))
                        if j >= HR:
                            act.wait_ge(hn_done.sem, hn_done.at("act", j - HR))
                        nc.scalar.activation(rs[j % HR][:, 0:width(it)], PS[:, j % 8, 0:width(it)], ACT.Sqrt,
                                             bias=V(it[4]), scale=it[3]).then_inc(hn_std.sem, 1)
                hn_sum.advance("act", len(items))
                hn_done.advance("act", len(items))

            def pe_fn(pe):
                for i, it in enumerate(items):
                    pe.wait_ge(hn_sq.sem, hn_sq.at("pe", i))
                    if i >= 8:
                        pe.wait_ge(hn_std.sem, hn_std.at("pe", i - 8))
                    pe.matmul(PS[:, i % 8, 0:width(it)], C(it[2]), sq[i % HR][:, 0:width(it)], start=True, stop=True).then_inc(hn_sum.sem, 1)
                hn_sq.advance("pe", len(items))
                hn_std.advance("pe", len(items))

            def dve_fn(dve):
                for i, (src, dst, _, _, _, gain, extra) in enumerate(items):
                    r = rs[i % HR][:, 0:src.shape[-1]]
                    dve.wait_ge(hn_std.sem, hn_std.at("dve", i))
                    v_link(dve, nc.vector.reciprocal(r, r))
                    v_link(dve, nc.vector.tensor_tensor(dst, src, r, ALU.mult))
                    if extra is None:
                        ins = nc.vector.tensor_scalar(dst, dst, gain, None, ALU.mult)
                    else:
                        ins = nc.vector.scalar_tensor_tensor(out=dst, in0=dst, scalar=gain, in1=extra, op0=ALU.mult, op1=ALU.mult)
                    ins.then_inc(hn_done.sem, 1)
                hn_std.advance("dve", len(items))

            return pe_fn, act_fn, dve_fn

        rope_rot, rope_used = signal("rotated_ready"), signal("rotated_used")

        def rope(tiles, d, at):
            def pe_fn(pe):
                for i, t in enumerate(tiles):
                    if i >= 4:
                        pe.wait_ge(rope_used.sem, rope_used.at("pe", i - 4))
                    pe.matmul(PS[:, i % 4, :], C(f"rot{d}"), t, start=True, stop=True).then_inc(rope_rot.sem, 1)
                rope_used.advance("pe", len(tiles))

            def dve_fn(dve):
                for i, t in enumerate(tiles):
                    tmp = area(at + 512 * (i % 2), 512)
                    dve.wait_ge(rope_rot.sem, rope_rot.at("dve", i))
                    nc.vector.tensor_tensor(tmp, PS[:, i % 4, :], C(f"sin{d}", 0, 512), ALU.mult)
                    v_link(dve, nc.vector.tensor_tensor(t, t, C(f"cos{d}", 0, 512), ALU.mult))
                    nc.vector.tensor_tensor(t, t, tmp, ALU.add).then_inc(rope_used.sem, 1)
                rope_rot.advance("dve", len(tiles))

            return pe_fn, dve_fn

        at_s, at_nb, at_p = signal("scores_ready"), signal("minus_max_ready"), signal("exp_ready")
        at_n, at_t, at_tc = signal("probs_normed"), signal("probs_turned"), signal("turned_probs_copied")
        at_o, at_oc = signal("head_outputs_ready"), signal("head_outputs_copied")

        def attention(groups, scale, p_at, pt_at):
            units = [(g, j) for g in groups for j in range(4)]
            probs = [area(p_at + 768 * i, 768) for i in range(2)]
            turned = [area(pt_at + 3072 * i, 6, 512) for i in range(2)]
            n = len(units)

            def nk(g):
                return CTX + (g["lat"][1] - g["lat"][0] if g["lat"] else 0)

            def s_all(i, g):
                return PS[:, 2 * (i % 2):2 * (i % 2) + 2, :].rearrange("p a b -> p (a b)")[:, 256:256 + nk(g)]

            def key_tiles(g):
                return list(range(NCT)) + (list(range(g["lat"][0] // P, g["lat"][1] // P)) if g["lat"] else [])

            def col(i, what):
                return small[:, 8 * what + i % 8:8 * what + i % 8 + 1]

            def pe_fn(pe):
                for i in range(n + 1):
                    if i < n:
                        g, j = units[i]
                        if i >= 2:
                            pe.wait_ge(at_p.sem, at_p.at("pe", i - 2))
                        ins = pe.matmul(PS[:, 2 * (i % 2), 256:512], g["q"][j], g["k"][j][:, 0:CTX], start=True, stop=True)
                        if g["lat"]:
                            lo, hi = g["lat"]
                            ins = pe.matmul(PS[:, 2 * (i % 2) + 1, 0:hi - lo], g["q"][j], g["k"][j][:, lo:hi], start=True, stop=True)
                        ins.then_inc(at_s.sem, 1)
                    if i >= 1:
                        u = i - 1
                        g, j = units[u]
                        kts = key_tiles(g)
                        pe.wait_ge(at_n.sem, at_n.at("pe", u))
                        if u >= 1:
                            pe.wait_ge(at_tc.sem, at_tc.at("pe", u - 1))
                        for t in range(len(kts)):
                            ins = pe.transpose(PS[:, 4 + t // 4, (t % 4) * P:(t % 4) * P + P], probs[u % 2][:, t * P:t * P + P], C("ident"))
                        ins.then_inc(at_t.sem, 1)
                        if j == 3:
                            gi = u // 4
                            pe.wait_ge(at_tc.sem, at_tc.at("pe", u))
                            if gi >= 2:
                                pe.wait_ge(at_oc.sem, at_oc.at("pe", gi - 2))
                            for t, kt in enumerate(kts):
                                ins = pe.matmul(PS[0:g["m"], 6 + gi % 2, :], g["v"](kt), turned[gi % 2][:, t, :],
                                                start=(t == 0), stop=(t == len(kts) - 1))
                            ins.then_inc(at_o.sem, 1)
                for s_, c_ in ((at_p, n), (at_n, n), (at_tc, n), (at_oc, len(groups))):
                    s_.advance("pe", c_)

            def dve_fn(dve):
                for i in range(n + 1):
                    if i < n:
                        g, j = units[i]
                        dve.wait_ge(at_s.sem, at_s.at("dve", i))
                        for c_, mask in g["masks"]:
                            s_c = s_all(i, g)[:, c_:c_ + P]
                            ins = nc.vector.tensor_tensor(s_c, s_c, C(mask), ALU.add)
                        if g["masks"]:
                            v_link(dve, ins)
                        v_link(dve, nc.vector.tensor_reduce(col(i, 0), s_all(i, g), AX, ALU.max))
                        if g["sinks"]:
                            v_link(dve, nc.vector.tensor_scalar(col(i, 1), col(i, 0), scale, g["sinks"][j], ALU.mult, ALU.max))
                            ins = nc.vector.tensor_scalar(col(i, 2), col(i, 1), -1.0, None, ALU.mult)
                        else:
                            ins = nc.vector.tensor_scalar(col(i, 2), col(i, 0), -scale, None, ALU.mult)
                        ins.then_inc(at_nb.sem, 1)
                    if i >= 1:
                        u = i - 1
                        g, j = units[u]
                        dve.wait_ge(at_p.sem, at_p.at("dve", u))
                        if g["sinks"]:
                            v_link(dve, nc.vector.tensor_tensor(col(u, 3), col(u, 3), col(u, 4), ALU.add))
                        v_link(dve, nc.vector.reciprocal(col(u, 5), col(u, 3)))
                        nc.vector.tensor_scalar(probs[u % 2][:, 0:nk(g)], probs[u % 2][:, 0:nk(g)], col(u, 5), None,
                                                ALU.mult).then_inc(at_n.sem, 1)
                at_s.advance("dve", n)
                at_p.advance("dve", n)

            def act_fn(act):
                for i in range(n + 1):
                    if i < n:
                        g, j = units[i]
                        act.wait_ge(at_nb.sem, at_nb.at("act", i))
                        if i >= 2:
                            act.wait_ge(at_t.sem, at_t.at("act", i - 2))
                        if g["sinks"]:
                            nc.scalar.activation(col(i, 4), g["sinks"][j], ACT.Exp, bias=col(i, 2))
                        nc.scalar.activation(probs[i % 2][:, 0:nk(g)], s_all(i, g), ACT.Exp, bias=col(i, 2), scale=scale,
                                             accum_out=col(i, 3)).then_inc(at_p.sem, 1)
                    if i >= 1:
                        u = i - 1
                        g, j = units[u]
                        gi = u // 4
                        act.wait_ge(at_t.sem, at_t.at("act", u))
                        if j == 0 and gi >= 2:
                            act.wait_ge(at_o.sem, at_o.at("act", gi - 2))
                        kt = len(key_tiles(g))
                        src = PS[:, 4:6, :].rearrange("p a b -> p (a b)")[:, 0:kt * P].rearrange("p (a b) -> p a b", a=kt)
                        nc.scalar.activation(turned[gi % 2][:, 0:kt, j * P:j * P + P], src, ACT.Copy).then_inc(at_tc.sem, 1)
                        if j == 3:
                            act.wait_ge(at_o.sem, at_o.at("act", gi))
                            g["put"](PS[0:g["m"], 6 + gi % 2, :].rearrange("p (h q) -> p h q", h=4)).then_inc(at_oc.sem, 1)
                at_nb.advance("act", n)
                at_t.advance("act", n)
                at_o.advance("act", len(groups))

            return pe_fn, act_fn, dve_fn

        qa, ka, oa, qb = (area(3072 * i, 4, TOK) for i in range(4))
        kb, gi, gf = area(12288, TOK), area(13056, TOK), area(13824, TOK)
        va = area(14592, 6, 512)
        vb = area(17664, 6, P)

        def to(dst):
            return lambda lo, hi: dst[:, lo:hi]

        def ab_plan():
            t = [ftile(x_h, ALL, "act", copy_act(to(qa[:, m, :]))) for m in range(4)]
            t += [ftile(x_h, ALL, "act", copy_act(to(ka[:, m, :]), P ** -0.5)) for m in range(4)]
            t += [ftile(x_h, ALL, "act", copy_act(to(oa[:, m, :]))) for m in range(4)]
            t += [ftile(x_h, ALL, "dve", copy_dve(to(qb[:, m, :]))) for m in range(4)]
            t += [ftile(x_h, ALL, "dve", copy_dve(to(d))) for d in (kb, gi, gf)]
            for half in range(2):
                t.append(ttile(x_h, range(NT), 2, "act",
                               copy_act(lambda lo, hi, half=half: va[:, lo // P, 256 * half:256 * half + 256])))
            t.append(ttile(x_h, range(NT), 1, "dve", copy_dve(lambda lo, hi: vb[:, lo // P, :])))
            return t

        def residual(l, gate, m):
            def ev(eng, ps, lo, hi):
                for s, a, b in streams(lo, hi):
                    ins = nc.vector.scalar_tensor_tensor(out=X[:, m, a:b], in0=ps[:, a - lo:b - lo],
                                                         scalar=mods[:, l, s, gate + m:gate + m + 1],
                                                         in1=X[:, m, a:b], op0=ALU.mult, op1=ALU.add)
                return ins
            return ev

        def out_plan(l, segs):
            return [ftile(x_h, segs, "dve", residual(l, 16, m)) for m in range(KD)]

        def relu_sq(dst):
            def ev(eng, ps, lo, hi):
                d = dst(lo, hi)
                v_link(eng, nc.vector.tensor_scalar(d, ps, 0.0, None, ALU.max))
                return nc.vector.tensor_tensor(d, d, d, ALU.mult)
            return ev

        def mlp_plans(l, segs):
            hid = area(0, FF1 // P, TOK)
            up = [ftile(x_h, segs, "dve", relu_sq(to(hid[:, m, :]))) for m in range(FF1 // P)]
            down = [ftile(lambda k, lo, hi: hid[:, k, lo:hi], segs, "dve", residual(l, 40, m), kt=FF1 // P) for m in range(KD)]
            return up, down

        F_, g_ = gf[0:64, :], gi[0:64, :]
        G_, EM, T1, T2 = (H[0:64, 4 + i, :] for i in range(4))
        gt = small[:, 0:48].rearrange("p (t d h) -> p t d h", t=6, d=2)
        gt_ready, gate_rows, gate_act, gate_abs = (signal(n) for n in ("gates_turned", "gate_rows_ready", "gate_logs_ready", "gate_args_ready"))

        def gates_act(act):
            a_link(act, nc.scalar.activation(F_, F_, ACT.Identity, bias=V("gb_f")[0:64]))
            nc.scalar.activation(g_, g_, ACT.Identity, bias=V("gb_i")[0:64])
            a_link(act, nc.scalar.activation(T1, F_, ACT.Abs))
            a_link(act, nc.scalar.activation(T1, T1, ACT.Exp, scale=-1.0))
            nc.scalar.activation(T1, T1, ACT.Ln, bias=V("one")[0:64]).then_inc(gate_act.sem, 1)
            act.wait_ge(gate_abs.sem, 1)
            nc.scalar.activation(EM, EM, ACT.Exp, scale=-1.0).then_inc(gate_act.sem, 1)
            act.wait_ge(gt_ready.sem, 1)
            nc.scalar.activation(gt, PS[:, 0, 0:384].rearrange("p (t d h) -> p t d h", t=6, d=2)[:, :, :, 0:4], ACT.Copy)

        def gates_dve(dve):
            v_link(dve, nc.vector.memset(T2, 0.0))
            dve.wait_ge(gate_act.sem, 1)
            v_link(dve, nc.vector.scalar_tensor_tensor(out=T1, in0=F_, scalar=0.0, in1=T1, op0=ALU.min, op1=ALU.subtract))

            def scan(dst, src, other, op, start):
                v_link(dve, nc.vector.tensor_tensor_scan(dst[0:32, :], src[0:32, :], other[0:32, :], start, op, op))
                v_link(dve, nc.vector.tensor_tensor_scan(dst[32:64, 0:CTX][:, ::-1], src[32:64, 0:CTX][:, ::-1],
                                                         other[32:64, 0:CTX][:, ::-1], start, op, op))
                v_link(dve, nc.vector.tensor_tensor_scan(dst[32:64, CTX:TOK][:, ::-1], src[32:64, CTX:TOK][:, ::-1],
                                                         other[32:64, CTX:TOK][:, ::-1], dst[32:64, 0:1], op, op))

            scan(F_, T1, T2, ALU.add, 0.0)
            nc.vector.tensor_tensor(g_, g_, F_, ALU.subtract).then_inc(gate_rows.sem, 1)
            dve.wait_ge(gate_rows.sem, 1)
            scan(G_, g_, g_, ALU.max, 0.0)
            nc.vector.tensor_tensor(EM, F_, G_, ALU.add).then_inc(gate_abs.sem, 1)

        def gates_pe(pe):
            pe.wait_ge(gate_rows.sem, 1)
            for t in range(NT):
                ins = pe.transpose(PS[:, 0, 64 * t:64 * t + 64], gi[0:64, P * t:P * t + P], C("ident")[0:64, 0:64])
            ins.then_inc(gt_ready.sem, 1)

        W_ = area(18432, 2, 6, 512)
        PASSES = [(h, seg) for h in range(4) for seg in ((0, CTX), (CTX, TOK))]

        def reach(d, s, lo, hi):
            if s * P < lo:
                return 0, hi - lo, None
            q = s * P - lo
            return (q, hi - lo, q) if d == 0 else (0, q + P, q)

        ml_g, ml_diag, ml_e = signal("row_max_spread"), signal("diagonal_args_ready"), signal("decays_ready")
        ml_s, ml_w = signal("mlstm_scores_ready"), signal("weighted_scores_ready")
        ml_em, ml_nd, ml_abs, ml_h = (signal(n) for n in ("exp_minus_m_spread", "num_den_ready", "abs_den_ready", "mlstm_head_done"))
        DG = [H[:, 6, 0:768], H[:, 7, 0:512]]

        def diag_buf(d, s):
            return H[:, 6 + d, P * s:P * s + P]

        def mlstm_pe(pe):
            for i, (h, (lo, hi)) in enumerate(PASSES):
                w = hi - lo
                if i >= 1:
                    pe.wait_ge(ml_h.sem, i)
                for d, sel in enumerate(("self", "selb")):
                    ins = pe.matmul(PS[:, d, 0:w], C(sel, P * h)[0:64], G_[:, lo:hi], start=True, stop=True)
                ins.then_inc(ml_g.sem, 1)
                ns = hi // P
                for s in range(ns):
                    if ml_s.seen.get("pe", 0) >= 2:
                        pe.wait_ge(ml_w.sem, ml_s.seen["pe"] - 1)
                    pe.matmul(PS[:, 2 + ml_s.seen.get("pe", 0) % 2, 0:w], ka[:, h, P * s:P * s + P], qa[:, h, lo:hi],
                              start=True, stop=True).then_inc(ml_s.sem, 1)
                    ml_s.advance("pe", 1)
                pe.wait_ge(ml_e.sem, ml_e.next("pe"))
                for d, sel in enumerate(("self", "selb")):
                    ins = pe.matmul(PS[:, d, 0:w], C(sel, P * h)[0:64], EM[:, lo:hi], start=True, stop=True)
                ins.then_inc(ml_em.sem, 1)
                pe.wait_ge(ml_w.sem, ml_s.seen["pe"])
                for d in range(2):
                    order = list(range(ns))
                    if d == 1 and lo == 0:
                        order.reverse()
                    for k, s in enumerate(order):
                        a, b, _ = reach(d, s, lo, hi)
                        pe.matmul(PS[:, 4 + 2 * d, a:b], va[:, s, P * h:P * h + P], W_[:, d, s, a:b], start=(k == 0), stop=(k == ns - 1))
                    for k, s in enumerate(order):
                        a, b, _ = reach(d, s, lo, hi)
                        ins = pe.matmul(PS[:, 5 + 2 * d, a:b], C("ones"), W_[:, d, s, a:b], start=(k == 0), stop=(k == ns - 1))
                    ins.then_inc(ml_nd.sem, 1)

        def mlstm_act(act):
            for i, (h, (lo, hi)) in enumerate(PASSES):
                act.wait_ge(ml_g.sem, i + 1)
                act.wait_ge(ml_diag.sem, i + 1)
                if i >= 1:
                    act.wait_ge(ml_nd.sem, 2 * i)
                for s in range(hi // P):
                    for d in range(2):
                        a, b, q = reach(d, s, lo, hi)
                        bias = gt[:, s, d, h:h + 1]
                        if q is not None:
                            ins = nc.scalar.activation(W_[:, d, s, q:q + P], diag_buf(d, s), ACT.Exp, bias=bias)
                            a, b = (q + P, b) if d == 0 else (a, q)
                        if b > a:
                            ins = nc.scalar.activation(W_[:, d, s, a:b], PS[:, d, a:b], ACT.Exp, bias=bias, scale=-1.0)
                ins.then_inc(ml_e.sem, 1)
                for d in range(2):
                    act.wait_ge(ml_nd.sem, 2 * i + d + 1)
                    nc.scalar.activation((rstd, mean)[d][:, 0:hi - lo], PS[:, 5 + 2 * d, 0:hi - lo], ACT.Abs).then_inc(ml_abs.sem, 1)

        def mlstm_dve(dve):
            n_s = 0
            for i, (h, (lo, hi)) in enumerate(PASSES):
                w = hi - lo
                dve.wait_ge(ml_g.sem, i + 1)
                for s in range(lo // P, hi // P):
                    for d, mask in enumerate(("neg_ge", "neg_le")):
                        q = s * P - lo
                        ins = nc.vector.scalar_tensor_tensor(out=diag_buf(d, s), in0=PS[:, d, q:q + P], scalar=-1.0, in1=C(mask),
                                                             op0=ALU.mult, op1=ALU.add)
                ins.then_inc(ml_diag.sem, 1)
                dve.wait_ge(ml_e.sem, i + 1)
                for s in range(hi // P):
                    n_s += 1
                    dve.wait_ge(ml_s.sem, n_s)
                    for d in range(2):
                        a, b, _ = reach(d, s, lo, hi)
                        ins = nc.vector.tensor_tensor(W_[:, d, s, a:b], W_[:, d, s, a:b], PS[:, 2 + (n_s - 1) % 2, a:b], ALU.mult)
                    ins.then_inc(ml_w.sem, 1)
                dve.wait_ge(ml_em.sem, i + 1)
                for d in range(2):
                    r = (rstd, mean)[d][:, 0:w]
                    dve.wait_ge(ml_abs.sem, 2 * i + d + 1)
                    v_link(dve, nc.vector.tensor_tensor(r, r, PS[:, d, 0:w], ALU.max))
                    v_link(dve, nc.vector.reciprocal(r, r))
                    if d == 0:
                        v_link(dve, nc.vector.tensor_tensor(H[:, h, lo:hi], r, PS[:, 4, 0:w], ALU.mult))
                    else:
                        v_link(dve, nc.vector.tensor_tensor(r, r, PS[:, 6, 0:w], ALU.mult))
                        nc.vector.tensor_tensor(H[:, h, lo:hi], H[:, h, lo:hi], r, ALU.add).then_inc(ml_h.sem, 1)

        def sig_o_act(act):
            for h in range(4):
                nc.scalar.activation(oa[:, h, :], oa[:, h, :], ACT.Sigmoid)

        mlstm_out = head_norm([(H[:, h, a:b], H[:, h, a:b], "ones", 1.0 / P, "eps1", V("mlstm_g", h), oa[:, h, a:b])
                               for h in range(4) for a, b in ALL], 18432)
        qk_norm_b = head_norm([(qb[:, m, a:b], qb[:, m, a:b], "blk64", 1.0 / 64, "eps1", V("swa_q"), None)
                               for m in range(4) for a, b in ALL]
                              + [(kb[:, a:b], kb[:, a:b], "blk64", 1.0 / 64, "eps1", V("swa_k"), None) for a, b in ALL], 18432)
        rope_b = rope([qb[:, m, CTX:TOK] for m in range(4)] + [kb[:, CTX:TOK]], 64, 18432)
        kd = area(0, 2, TOK)
        dup_ready = signal("keys_doubled")

        def dup_pe(pe):
            for n in range(2):
                for j, (a, b) in enumerate(ALL):
                    ins = pe.matmul(PS[:, 2 * n + j, 0:b - a], C(f"dup{n}"), kb[:, a:b], start=True, stop=True)
            ins.then_inc(dup_ready.sem, 1)

        def dup_act(act):
            act.wait_ge(dup_ready.sem, 1)
            for n in range(2):
                for j, (a, b) in enumerate(ALL):
                    nc.scalar.activation(kd[:, n, a:b], PS[:, 2 * n + j, 0:b - a], ACT.Copy)

        def b_groups():
            out = []
            for blk in range(NT):
                if blk < NCT:
                    lat, masks = None, []
                else:
                    a, b = max(blk - 1, NCT), min(blk + 2, NT)
                    lat = (a * P, b * P)
                    masks = [(CTX + (t - a) * P, m) for t, m in ((blk - 1, "neg_ge"), (blk + 1, "neg_le")) if a <= t < b]
                for kv in range(2):
                    heads = [4 * kv + j for j in range(4)]
                    half = [64 * (h % 2) for h in heads]

                    def put(ps, kv=kv, blk=blk):
                        for par in range(2):
                            ins = nc.scalar.activation(H[64 * par:64 * par + 64, 4 + 2 * kv:6 + 2 * kv, blk * P:blk * P + P],
                                                       ps[:, par::2, :], ACT.Copy)
                        return ins

                    out.append(dict(q=[qb[o:o + 64, h // 2, blk * P:blk * P + P] for h, o in zip(heads, half)],
                                    k=[kd[o:o + 64, kv, :] for o in half], v=lambda kt, kv=kv: vb[:, kt, 64 * kv:64 * kv + 64],
                                    lat=lat, masks=masks, sinks=[V("sink", h) for h in heads], put=put, m=64))
            return out

        attn_b = attention(b_groups(), 64 ** -0.5, 3072, 18432)

        qc = area(0, 8, 512)
        kc = area(4096, 2, TOK)
        vc = area(5632, 6, 256)

        def c_plan():
            t = [ftile(x_h, LAT, "act", copy_act(to_lat(qc[:, m, :]))) for m in range(8)]
            t += [ftile(x_h, ALL, "dve", copy_dve(to(kc[:, m, :]))) for m in range(2)]
            t.append(ttile(x_h, range(NT), 2, "act", copy_act(lambda lo, hi: vc[:, lo // P, :])))
            return t

        def to_lat(dst):
            return lambda lo, hi: dst[:, lo - CTX:hi - CTX]

        qk_norm_c = head_norm([(qc[:, m, :], qc[:, m, :], "ones", 1.0 / P, "eps1", V("c_q"), None) for m in range(8)]
                              + [(kc[:, m, a:b], kc[:, m, a:b], "ones", 1.0 / P, "eps1", V("c_k"), None) for m in range(2) for a, b in ALL], 18432)
        rope_c = rope([qc[:, m, :] for m in range(8)] + [kc[:, m, CTX:TOK] for m in range(2)], 128, 18432)

        def c_groups():
            out = []
            for blk in range(NLT):
                for kv in range(2):
                    def put(ps, kv=kv, blk=blk):
                        return nc.scalar.activation(H[:, 4 * kv:4 * kv + 4, CTX + blk * P:CTX + blk * P + P], ps, ACT.Copy)
                    out.append(dict(q=[qc[:, 4 * kv + j, blk * P:blk * P + P] for j in range(4)], k=[kc[:, kv, :]] * 4,
                                    v=lambda kt, kv=kv: vc[:, kt, P * kv:P * kv + P], lat=(CTX, TOK), masks=[], sinks=None, put=put, m=P))
            return out

        attn_c = attention(c_groups(), P ** -0.5, 7168, 8704)

        up_, vp_ = area(0, 2, 512), area(1024, 2, 512)
        qkv = area(2048, 12, 512)
        zp = area(8192, 4, 512)
        be, de = area(10240, 512), area(10752, 512)
        qg, kg = area(11264, 512), area(11776, 512)
        rg = area(12288, 2, 512)
        gl = area(13312, 512)
        vg = area(13824, 4, 256)
        ktok, vtok = area(14848, 4, 512), area(16896, 4, 512)
        SC = 14848
        XL = X[:, :, CTX:TOK]
        Y = H[:, :, CTX:TOK]

        def x_x(k, lo, hi):
            return X[:, k, lo:hi]

        def ffn_plans(l):
            hid = area(0, FF2 // P, 512)
            up = []
            for m in range(FF2 // P):
                a = ftile(x_x, LAT, "act", lambda eng, ps, lo, hi, m=m: nc.scalar.activation(hid[:, m, :], ps, ACT.Silu))
                gate_out = a["outs"][0]

                def times(eng, ps, lo, hi, m=m, gate_out=gate_out):
                    eng.wait_ge(evac["act"].sem, gate_out.freed)
                    return nc.vector.tensor_tensor(hid[:, m, :], hid[:, m, :], ps, ALU.mult)

                up += [a, ftile(x_x, LAT, "dve", times)]

            def skip_add(m):
                def ev(eng, ps, lo, hi):
                    v_link(eng, nc.vector.tensor_scalar(X[:, m, lo:hi], X[:, m, lo:hi], ALPHA, None, ALU.mult))
                    return nc.vector.scalar_tensor_tensor(out=X[:, m, lo:hi], in0=ps, scalar=0.5, in1=X[:, m, lo:hi],
                                                          op0=ALU.mult, op1=ALU.add)
                return ev

            down = [ftile(lambda k, lo, hi: hid[:, k, :], LAT, "dve", skip_add(m), kt=FF2 // P) for m in range(KD)]
            return up, down

        def in_plan():
            dsts = [up_[:, 0, :], up_[:, 1, :], vp_[:, 0, :], vp_[:, 1, :]] + [qkv[:, m, :] for m in range(12)] \
                + [zp[:, m, :] for m in range(4)] + [be, de, qg, kg, rg[:, 0, :], rg[:, 1, :], gl]
            t = [ftile(x_x, LAT, "act" if i % 2 else "dve", (copy_act if i % 2 else copy_dve)(to_lat(d))) for i, d in enumerate(dsts)]
            t.append(ttile(x_x, range(NCT, NT), 2, "act", copy_act(lambda lo, hi: vg[:, lo // P - NCT, :])))
            return t

        def mix_plan():
            def ev_for(m):
                def ev(eng, ps, lo, hi):
                    v_link(eng, nc.vector.tensor_scalar(X[:, m, lo:hi], X[:, m, lo:hi], ALPHA, None, ALU.mult))
                    return nc.vector.tensor_tensor(X[:, m, lo:hi], X[:, m, lo:hi], ps, ALU.add)
                return ev
            return [ftile(x_h, LAT, "dve", ev_for(m)) for m in range(KD)]

        sg_sum, sg_mean, sg_sq, sg_std, sg_v, sg_t, sg_tc, sg_z, sg_w = (signal(n) for n in (
            "sgu_sums", "sgu_centred", "sgu_squares", "sgu_std", "sgu_v_normed", "sgu_v_turned", "sgu_v_token_major", "sgu_mixed", "sgu_w_masked"))
        wsT = area(SC, 4, P)
        bs_row = area(SC + 512, 512)
        gup = area(SC + 1024, P)
        vt = area(SC + 1536, 4, 256)
        sq2 = area(SC + 2560, 2, 512)

        def sgu_act(act):
            for t in range(2):
                nc.scalar.activation(vp_[:, t, :], vp_[:, t, :], ACT.Gelu_apprx_tanh).then_inc(sg_sum.sem, 1)
            for t in range(2):
                nc.scalar.activation(up_[:, t, :], up_[:, t, :], ACT.Gelu_apprx_tanh)
            act.wait_ge(sg_mean.sem, sg_mean.next("act"))
            for t in range(2):
                ins = nc.scalar.activation(sq2[:, t, :], vp_[:, t, :], ACT.Square)
            ins.then_inc(sg_sq.sem, 1)
            act.wait_ge(sg_t.sem, sg_t.next("act"))
            nc.scalar.activation(rstd[:], PS[:, 1, :], ACT.Sqrt, bias=V("eps2"), scale=1.0 / 256).then_inc(sg_std.sem, 1)
            act.wait_ge(sg_t.sem, sg_t.next("act"))
            nc.scalar.activation(vt[:, 0:2, :], PS[:, 2, :].rearrange("p (a b) -> p a b", a=2), ACT.Copy)
            nc.scalar.activation(vt[:, 2:4, :], PS[:, 3, :].rearrange("p (a b) -> p a b", a=2), ACT.Copy).then_inc(sg_tc.sem, 1)

        def sgu_pe(pe):
            pe.wait_ge(sg_sum.sem, sg_sum.next("pe", 2))
            for t in range(2):
                ins = pe.matmul(PS[:, 0, :], C("ones"), vp_[:, t, :], start=(t == 0), stop=(t == 1))
            ins.then_inc(sg_z.sem, 1)
            pe.wait_ge(sg_sq.sem, sg_sq.next("pe"))
            for t in range(2):
                ins = pe.matmul(PS[:, 1, :], C("ones"), sq2[:, t, :], start=(t == 0), stop=(t == 1))
            ins.then_inc(sg_t.sem, 1)
            pe.wait_ge(sg_v.sem, sg_v.next("pe"))
            for n in range(NLT):
                for t in range(2):
                    ins = pe.transpose(PS[:, 2 + n // 2, 256 * (n % 2) + P * t:256 * (n % 2) + P * t + P],
                                       vp_[:, t, P * n:P * n + P], C("ident"))
            ins.then_inc(sg_t.sem, 1)
            pe.wait_ge(sg_tc.sem, sg_tc.next("pe"))
            pe.wait_ge(sg_w.sem, sg_w.next("pe"))
            for h in range(4):
                o = 64 * (h % 2)
                for n in range(NLT):
                    dst = PS[o:o + 64, 4 + h // 2, P * n:P * n + P]
                    pe.matmul(dst, vt[:, n, 64 * h:64 * h + 64], wsT[:, h, :], start=True, stop=False)
                    ins = pe.matmul(dst, C("ones")[0:1, 0:64], bs_row[0:1, P * h:P * h + P], start=False, stop=True)
            ins.then_inc(sg_z.sem, 1)

        def sgu_dve(dve, l):
            dve.wait_ge(small_loaded.sem, 64 + 48 * l)
            nc.vector.tensor_tensor(wsT, wsT, C("m_ge").unsqueeze(1).to_broadcast([P, 4, P]), ALU.mult).then_inc(sg_w.sem, 1)
            dve.wait_ge(sg_z.sem, sg_z.next("dve"))
            v_link(dve, nc.vector.tensor_scalar(mean[:], PS[:, 0, :], 1.0 / 256, None, ALU.mult))
            for t in range(2):
                ins = nc.vector.tensor_tensor(vp_[:, t, :], vp_[:, t, :], mean[:], ALU.subtract)
            ins.then_inc(sg_mean.sem, 1)
            dve.wait_ge(sg_mean.sem, sg_mean.next("dve"))
            dve.wait_ge(sg_std.sem, sg_std.next("dve"))
            v_link(dve, nc.vector.reciprocal(rstd[:], rstd[:]))
            for t in range(2):
                v_link(dve, nc.vector.tensor_tensor(vp_[:, t, :], vp_[:, t, :], rstd[:], ALU.mult))
                ins = nc.vector.tensor_scalar(vp_[:, t, :], vp_[:, t, :], V("sgu_g", 2 * l + t), V("sgu_b", 2 * l + t), ALU.mult, ALU.add)
            ins.then_inc(sg_v.sem, 1)
            dve.wait_ge(sg_z.sem, sg_z.next("dve"))
            for t in range(2):
                nc.vector.tensor_tensor(Y[:, t, :], up_[:, t, :], PS[:, 4 + t, :], ALU.mult)

        bc, qd_, kx, kdec = (area(SC + 2048 + 512 * i, 512) for i in range(4))
        kdt = area(SC + 4096, 4, P)
        pTg = area(SC + 4608, 4, 512)
        Sg = area(SC + 6656, 9, 256)
        blocks = area(0, 256)
        gtg = small[:, 48:56]
        (ga_low, ga_arg, ga_log, ga_cum, ga_exp, ga_prod, ga_kt, ga_ktc, ga_s, ga_pt, ga_st, ga_state, ga_o) = (signal(n) for n in (
            "gla_gate_product", "gla_gate_arg", "gla_gate_log", "gla_decay_sums", "gla_decays", "gla_decayed_qk", "gla_k_turned",
            "gla_k_token_major", "gla_scores", "gla_scores_masked", "gla_updates", "gla_states", "gla_outputs"))

        GS = (0, 1, 6, 7)

        def update_bank(c):
            return PS[:, 2 + 2 * (c % 2) + c // 4, 256 * (c // 2 % 2):256 * (c // 2 % 2) + 256]

        def gla_act(act, l):
            act.wait_ge(ga_low.sem, ga_low.next("act"))
            a_link(act, nc.scalar.activation(bc, PS[:, 0, :], ACT.Identity, bias=V("gla_gb", l)))
            a_link(act, nc.scalar.activation(qd_, bc, ACT.Abs))
            a_link(act, nc.scalar.activation(qd_, qd_, ACT.Exp, scale=-1.0))
            nc.scalar.activation(qd_, qd_, ACT.Ln, bias=V("one")).then_inc(ga_log.sem, 1)
            act.wait_ge(ga_cum.sem, ga_cum.next("act"))
            nc.scalar.activation(qd_, bc, ACT.Exp)
            nc.scalar.activation(gtg, bc.rearrange("p (c t) -> p c t", t=64)[:, :, 63], ACT.Exp)
            nc.scalar.activation(kx, bc, ACT.Exp, scale=-1.0)
            nc.scalar.activation(kdec, kdec, ACT.Exp).then_inc(ga_exp.sem, 1)
            act.wait_ge(ga_kt.sem, ga_kt.next("act"))
            nc.scalar.activation(kdt, PS[:, 1, :].rearrange("p (a b) -> p a b", a=4), ACT.Copy).then_inc(ga_ktc.sem, 1)

        def gla_dve(dve, l):
            dve.wait_ge(ga_log.sem, ga_log.next("dve"))
            v_link(dve, nc.vector.scalar_tensor_tensor(out=bc, in0=bc, scalar=0.0, in1=qd_, op0=ALU.min, op1=ALU.subtract))
            v_link(dve, nc.vector.tensor_scalar(kx, bc, 1.0 / 16.0, None, ALU.mult))
            v_link(dve, nc.vector.tensor_tensor_scan(bc, C("rs64", 0, 512), kx, 0.0, ALU.mult, ALU.add))
            b3 = bc.rearrange("p (c t) -> p c t", t=64)
            nc.vector.tensor_tensor(kdec.rearrange("p (c t) -> p c t", t=64), b3[:, :, 63:64].to_broadcast([P, 8, 64]), b3,
                                    ALU.subtract).then_inc(ga_cum.sem, 1)
            dve.wait_ge(ga_exp.sem, ga_exp.next("dve"))
            nc.vector.scalar_tensor_tensor(out=qd_, in0=qg, scalar=32 ** -0.5, in1=qd_, op0=ALU.mult, op1=ALU.mult)
            nc.vector.tensor_tensor(kx, kx, kg, ALU.mult)
            nc.vector.tensor_tensor(kdec, kdec, kg, ALU.mult).then_inc(ga_prod.sem, 1)
            v_link(dve, nc.vector.memset(Sg[:, 0, :], 0.0))
            dve.wait_ge(ga_st.sem, ga_st.next("dve"))
            for c in range(7):
                nc.vector.tensor_scalar(Sg[:, c + 1, :], Sg[:, c, :], gtg[:, c:c + 1], None, ALU.mult)
                v_link(dve, nc.vector.tensor_tensor(blocks, update_bank(c), C("bd_gla", 0, 256), ALU.mult))
                v_link(dve, nc.vector.tensor_tensor(Sg[:, c + 1, :], Sg[:, c + 1, :], blocks, ALU.add))
            for h in range(4):
                dve.wait_ge(ga_s.sem, ga_s.next("dve"))
                nc.vector.tensor_tensor(pTg[:, :, P * h:P * h + P], PS[:, GS[h], :].rearrange("p (n t) -> p n t", n=4),
                                        C("m_gla").unsqueeze(1).to_broadcast([P, 4, P]), ALU.mult).then_inc(ga_pt.sem, 1)
            dve.wait_ge(ga_o.sem, ga_o.next("dve"))
            for p in range(2):
                nc.vector.tensor_copy(Y[:, 6 + p, :], PS[:, 6 + p, :])

        def gla_pe(pe, l):
            pe.wait_ge(small_loaded.sem, 64 + 48 * l)
            pe.matmul(PS[:, 0, :], gup[0:16, :], gl[0:16, :], start=True, stop=True).then_inc(ga_low.sem, 1)
            pe.wait_ge(ga_prod.sem, ga_prod.next("pe"))
            for n in range(NLT):
                ins = pe.transpose(PS[:, 1, P * n:P * n + P], kdec[:, P * n:P * n + P], C("ident"))
            ins.then_inc(ga_kt.sem, 1)
            pe.wait_ge(ga_ktc.sem, ga_ktc.next("pe"))
            for c in range(7):
                o, n = 64 * (c % 2), c // 2
                ins = pe.matmul(update_bank(c), kdt[o:o + 64, n, :], vg[o:o + 64, n, :], start=True, stop=True)
            ins.then_inc(ga_st.sem, 1)
            for h in range(4):
                for n in range(NLT):
                    a, b = 32 * h, P * n
                    ins = pe.matmul(PS[:, GS[h], b:b + P], kx[a:a + 32, b:b + P], qd_[a:a + 32, b:b + P], start=True, stop=True)
                ins.then_inc(ga_s.sem, 1)
            pe.wait_ge(ga_pt.sem, ga_pt.next("pe", 4))
            for n in range(NLT):
                for p in range(2):
                    for j in range(2):
                        h = 2 * p + j
                        pe.matmul(PS[64 * j:64 * j + 64, 6 + p, P * n:P * n + P], vg[:, n, 64 * h:64 * h + 64],
                                  pTg[:, n, P * h:P * h + P], start=True, stop=False, skip_group_check=True)
                    for c in (2 * n, 2 * n + 1):
                        ins = pe.matmul(PS[:, 6 + p, 64 * c:64 * c + 64], Sg[:, c, P * p:P * p + P], qd_[:, 64 * c:64 * c + 64],
                                        start=False, stop=True, skip_group_check=True)
            ins.then_inc(ga_o.sem, 1)

        def silu_act(tiles):
            def fn(act):
                for t in tiles:
                    nc.scalar.activation(t, t, ACT.Silu)
            return fn

        silu_r, silu_z = silu_act([rg[:, i, :] for i in range(2)]), silu_act([zp[:, i, :] for i in range(4)])
        gla_norm = [head_norm([(Y[:, 6 + p, :], Y[:, 6 + p, :], "blk64", 1.0 / 64, "eps2", V("gla_g", l), rg[:, p, :]) for p in range(2)], SC)
                    for l in range(2)]

        cv, cv_done = signal("convolved"), signal("silu_of_conv_done")

        def conv_dve(dve, l):
            for t in range(12):
                y = area(SC + 512 * (t % 2), 512)
                x = qkv[:, t, :]
                if t >= 2:
                    dve.wait_ge(cv_done.sem, cv_done.at("dve", t - 2))
                tap = [V("conv", 48 * l + 12 * i + t) for i in range(4)]
                v_link(dve, nc.vector.tensor_scalar(y, x, tap[3], None, ALU.mult))
                for back in range(1, 4):
                    ins = nc.vector.scalar_tensor_tensor(out=y[:, back:], in0=x[:, 0:512 - back], scalar=tap[3 - back], in1=y[:, back:],
                                                         op0=ALU.mult, op1=ALU.add)
                    if back < 3:
                        v_link(dve, ins)
                ins.then_inc(cv.sem, 1)
            cv_done.advance("dve", 12)

        def conv_act(act, l):
            for t in range(12):
                act.wait_ge(cv.sem, cv.next("act"))
                nc.scalar.activation(qkv[:, t, :], area(SC + 512 * (t % 2), 512), ACT.Silu).then_inc(cv_done.sem, 1)

        l2_qk = head_norm([(qkv[:, t, :], qkv[:, t, :], "blk64", 1.0, "epsl", 0.125 if t < 4 else 1.0, None) for t in range(8)], SC)
        R4 = area(18944, 512)
        R4T = area(19456, 4, P)
        bk = area(19968, 4, 512)
        wT = area(22016, 4, 512)
        ub = area(6144, 4, 512)
        (gr_exp, gr_rows, gr_r4, gr_t, gr_tc, gr_kv, gr_kvc) = (signal(n) for n in (
            "gdn_gate_exps", "gdn_row_args", "gdn_rows", "gdn_rows_turned", "gdn_rows_token_major", "gdn_kv_turned", "gdn_kv_token_major"))

        def rows_act(act, l):
            r = de[0:8]
            s0, s1 = rstd[0:8, :], mean[0:8, :]
            a_link(act, nc.scalar.activation(r, r, ACT.Identity, bias=V("dt_b", l)[0:8]))
            a_link(act, nc.scalar.activation(s0, r, ACT.Abs))
            a_link(act, nc.scalar.activation(s0, s0, ACT.Exp, scale=-1.0))
            nc.scalar.activation(s0, s0, ACT.Ln, bias=V("one")[0:8])
            nc.scalar.activation(small[0:8, 56:57], V("a_log", l)[0:8], ACT.Exp).then_inc(gr_exp.sem, 1)
            act.wait_ge(gr_rows.sem, gr_rows.next("act"))
            nc.scalar.activation(R4[0:8, :], be[0:8, :], ACT.Sigmoid)
            nc.scalar.activation(R4[32:40, :], r, ACT.Copy)
            nc.scalar.activation(R4[64:72, :], s1, ACT.Exp)
            nc.scalar.activation(R4[96:104, :], r, ACT.Exp).then_inc(gr_r4.sem, 1)
            act.wait_ge(gr_t.sem, gr_t.next("act"))
            nc.scalar.activation(R4T, PS[:, 0, :].rearrange("p (a b) -> p a b", a=4), ACT.Copy).then_inc(gr_tc.sem, 1)
            for i in range(8):
                act.wait_ge(gr_kv.sem, gr_kv.next("act"))
                nc.scalar.activation((ktok, vtok)[i // 4][:, i % 4, :], PS[:, 1 + i % 4, :], ACT.Copy).then_inc(gr_kvc.sem, 1)

        def rows_dve(dve, l):
            r = de[0:8]
            s0, s1 = rstd[0:8, :], mean[0:8, :]
            v_link(dve, nc.vector.memset(R4, 0.0))
            dve.wait_ge(gr_exp.sem, gr_exp.next("dve"))
            v_link(dve, nc.vector.scalar_tensor_tensor(out=s0, in0=r, scalar=0.0, in1=s0, op0=ALU.max, op1=ALU.add))
            v_link(dve, nc.vector.tensor_scalar(s0, s0, small[0:8, 56:57], -1.0, ALU.mult, ALU.mult))
            v_link(dve, nc.vector.tensor_tensor_scan(r, C("rs128", 0, 512)[0:8], s0, 0.0, ALU.mult, ALU.add))
            r3 = r.rearrange("p (c t) -> p c t", t=P)
            nc.vector.tensor_tensor(s1.rearrange("p (c t) -> p c t", t=P), r3[:, :, P - 1:P].to_broadcast([8, 4, P]), r3,
                                    ALU.subtract).then_inc(gr_rows.sem, 1)
            dve.wait_ge(gr_tc.sem, gr_tc.next("dve"))
            v_link(dve, nc.vector.tensor_tensor(R4T[:, :, 96:104], R4T[:, :, 96:104], R4T[:, :, 0:8], ALU.mult))
            for n in range(4):
                def heads(t):
                    return t[:, n, :].rearrange("p (h d) -> p h d", h=8)

                def per_head(c):
                    return R4T[:, n, c:c + 8].unsqueeze(2).to_broadcast([P, 8, 64])

                dve.wait_ge(gr_kvc.sem, gr_kvc.at("dve", n))
                v_link(dve, nc.vector.tensor_tensor(heads(bk), heads(ktok), per_head(96), ALU.mult))
                nc.vector.tensor_tensor(heads(ktok), heads(ktok), per_head(64), ALU.mult)
            for n in range(4):
                dve.wait_ge(gr_kvc.sem, gr_kvc.at("dve", 4 + n))
                nc.vector.tensor_tensor(vtok[:, n, :].rearrange("p (h d) -> p h d", h=8), vtok[:, n, :].rearrange("p (h d) -> p h d", h=8),
                                        R4T[:, n, 0:8].unsqueeze(2).to_broadcast([P, 8, 64]), ALU.mult)
            gr_kvc.advance("dve", 8)

        def rows_pe(pe, l):
            pe.wait_ge(gr_r4.sem, gr_r4.next("pe"))
            for n in range(4):
                ins = pe.transpose(PS[:, 0, P * n:P * n + P], R4[:, P * n:P * n + P], C("ident"))
            ins.then_inc(gr_t.sem, 1)
            for i in range(8):
                if i >= 4:
                    pe.wait_ge(gr_kvc.sem, gr_kvc.at("pe", i - 4))
                n = i % 4
                for p in range(4):
                    ins = pe.transpose(PS[:, 1 + n, P * p:P * p + P], qkv[:, 4 + 4 * (i // 4) + p, P * n:P * n + P], C("ident"))
                ins.then_inc(gr_kv.sem, 1)
            gr_kvc.advance("pe", 8)

        class Block4:

            def __init__(self, view):
                self.all = view

            def chunk(self, n):
                return self.all[:, n // 2, P * (n % 2):P * (n % 2) + P]

        def pair(view512):
            return Block4(view512.rearrange("p (a b) -> p a b", a=2))

        sets = [[pair(area(11264 + 512 * i, 512)) for i in range(7)],
                [Block4(H[:, 2 * i:2 * i + 2, 0:CTX]) for i in range(4)] + [Block4(X[:, 2 * i:2 * i + 2, 0:CTX]) for i in range(3)]]

        def pt_of(h):
            return pair(area(512 * h, 512)) if h < 4 else pair(H[:, h - 2, CTX:TOK])

        (so_in, so_arg, so_dec, so_L, so_t, so_tc, so_lb, so_y, so_yc, so_x, so_xn, so_out, so_oc) = (signal(n) for n in (
            "solve_inputs", "solve_decay_args", "solve_decays", "solve_L", "solve_L_turned", "solve_LT", "solve_level_masked",
            "solve_y", "solve_y_copied", "solve_products", "solve_inverse_updated", "solve_outputs", "solve_outputs_copied"))
        LEVELS = 7

        def bank(sidx, i):
            return PS[:, 4 * sidx + i, :]

        def half(h):
            return slice(64 * (h % 2), 64 * (h % 2) + 64)

        def solve_pe(pe):
            for hp in range(4):
                for s in range(2):
                    h = 2 * hp + s
                    if hp >= 1:
                        pe.wait_ge(so_oc.sem, so_oc.next("pe"))
                    pe.matmul(bank(s, 0), C("sel", P * h)[0:8], de[0:8, :], start=True, stop=True)
                    for n in range(4):
                        kk = qkv[half(h), 4 + hp, P * n:P * n + P]
                        pe.matmul(bank(s, 1)[:, P * n:P * n + P], kk, kk, start=True, stop=True)
                    for n in range(4):
                        ins = pe.matmul(bank(s, 2)[:, P * n:P * n + P], qkv[half(h), 4 + hp, P * n:P * n + P],
                                        qkv[half(h), hp, P * n:P * n + P], start=True, stop=True)
                    ins.then_inc(so_in.sem, 1)
                for s in range(2):
                    L = sets[s][1]
                    pe.wait_ge(so_L.sem, so_L.next("pe"))
                    for n in range(4):
                        ins = pe.transpose(bank(s, 3)[:, P * n:P * n + P], L.chunk(n), C("ident"))
                    ins.then_inc(so_t.sem, 1)
                for lv in range(1, LEVELS):
                    for s in range(2):
                        _, _, LT, Xi, XT, Yb, Lb = sets[s]
                        pe.wait_ge(so_lb.sem, so_lb.next("pe"))
                        for n in range(4):
                            ins = pe.matmul(bank(s, 0)[:, P * n:P * n + P], Lb.chunk(n), Xi.chunk(n), start=True, stop=True)
                        ins.then_inc(so_y.sem, 1)
                    for s in range(2):
                        _, _, LT, Xi, XT, Yb, Lb = sets[s]
                        pe.wait_ge(so_yc.sem, so_yc.next("pe"))
                        for n in range(4):
                            if lv < LEVELS - 1:
                                pe.matmul(bank(s, 1)[:, P * n:P * n + P], XT.chunk(n), Yb.chunk(n), start=True, stop=True)
                            ins = pe.matmul(bank(s, 2)[:, P * n:P * n + P], Yb.chunk(n), XT.chunk(n), start=True, stop=True)
                        ins.then_inc(so_x.sem, 1)
                for s in range(2):
                    h = 2 * hp + s
                    XT = sets[s][4]
                    pe.wait_ge(so_xn.sem, so_xn.next("pe"))
                    for n in range(4):
                        pe.matmul(bank(s, 3)[:, 64 * n:64 * n + 64], XT.chunk(n), vtok[:, n, 64 * h:64 * h + 64], start=True, stop=True)
                        ins = pe.matmul(bank(s, 0)[half(h), P * n:P * n + P], bk[:, n, 64 * h:64 * h + 64], XT.chunk(n), start=True, stop=True)
                    ins.then_inc(so_out.sem, 1)
            pe.wait_ge(so_oc.sem, so_oc.next("pe", 2))

        def solve_act(act):
            for hp in range(4):
                for s in range(2):
                    A, L = sets[s][0], sets[s][1]
                    act.wait_ge(so_arg.sem, so_arg.next("act"))
                    nc.scalar.activation(A.all, A.all, ACT.Exp)
                    nc.scalar.activation(L.all, L.all, ACT.Exp, scale=-1.0).then_inc(so_dec.sem, 1)
                for s in range(2):
                    act.wait_ge(so_t.sem, so_t.next("act"))
                    nc.scalar.activation(sets[s][2].all, bank(s, 3).rearrange("p (a b) -> p a b", a=2), ACT.Copy).then_inc(so_tc.sem, 1)
                for lv in range(1, LEVELS):
                    for s in range(2):
                        act.wait_ge(so_y.sem, so_y.next("act"))
                        nc.scalar.activation(sets[s][5].all, bank(s, 0).rearrange("p (a b) -> p a b", a=2), ACT.Copy).then_inc(so_yc.sem, 1)
                for s in range(2):
                    h = 2 * hp + s
                    act.wait_ge(so_out.sem, so_out.next("act"))
                    nc.scalar.activation(ub[:, :, 64 * h:64 * h + 64], bank(s, 3)[:, 0:256].rearrange("p (n d) -> p n d", n=4), ACT.Copy)
                    nc.scalar.activation(wT[half(h), hp, :], bank(s, 0)[half(h), :], ACT.Copy).then_inc(so_oc.sem, 1)

        def solve_dve(dve):
            for hp in range(4):
                for s in range(2):
                    h = 2 * hp + s
                    A, L = sets[s][0], sets[s][1]
                    dve.wait_ge(so_in.sem, so_in.next("dve"))
                    for n in range(4):
                        gam = R4T[:, n, 32 + h:33 + h]
                        g = bank(s, 0)[:, P * n:P * n + P]
                        nc.vector.scalar_tensor_tensor(out=A.chunk(n), in0=g, scalar=gam, in1=C("neg_ge"), op0=ALU.subtract, op1=ALU.add)
                        ins = nc.vector.scalar_tensor_tensor(out=L.chunk(n), in0=g, scalar=gam, in1=C("pos_lt"), op0=ALU.subtract, op1=ALU.add)
                    ins.then_inc(so_arg.sem, 1)
                for s in range(2):
                    h = 2 * hp + s
                    A, L = sets[s][0], sets[s][1]
                    dve.wait_ge(so_dec.sem, so_dec.next("dve"))
                    for n in range(4):
                        ins = nc.vector.scalar_tensor_tensor(out=L.chunk(n), in0=bank(s, 1)[:, P * n:P * n + P], scalar=R4T[:, n, h:h + 1],
                                                             in1=L.chunk(n), op0=ALU.mult, op1=ALU.mult)
                    ins.then_inc(so_L.sem, 1)
                    nc.vector.tensor_tensor(pt_of(h).all, A.all, bank(s, 2).rearrange("p (a b) -> p a b", a=2), ALU.mult)
                for s in range(2):
                    _, L, LT, Xi, XT, _, Lb = sets[s]
                    dve.wait_ge(so_tc.sem, so_tc.next("dve"))
                    for n in range(4):
                        nc.vector.tensor_tensor(Xi.chunk(n), L.chunk(n), C("lev"), ALU.mult)
                        v_link(dve, nc.vector.tensor_tensor(XT.chunk(n), LT.chunk(n), C("levt"), ALU.mult))
                        nc.vector.tensor_tensor(Xi.chunk(n), C("ident"), Xi.chunk(n), ALU.subtract)
                        v_link(dve, nc.vector.tensor_tensor(XT.chunk(n), C("ident"), XT.chunk(n), ALU.subtract))
                for lv in range(1, LEVELS):
                    for s in range(2):
                        LT, Lb = sets[s][2], sets[s][6]
                        if lv == 1:
                            for n in range(4):
                                ins = nc.vector.tensor_tensor(Lb.chunk(n), LT.chunk(n), C("levt", P), ALU.mult)
                            ins.then_inc(so_lb.sem, 1)
                    for s in range(2):
                        _, _, LT, Xi, XT, _, Lb = sets[s]
                        dve.wait_ge(so_x.sem, so_x.next("dve"))
                        ps1, ps2 = (bank(s, i).rearrange("p (a b) -> p a b", a=2) for i in (1, 2))
                        if lv < LEVELS - 1:
                            nc.vector.tensor_tensor(Xi.all, Xi.all, ps1, ALU.subtract)
                            nc.vector.tensor_tensor(XT.all, XT.all, ps2, ALU.subtract)
                            for n in range(4):
                                ins = nc.vector.tensor_tensor(Lb.chunk(n), LT.chunk(n), C("levt", P * (lv + 1)), ALU.mult)
                            ins.then_inc(so_lb.sem, 1)
                        else:
                            nc.vector.tensor_tensor(XT.all, XT.all, ps2, ALU.subtract).then_inc(so_xn.sem, 1)

        S = area(11264, 4, P)
        uu = area(11776, 512)
        tS = area(12288, 4, P)
        egx = area(12800, 512)
        gtot = small[:, 64:80].rearrange("p (q n) -> p q n", q=4)
        (re_eg0, re_eg, re_qd, re_gt, re_gtx, re_w, re_u, re_s, re_sn, re_o) = (signal(n) for n in (
            "rec_exp_rows", "rec_exp_spread", "rec_q_decayed", "rec_total_spread", "rec_total_exp", "rec_w_product", "rec_u", "rec_update", "rec_state", "rec_outputs"))

        def rec_pe(pe):
            for p in range(4):
                ins = pe.matmul(PS[:, 0, 4 * p:4 * p + 4], C("selp", P * p)[0:8], de[0:8, P - 1::P], start=True, stop=True)
            ins.then_inc(re_gt.sem, 1)
            pe.wait_ge(re_eg0.sem, re_eg0.next("pe"))
            for p in range(4):
                if p >= 2:
                    pe.wait_ge(re_qd.sem, re_qd.next("pe"))
                pe.matmul(PS[:, 1 + p % 2, :], C("selp", P * p)[0:8], egx[0:8, :], start=True, stop=True).then_inc(re_eg.sem, 1)
            pe.wait_ge(re_qd.sem, re_qd.next("pe", 2))
            pe.wait_ge(re_sn.sem, re_sn.next("pe"))
            for n in range(4):
                cols = slice(P * n, P * n + P)
                for p in range(4):
                    ins = pe.matmul(PS[:, 0, P * p:P * p + P], wT[:, p, cols], S[:, p, :], start=True, stop=True)
                ins.then_inc(re_w.sem, 1)
                for p in range(4):
                    ins = pe.matmul(PS[:, 4 + p, cols], S[:, p, :], qkv[:, p, cols], start=True, stop=False, skip_group_check=True)
                pe.wait_ge(re_u.sem, re_u.next("pe"))
                if n < 3:
                    for p in range(4):
                        ins = pe.matmul(PS[:, 3, P * p:P * p + P], ktok[:, n, P * p:P * p + P], uu[:, P * p:P * p + P], start=True, stop=True)
                    ins.then_inc(re_s.sem, 1)
                for h in range(8):
                    ins = pe.matmul(PS[half(h), 4 + h // 2, cols], uu[:, 64 * h:64 * h + 64], pt_of(h).chunk(n), start=False, stop=True,
                                    skip_group_check=True)
                ins.then_inc(re_o.sem, 1)
                if n < 3:
                    pe.wait_ge(re_sn.sem, re_sn.next("pe"))

        def rec_act(act):
            nc.scalar.activation(egx[0:8, :], de[0:8, :], ACT.Exp).then_inc(re_eg0.sem, 1)
            act.wait_ge(re_gt.sem, re_gt.next("act"))
            nc.scalar.activation(gtot, PS[:, 0, 0:16].rearrange("p (q n) -> p q n", q=4), ACT.Exp).then_inc(re_gtx.sem, 1)

        def rec_dve(dve):
            v_link(dve, nc.vector.memset(S, 0.0))
            for p in range(4):
                dve.wait_ge(re_eg.sem, re_eg.next("dve"))
                nc.vector.tensor_tensor(qkv[:, p, :], qkv[:, p, :], PS[:, 1 + p % 2, :], ALU.mult).then_inc(re_qd.sem, 1)
            dve.wait_ge(re_gtx.sem, re_gtx.next("dve"))
            nc.vector.tensor_copy(tS[:, 0, 0:1], S[:, 0, 0:1]).then_inc(re_sn.sem, 1)
            for n in range(4):
                dve.wait_ge(re_w.sem, re_w.next("dve"))
                if n >= 1:
                    dve.wait_ge(re_o.sem, re_o.next("dve"))
                nc.vector.tensor_tensor(uu, ub[:, n, :], PS[:, 0, :], ALU.subtract).then_inc(re_u.sem, 1)
                if n < 3:
                    dve.wait_ge(re_s.sem, re_s.next("dve"))
                    nc.vector.tensor_tensor(S, S, gtot[:, :, n:n + 1].to_broadcast([P, 4, P]), ALU.mult)
                    v_link(dve, nc.vector.tensor_tensor(tS, PS[:, 3, :].rearrange("p (a b) -> p a b", a=4),
                                                        C("blk64").unsqueeze(1).to_broadcast([P, 4, P]), ALU.mult))
                    nc.vector.tensor_tensor(S, S, tS, ALU.add).then_inc(re_sn.sem, 1)
            dve.wait_ge(re_o.sem, re_o.next("dve"))
            for p in range(4):
                nc.vector.tensor_copy(Y[:, 2 + p, :], PS[:, 4 + p, :])

        gdn_norm = [head_norm([(Y[:, 2 + p, :], Y[:, 2 + p, :], "blk64", 1.0 / 64, "eps2", V("gdn_g", l), zp[:, p, :]) for p in range(4)], SC)
                    for l in range(2)]

        def second_loads(l):
            def fn(act):
                if l == 0:
                    act.dma_start(con2[:, 0:N_SECOND], second_d).then_inc(small_loaded.sem, 16)
                act.dma_start(wsT, sguw_d[l]).then_inc(small_loaded.sem, 16)
                act.dma_start(bs_row[0:1, :], sgub_d[l:l + 1]).then_inc(small_loaded.sem, 16)
                act.dma_start(gup[0:16, :], gup_d[l]).then_inc(small_loaded.sem, 16)
            return fn

        stages = []

        def add(pe=None, act=None, dve=None):
            stages.append((pe, act, dve))

        def add_gemm(tiles, before=None):
            def act_fn(e):
                if before:
                    before(e)
                gemm_evac(e, "act", tiles)
            add(lambda e: gemm_pe(e, tiles), act_fn, lambda e: gemm_evac(e, "dve", tiles))

        def add_norm(segs, eps, centred, affine):
            add(lambda e: norm_pe(e, segs, centred), lambda e: norm_act(e, segs, eps, centred, affine), lambda e: norm_dve(e, segs, centred))

        add(ada_pe, ada_act, ada_dve)
        add_norm(ALL, "eps1", False, modulate(0, 0))
        add_gemm(ab_plan())
        add(gates_pe, gates_act, gates_dve)
        add(mlstm_pe, mlstm_act, mlstm_dve)
        add(None, sig_o_act, None)
        add(*mlstm_out)
        add(*qk_norm_b)
        add(rope_b[0], None, rope_b[1])
        add(dup_pe, dup_act, None)
        add(*attn_b)
        add_gemm(out_plan(0, ALL))
        add_norm(ALL, "eps1", False, modulate(0, 1))
        up, down = mlp_plans(0, ALL)
        add_gemm(up)
        add_gemm(down)
        add_norm(ALL, "eps1", False, modulate(1, 0))
        add_gemm(c_plan())
        add(*qk_norm_c)
        add(rope_c[0], None, rope_c[1])
        add(*attn_c)
        add_gemm(out_plan(1, LAT))
        add_norm(LAT, "eps1", False, modulate(1, 1))
        up, down = mlp_plans(1, LAT)
        add_gemm(up)
        add_gemm(down)
        for l in range(2):
            up, down = ffn_plans(l)
            add_gemm(up, before=second_loads(l))
            add_gemm(down)
            add_norm(LAT, "eps2", True, layer_norm_affine("ln1", l))
            add_gemm(in_plan())
            add(sgu_pe, sgu_act, lambda e, l=l: sgu_dve(e, l))
            add(lambda e, l=l: gla_pe(e, l), lambda e, l=l: gla_act(e, l), lambda e, l=l: gla_dve(e, l))
            add(None, silu_r, None)
            add(*gla_norm[l])
            add(None, lambda e, l=l: conv_act(e, l), lambda e, l=l: conv_dve(e, l))
            add(None, silu_z, None)
            add(*l2_qk)
            add(lambda e, l=l: rows_pe(e, l), lambda e, l=l: rows_act(e, l), lambda e, l=l: rows_dve(e, l))
            add(solve_pe, solve_act, solve_dve)
            add(rec_pe, rec_act, rec_dve)
            add(*gdn_norm[l])
            add_gemm(mix_plan())
            add_norm(LAT, "eps2", True, layer_norm_affine("ln2", l))
            up, down = ffn_plans(l)
            add_gemm(up)
            add_gemm(down)
            add_norm(LAT, "eps2", True, layer_norm_affine("ln3", l))

        block = ctx.enter_context(nc.Block())

        @block.tensor
        def _(pe):
            for pe_part, _, _ in stages:
                if pe_part:
                    pe_part(pe)
                end_stage(pe, "pe")

        @block.scalar
        def _(act):
            for _, act_part, _ in stages:
                if act_part:
                    act_part(act)
                end_stage(act, "act")

        @block.vector
        def _(dve):
            for _, _, dve_part in stages:
                if dve_part:
                    dve_part(dve)
                end_stage(dve, "dve")

        @block.sync
        def _(sp):
            sp.dma_start(vec[:], vec_d).then_inc(loaded.sem, 16)
            sp.dma_start(con[:], shared_d).then_inc(loaded.sem, 16)
            sp.dma_start(con2[:, 0:N_FIRST], first_d).then_inc(loaded.sem, 16)
            sp.dma_start(X[:], xT_d.rearrange("(k p) t -> p k t", p=P)).then_inc(loaded.sem, 16)
            for n in range(-(-Weights.at // SLAB)):
                if n >= RING:
                    used, count = Weights.used[n - RING]
                    sp.wait_ge(used.sem, count)
                sp.dma_start(ring[:, n % RING, :, :].rearrange("p a b -> p (a b)"), w_d[n]).then_inc(slab_loaded[n % RING].sem, 16)
            sp.wait_ge(stage.sem, 3 * len(stages))
            sp.dma_start(out_d.rearrange("(k p) t -> p k t", p=P), X[:, :, CTX:TOK]).then_inc(stored.sem, 16)
            sp.wait_ge(stored.sem, 16)


def kernel(**inputs):
    import concourse.bacc as bacc
    from concourse.bass_utils import run_bass_kernel_spmd as run

    a = {k: np.ascontiguousarray(v) for k, v in inputs.items()}

    def columns(v):
        return v.reshape(-1, P).T

    def rows(v, at):
        out = np.zeros((P, v.shape[0]), np.float32)
        out[at, :] = v.T
        return out

    gb = a["ab_gate_b"][0]
    gate_rows = np.r_[0:4, 32:36]
    packed = dict(
        c=columns(a["c"]), c_ctx=columns(a["c_ctx"]), ada_b=columns(a["ada_b"]), norm1_g=columns(a["norm1_g"]),
        norm2_g=columns(a["norm2_g"]), mlstm_g=columns(a["mlstm_norm_g"]), swa_q=columns(np.tile(a["swa_q_norm_g"][0], 2)),
        swa_k=columns(np.tile(a["swa_k_norm_g"][0], 2)), c_q=columns(a["c_q_norm_g"]), c_k=columns(a["c_k_norm_g"]),
        sink=np.broadcast_to(a["swa_sink"], (P, 8)), gb_i=rows(np.r_[gb[0:4], gb[8:12]][None], gate_rows),
        gb_f=rows(np.r_[gb[4:8], gb[12:16]][None], gate_rows), ln1_g=columns(a["ln1_g_2"]), ln1_b=columns(a["ln1_b_2"]),
        ln2_g=columns(a["ln2_g_2"]), ln2_b=columns(a["ln2_b_2"]), ln3_g=columns(a["ln3_g_2"]), ln3_b=columns(a["ln3_b_2"]),
        sgu_g=columns(a["sgu_ln_g_2"]), sgu_b=columns(a["sgu_ln_b_2"]), conv=columns(a["gdn_conv_w_2"]),
        a_log=rows(a["gdn_a_log_2"], np.arange(8)), dt_b=rows(a["gdn_dt_bias_2"], np.arange(8)),
        gdn_g=np.tile(a["gdn_norm_g_2"], (1, 2)).T, gla_gb=columns(a["gla_gate_b_2"]), gla_g=np.tile(a["gla_norm_g_2"], (1, 2)).T,
        eps1=np.full((P, 1), EPS1), eps2=np.full((P, 1), EPS2), epsl=np.full((P, 1), EPSL), one=np.ones((P, 1)))
    vec = np.concatenate([np.asarray(packed[n], np.float32) for n, _ in VECS], 1)
    assert vec.shape == (P, NVEC)

    def spread(w, pieces):
        out = np.zeros((w.shape[0], P), w.dtype)
        for c, n, at in pieces:
            out[:, at:at + n] = w[:, c:c + n]
        return out

    ab = a["ab_w_in"][0]
    mats = dict(ada0=a["ada_w"][0], ada1=a["ada_w"][1], ab=ab, gi=spread(ab, [(2048, 4, 0), (2056, 4, 32)]),
                gf=spread(ab, [(2052, 4, 0), (2060, 4, 32)]), abo=a["ab_w_out"][0], cw=a["c_w_in"][0], co=a["c_w_out"][0])
    for l in range(2):
        w = a["w_in_2"][l]
        mats.update({f"m1_{l}": a["mlp_w1"][l], f"m2_{l}": a["mlp_w2"][l], f"in{l}": w, f"be{l}": spread(w, [(2560, 8, 0)]),
                     f"de{l}": spread(w, [(2568, 8, 0)]), f"gl{l}": spread(w, [(3344, 16, 0)]), f"out{l}": a["w_out_2"][l],
                     f"f1_{l}": a["ffn1_w1_2"][l], f"f3_{l}": a["ffn1_w3_2"][l], f"f2_{l}": a["ffn1_w2_2"][l],
                     f"g1_{l}": a["ffn2_w1_2"][l], f"g3_{l}": a["ffn2_w3_2"][l], f"g2_{l}": a["ffn2_w2_2"][l]})
    w_all = np.zeros((N_SLABS, P, SLAB * P), np.float32)
    for i, (name, k, c, n) in enumerate(stream()):
        w_all[i // SLAB, :, (i % SLAB) * P:(i % SLAB) * P + P] = mats[name][k * P:k * P + P, c:c + P]

    shared, first, second = consts()
    arrays = dict(
        xT=np.concatenate([a["ctx"][0], a["x"][0]], 0).T, vec=vec, shared=shared, first=first, second=second,
        gup=a["gla_gate_up_2"], sguw=a["sgu_w_2"].transpose(0, 3, 1, 2), sgub=a["sgu_b_2"].reshape(2, 512), weights=w_all)
    nc = bacc.Bacc("TRN2", target_bir_lowering=False, num_devices=1)
    ins, args = {}, []
    for name, arr in arrays.items():
        arr = np.ascontiguousarray(arr)
        ins[name + "_dram"] = arr
        args.append(nc.dram_tensor(name + "_dram", arr.shape, F32, kind="ExternalInput").ap())
    out = nc.dram_tensor("out_dram", (D, SEQ), F32, kind="ExternalOutput").ap()
    program(nc, *args, out)
    got = run(nc, [ins], core_ids=[0]).results[0]["out_dram"]
    return np.ascontiguousarray(got.T)[None]
```

```python
from contextlib import ExitStack

import numpy as np

import concourse.bass as bass
from concourse import mybir

F32 = mybir.dt.float32
F32R = mybir.dt.float32r
ALU = mybir.AluOpType
ACT = mybir.ActivationFunctionType
AX = mybir.AxisListType.X

P = 128
D = 1024
KD = D // P
CTX = 256
SEQ = 512
TOK = CTX + SEQ
NT = TOK // P
NCT = CTX // P
NLT = SEQ // P
FF1 = 4 * D
FF2 = 2816
EPS1, EPS2, EPSL = 1e-6, 1e-5, 1e-6
ALPHA = 4.0 ** 0.25
NEG = -1e30
ALL = [(0, 384), (384, 768)]
LAT = [(256, 768)]
SLAB = 8
RING = 4
PARTS = (4, 2, 2)

VECS = [("c", 8), ("c_ctx", 8), ("ada_b", 96), ("norm1_g", 16), ("norm2_g", 16), ("mlstm_g", 4),
        ("swa_q", 1), ("swa_k", 1), ("c_q", 1), ("c_k", 1), ("sink", 8), ("gb_i", 1), ("gb_f", 1),
        ("ln1_g", 16), ("ln1_b", 16), ("ln2_g", 16), ("ln2_b", 16), ("ln3_g", 16), ("ln3_b", 16),
        ("sgu_g", 4), ("sgu_b", 4), ("conv", 96), ("a_log", 2), ("dt_b", 2), ("gdn_g", 2),
        ("gla_gb", 2), ("gla_g", 2), ("eps1", 1), ("eps2", 1), ("epsl", 1), ("one", 1)]
VOFF = {}
_o = 0
for _n, _w in VECS:
    VOFF[_n] = (_o, _w)
    _o += _w
NVEC = _o

SHARED = [("ident", 128), ("ones", 128), ("blk64", 128), ("neg_ge", 128), ("neg_le", 128)]
FIRST = [("rot64", 128), ("rot128", 128), ("dup0", 128), ("dup1", 128), ("self", 512), ("selb", 512),
         ("cos64", 512), ("sin64", 512), ("cos128", 512), ("sin128", 512)]
SECOND = [("pos_lt", 128), ("m_ge", 128), ("sel", 1024), ("selp", 512), ("m_gla", 128), ("bd_gla", 256),
          ("rs128", 512), ("rs64", 512), ("lev", 896), ("levt", 896)]


def offsets(names):
    at, out = 0, {}
    for name, cols in names:
        out[name] = at
        at += cols
    return out, at


SHARED_AT, N_SHARED = offsets(SHARED)
FIRST_AT, N_FIRST = offsets(FIRST)
SECOND_AT, N_SECOND = offsets(SECOND)


def consts():
    r, c = np.arange(P)[:, None], np.arange(P)[None, :]
    a = {}
    a["ident"] = (r == c)
    a["ones"] = np.ones((P, P))
    a["blk64"] = (r // 64 == c // 64)

    def rot(n):
        h = n // 2
        return np.where((c % n < h) & (r == c + h), -1.0, 0.0) + np.where((c % n >= h) & (r == c - h), 1.0, 0.0)

    a["rot64"], a["rot128"] = rot(64), rot(128)
    a["dup0"], a["dup1"] = (r == c % 64), (r == 64 + c % 64)
    a["neg_ge"] = np.where(c >= r, 0.0, NEG)
    a["neg_le"] = np.where(c <= r, 0.0, NEG)
    a["pos_lt"] = np.where(c < r, 0.0, -NEG)
    a["m_ge"] = (c >= r)
    for name, base, heads in (("self", 0, 4), ("selb", 32, 4), ("sel", 0, 8)):
        a[name] = np.concatenate([np.broadcast_to(r == base + h, (P, P)) for h in range(heads)], 1)
    a["selp"] = np.concatenate([(r == 2 * p + c // 64) for p in range(4)], 1)
    a["m_gla"] = (c >= r) & (c // 64 == r // 64)
    a["bd_gla"] = (r // 32 == np.arange(256)[None, :] // 64)
    t = np.arange(512)[None, :]
    a["rs128"] = np.broadcast_to(t % 128 != 0, (P, 512))
    a["rs64"] = np.broadcast_to(t % 64 != 0, (P, 512))
    lev = [((r // (2 * b) == c // (2 * b)) & (r % (2 * b) >= b) & (c % (2 * b) < b)) for b in (1, 2, 4, 8, 16, 32, 64)]
    a["lev"] = np.concatenate(lev, 1)
    a["levt"] = np.concatenate([m.T for m in lev], 1)
    a["cos64"], a["sin64"] = rope_tables(64)
    a["cos128"], a["sin128"] = rope_tables(128)
    return [np.concatenate([np.asarray(a[n], np.float32) for n, _ in group], 1) for group in (SHARED, FIRST, SECOND)]


def rope_tables(head_dim):
    t = np.arange(SEQ)
    row, col = (t // 64).astype(np.float32), (t % 64).astype(np.float32)
    pairs = head_dim // 4
    inv = (np.float32(10000.0) ** (-np.arange(pairs, dtype=np.float32) / np.float32(pairs))).astype(np.float32)
    ang = np.concatenate([inv[:, None] * row[None], inv[:, None] * col[None]], 0)
    reps = P // ang.shape[0]
    return np.tile(np.cos(ang), (reps, 1)).astype(np.float32), np.tile(np.sin(ang), (reps, 1)).astype(np.float32)


def ftiles(w, cols, kt=KD):
    return [(w, k, c, P) for c in range(cols[0], cols[1], P) for k in range(kt)]


def down_tiles(w, rows):
    return [(w, k, c, P) for c in range(0, D, P) for k in range(rows[0], rows[1])]


def mlp_stream(up, down, ff, parts):
    s, n = [], ff // P // parts
    for q in range(parts):
        for m in range(q * n, q * n + n):
            for w in up:
                s += ftiles(w, (m * P, m * P + P))
        s += down_tiles(down, (q * n, q * n + n))
    return s


def ttiles(w, cols, kt=KD):
    return [(w, k, c, P) for k in range(kt) for c in range(cols[0], cols[1], P)]


def stream():
    s = []
    for l in range(2):
        for c in range(0, 6144, 512):
            s += ttiles(f"ada{l}", (c, c + 512))
    s += ftiles("ab", (0, 1024)) + ftiles("ab", (1536, 2048)) + ftiles("ab", (2064, 2576)) + ftiles("ab", (2576, 2704))
    s += ftiles("gi", (0, P)) + ftiles("gf", (0, P))
    s += ttiles("ab", (1024, 1280)) + ttiles("ab", (1280, 1536)) + ttiles("ab", (2704, 2832))
    s += ftiles("abo", (0, D)) + mlp_stream(["m1_0"], "m2_0", FF1, PARTS[0])
    s += ftiles("cw", (0, 1280)) + ttiles("cw", (1280, 1536)) + ftiles("co", (0, D))
    s += mlp_stream(["m1_1"], "m2_1", FF1, PARTS[1])
    for l in range(2):
        for f in ("f", None, "g"):
            if f is None:
                w = f"in{l}"
                s += ftiles(w, (0, 512)) + ftiles(w, (512, 2048)) + ftiles(w, (2048, 2560))
                s += ftiles(f"be{l}", (0, P)) + ftiles(f"de{l}", (0, P))
                s += ftiles(w, (2576, 2832)) + ftiles(w, (3088, 3344)) + ftiles(f"gl{l}", (0, P))
                s += ttiles(w, (2832, 3088)) + ftiles(f"out{l}", (0, D))
            else:
                s += mlp_stream([f"{f}1_{l}", f"{f}3_{l}"], f"{f}2_{l}", FF2, PARTS[2])
    return s


N_SLABS = -(-len(stream()) // SLAB)
RAW_SLABS = 2 * 6144 * D // (P * P) // SLAB


class Signal:

    def __init__(self, sem):
        self.sem = sem
        self.seen = {}

    def at(self, who, k):
        return self.seen.get(who, 0) + k + 1

    def advance(self, who, n):
        self.seen[who] = self.seen.get(who, 0) + n

    def next(self, who, step=1):
        self.seen[who] = self.seen.get(who, 0) + step
        return self.seen[who]


class Out:

    def __init__(self, bank, ready, who, freed, reuse):
        self.bank, self.ready, self.who, self.freed, self.reuse = bank, ready, who, freed, reuse


class Banks:

    def __init__(self):
        self.n, self.done, self.user = 0, {"act": 0, "dve": 0}, [None] * 8

    def take(self, who):
        bank = self.n % 8
        self.n += 1
        self.done[who] += 1
        out = Out(bank, self.n, who, self.done[who], self.user[bank])
        self.user[bank] = (who, self.done[who])
        return out


def program(nc, xT_d, vec_d, shared_d, first_d, second_d, gup_d, sguw_d, sgub_d, w_d, out_d):
    with ExitStack() as ctx:
        def sb(name, cols):
            return ctx.enter_context(nc.sbuf_tensor(name, [P, cols], F32))

        def signal(name):
            return Signal(ctx.enter_context(nc.semaphore(name)))

        def with_rounded(name, shape):
            at = -(-nc.sbuf_base // 32) * 32
            return (ctx.enter_context(nc.sbuf_tensor(name, shape, F32)),
                    nc.alloc_sbuf_tensor_at(name + "_r", shape, F32R, offset=at))

        X = ctx.enter_context(nc.sbuf_tensor("X", [P, KD, TOK], F32))
        H, H_r = with_rounded("H", [P, KD, TOK])
        ring, ring_lo = with_rounded("ring", [P, RING, SLAB, P])
        ring_hi = ctx.enter_context(nc.sbuf_tensor("ring_hi", [P, RING, SLAB, P], F32R))
        ARENA = 24576
        arena, arena_r = with_rounded("arena", [P, ARENA])
        vec = sb("vec", NVEC)
        con = sb("con", N_SHARED)
        con2 = sb("con2", max(N_FIRST, N_SECOND))
        mods = ctx.enter_context(nc.sbuf_tensor("mods", [P, 2, 2, 48], F32))
        amul = ctx.enter_context(nc.sbuf_tensor("amul", [P, 2, 2, 2, 8], F32))
        cs = ctx.enter_context(nc.sbuf_tensor("cs", [P, 8, 2], F32))
        small = sb("small", 160)
        PS = ctx.enter_context(nc.psum_tensor("PS", [P, 8, 512], F32))

        def V(name, i=0, n=1):
            return vec[:, VOFF[name][0] + i:VOFF[name][0] + i + n]

        def C(name, i=0, n=P):
            if name in SHARED_AT:
                return con[:, SHARED_AT[name] + i:SHARED_AT[name] + i + n]
            at = FIRST_AT[name] if name in FIRST_AT else SECOND_AT[name]
            return con2[:, at + i:at + i + n]

        def area(at, *dims, of=arena):
            n = int(np.prod(dims))
            assert at + n <= ARENA, (at, n)
            a = of[:, at:at + n]
            if len(dims) == 2:
                return a.rearrange("p (a b) -> p a b", a=dims[0])
            if len(dims) == 3:
                return a.rearrange("p (a b c) -> p a b c", a=dims[0], b=dims[1])
            return a

        loaded = signal("inputs_loaded")
        rope_loaded = signal("rope_loaded")
        small_loaded = signal("sgu_loaded")
        slab_loaded = [signal(f"slab_loaded{i}") for i in range(RING)]
        slab_used = signal("slab_used")
        hi_ready = signal("slab_high_parts_ready")
        lo_ready = signal("slab_low_parts_ready")
        mm_done = signal("product_ready")
        evac = {"act": signal("evacuated_by_act"), "dve": signal("evacuated_by_dve")}
        stage = signal("stage_done")
        stored = signal("stored")
        act_step = signal("act_step")
        dve_step = signal("dve_step")
        silu_c = signal("silu_c_ready")
        ada_done = signal("ada_products_ready")
        sq_ready = signal("squares_ready")
        sum_ready = signal("sums_ready")
        mean_sums = signal("mean_sums_ready")
        std_ready = signal("std_ready")
        norm_ready = signal("normed_ready")
        mean_used = signal("mean_used")
        affine_done = signal("norm_scaled")
        xhi_ready = signal("input_high_parts_ready")
        xlo_ready = signal("input_low_parts_ready")

        def a_link(act, ins):
            ins.then_inc(act_step.sem, 1)
            act.wait_ge(act_step.sem, act_step.next("act"))

        def v_link(dve, ins):
            ins.then_inc(dve_step.sem, 1)
            dve.wait_ge(dve_step.sem, dve_step.next("dve"))

        def end_stage(eng, who):
            eng.drain().then_inc(stage.sem, 1)
            eng.wait_ge(stage.sem, stage.next(who, 3))

        class Weights:
            at = 0
            used = []

        def used_up(ins):
            ins.then_inc(slab_used.sem, 1)
            Weights.used.append((slab_used, slab_used.next("pe")))

        def high_part(out, src):
            return nc.vector.tensor_copy(out, src)

        def raw_tiles(pe, n):
            slab, pos = divmod(Weights.at, SLAB)
            assert pos + n <= SLAB
            if pos == 0:
                pe.wait_ge(slab_loaded[slab % RING].sem, 16 * (slab // RING + 1))
            Weights.at += n
            return ring[:, slab % RING, pos:pos + n, :], Weights.at % SLAB == 0

        def split_tiles(pe, n):
            slab, pos = divmod(Weights.at, SLAB)
            assert pos + n <= SLAB
            if pos == 0:
                pe.wait_ge(lo_ready.sem, slab - RAW_SLABS + 1)
            Weights.at += n
            return ring_hi[:, slab % RING, pos:pos + n, :], ring_lo[:, slab % RING, pos:pos + n, :], Weights.at % SLAB == 0

        class Splits:
            at = RAW_SLABS
            order = []
            inputs = 0

        def split_up_to(dve, slab):
            while Splits.at < min(slab, N_SLABS):
                n = Splits.at
                dve.wait_ge(slab_loaded[n % RING].sem, 16 * (n // RING + 1))
                high_part(ring_hi[:, n % RING, :, :], ring[:, n % RING, :, :]).then_inc(hi_ready.sem, 1)
                Splits.order.append(("slab", n))
                Splits.at += 1

        def gemm_pe(pe, tiles, fresh=0):
            for i, t in enumerate(tiles):
                if i:
                    fresh = 0
                for o in t["outs"]:
                    if o.reuse:
                        pe.wait_ge(evac[o.reuse[0]].sem, o.reuse[1])
                kt = t["kt"]
                for k in range(kt):
                    if fresh:
                        pe.wait_ge(xlo_ready.sem, fresh - KD + k + 1)
                    w_hi, w_lo, last_of_slab = split_tiles(pe, t["n"])
                    for o, (lo, hi) in zip(t["outs"], t["segs"]):
                        x_hi, x_lo = t["rhs"](k, lo, hi)
                        for j, (w, x) in enumerate(((w_hi, x_hi), (w_hi, x_lo), (w_lo, x_hi))):
                            flags = dict(start=(k == 0 and j == 0), stop=(k == kt - 1 and j == 2))
                            if t["mode"] == "F":
                                ins = pe.matmul(PS[:, o.bank, 0:hi - lo], w[:, 0, :], x, **flags)
                            else:
                                ins = pe.matmul(PS[:, o.bank, 0:t["n"] * P], x, w.rearrange("p a b -> p (a b)"), **flags)
                        if k == kt - 1:
                            ins.then_inc(mm_done.sem, 1)
                    if last_of_slab:
                        if k == kt - 1:
                            Weights.used.append((mm_done, t["outs"][-1].ready))
                        else:
                            used_up(ins)

        def gemm_evac(eng, who, tiles):
            for i, t in enumerate(tiles + [dict(late=None), dict(late=None)]):
                if who == "act" and i >= 2 and tiles[i - 2]["late"]:
                    tiles[i - 2]["late"](eng)
                if i >= len(tiles):
                    continue
                if who == "dve":
                    split_up_to(eng, t["last_slab"] + 3)
                for o, (lo, hi) in zip(t["outs"], t["segs"]):
                    if o.who == who:
                        eng.wait_ge(mm_done.sem, o.ready)
                        width = hi - lo if t["mode"] == "F" else t["n"] * P
                        t["ev"](eng, PS[:, o.bank, 0:width], lo, hi).then_inc(evac[who].sem, 1)
                    if who == "dve" and t["post"]:
                        t["post"](eng, o, lo, hi)

        banks = Banks()

        class Planned:
            at = RAW_SLABS * SLAB

        def planned(n):
            Planned.at += n
            return (Planned.at - 1) // SLAB

        def ftile(rhs, segs, who, ev, kt=KD, post=None, late=None):
            return dict(mode="F", n=1, kt=kt, segs=segs, rhs=rhs, ev=ev, post=post, late=late, outs=[banks.take(who) for _ in segs],
                        last_slab=planned(kt))

        def ttile(rhs, toks, n, who, ev):
            return dict(mode="T", n=n, kt=KD, segs=[(P * t, P * t + P) for t in toks], rhs=rhs, ev=ev, post=None, late=None,
                        outs=[banks.take(who) for _ in toks], last_slab=planned(KD * n))

        XHI = area(18432, KD, TOK, of=arena_r)
        XHI2 = area(20480, KD, SEQ, of=arena_r)

        def x_h(k, lo, hi):
            return XHI[:, k, lo:hi], H_r[:, k, lo:hi]

        def x_x(k, lo, hi):
            return XHI2[:, k, lo - CTX:hi - CTX], H_r[:, k, lo:hi]

        def xhi(second, k, lo, hi):
            return XHI2[:, k, lo - CTX:hi - CTX] if second else XHI[:, k, lo:hi]

        split_inputs = []

        def split_tiles_of(src, second, segs):
            for lo, hi in segs:
                for k in range(KD):
                    split_inputs.append((src[:, k, lo:hi], xhi(second, k, lo, hi), H_r[:, k, lo:hi]))

        def split_dve(src, second, segs):
            def fn(dve):
                for lo, hi in segs:
                    for k in range(KD):
                        high_part(xhi(second, k, lo, hi), src[:, k, lo:hi]).then_inc(xhi_ready.sem, 1)
                        Splits.order.append(("input", Splits.inputs))
                        Splits.inputs += 1
            return fn

        def copy_act(dst, scale=1.0):
            def ev(eng, ps, lo, hi):
                return nc.scalar.activation(dst(lo, hi), ps, ACT.Copy, scale=scale)
            return ev

        def func_act(dst, func):
            def ev(eng, ps, lo, hi):
                return nc.scalar.activation(dst(lo, hi), ps, func)
            return ev

        def copy_dve(dst):
            def ev(eng, ps, lo, hi):
                return nc.vector.tensor_copy(dst(lo, hi), ps)
            return ev

        def streams(lo, hi):
            return [(s, max(lo, a), min(hi, b)) for s, a, b in ((1, 0, CTX), (0, CTX, TOK)) if max(lo, a) < min(hi, b)]

        rstd = sb("rstd", 512)
        mean = sb("mean", 512)

        def norm_act(act, segs, eps, centred, affine):
            for lo, hi in segs:
                if centred:
                    act.wait_ge(mean_used.sem, mean_used.next("act"))
                for k in range(KD):
                    src = H if centred else X
                    dst = tmp_sq
                    ins = nc.scalar.activation(dst[:, k, lo:hi], src[:, k, lo:hi], ACT.Square)
                ins.then_inc(sq_ready.sem, 1)
                act.wait_ge(sum_ready.sem, sum_ready.next("act"))
                a_link(act, nc.scalar.activation(rstd[:, 0:hi - lo], PS[:, 0, 0:hi - lo], ACT.Ln, bias=V(eps), scale=1.0 / D))
                nc.scalar.activation(rstd[:, 0:hi - lo], rstd[:, 0:hi - lo], ACT.Exp, scale=-0.5).then_inc(std_ready.sem, 1)
                for k in range(KD):
                    act.wait_ge(norm_ready.sem, norm_ready.next("act"))
                    affine(act, k, lo, hi).then_inc(affine_done.sem, 1)

        def norm_pe(pe, segs, centred):
            for lo, hi in segs:
                if centred:
                    for k in range(KD):
                        ins = pe.matmul(PS[:, 1, 0:hi - lo], C("ones"), X[:, k, lo:hi], start=(k == 0), stop=(k == KD - 1))
                    ins.then_inc(mean_sums.sem, 1)
                pe.wait_ge(sq_ready.sem, sq_ready.next("pe"))
                for k in range(KD):
                    ins = pe.matmul(PS[:, 0, 0:hi - lo], C("ones"), tmp_sq[:, k, lo:hi], start=(k == 0), stop=(k == KD - 1))
                ins.then_inc(sum_ready.sem, 1)

        def norm_dve(dve, segs, centred):
            for lo, hi in segs:
                src = X
                if centred:
                    dve.wait_ge(mean_sums.sem, mean_sums.next("dve"))
                    v_link(dve, nc.vector.tensor_scalar(mean[:, 0:hi - lo], PS[:, 1, 0:hi - lo], 1.0 / D, None, ALU.mult))
                    for k in range(KD):
                        ins = nc.vector.tensor_tensor(H[:, k, lo:hi], X[:, k, lo:hi], mean[:, 0:hi - lo], ALU.subtract)
                    ins.then_inc(mean_used.sem, 1)
                    src = H
                dve.wait_ge(std_ready.sem, std_ready.next("dve"))
                for k in range(KD):
                    nc.vector.tensor_tensor(H[:, k, lo:hi], src[:, k, lo:hi], rstd[:, 0:hi - lo],
                                            ALU.mult).then_inc(norm_ready.sem, 1)
                for k in range(KD):
                    dve.wait_ge(affine_done.sem, affine_done.next("dve"))
                    high_part(xhi(centred, k, lo, hi), (X if centred else H)[:, k, lo:hi]).then_inc(xhi_ready.sem, 1)
                    Splits.order.append(("input", Splits.inputs))
                    Splits.inputs += 1

        tmp_sq = area(0, KD, TOK)

        def modulate(l, n):
            def affine(act, k, lo, hi):
                for s, a, b in streams(lo, hi):
                    ins = nc.scalar.activation(H[:, k, a:b], H[:, k, a:b], ACT.Identity,
                                               bias=mods[:, l, s, 24 * n + k:24 * n + k + 1], scale=amul[:, l, s, n, k:k + 1])
                return ins
            return affine

        def layer_norm_affine(name, l):
            def affine(act, k, lo, hi):
                return nc.scalar.activation(X[:, k, lo:hi], H[:, k, lo:hi], ACT.Identity, bias=V(name + "_b", 8 * l + k),
                                            scale=V(name + "_g", 8 * l + k))
            return affine

        ada_out, ada_row = signal("ada_rows_ready"), signal("ada_rows_copied")
        ada_rows = area(0, 2, 6144)

        def ada_act(act):
            act.wait_ge(loaded.sem, 64)
            nc.scalar.activation(cs[:, :, 0], V("c", 0, 8), ACT.Silu)
            nc.scalar.activation(cs[:, :, 1], V("c_ctx", 0, 8), ACT.Silu).then_inc(silu_c.sem, 1)
            for i in range(24):
                act.wait_ge(ada_out.sem, i + 1)
                nc.scalar.activation(ada_rows[0:2, i // 12, 512 * (i % 12):512 * (i % 12) + 512], PS[0:2, 2 + i % 6, :],
                                     ACT.Copy).then_inc(ada_row.sem, 1)

        def ada_pe(pe):
            pe.wait_ge(loaded.sem, 64)
            pe.wait_ge(silu_c.sem, 1)
            for i in range(24):
                if i >= 6:
                    pe.wait_ge(ada_row.sem, i - 5)
                for k in range(KD):
                    w, last_of_slab = raw_tiles(pe, 4)
                    ins = pe.matmul(PS[0:2, 2 + i % 6, :], cs[:, k, :], w.rearrange("p a b -> p (a b)"), start=(k == 0), stop=(k == KD - 1))
                    if last_of_slab:
                        if k == KD - 1:
                            ins.then_inc(ada_out.sem, 1)
                            Weights.used.append((ada_out, i + 1))
                        else:
                            used_up(ins)
            for l in range(2):
                pe.wait_ge(ada_row.sem, 12 * l + 12)
                for m in range(48):
                    ins = pe.transpose(PS[:, l, 2 * m:2 * m + 2], ada_rows[0:2, l, P * m:P * m + P], C("ident")[0:2, 0:2])
            ins.then_inc(ada_done.sem, 1)

        def ada_dve(dve):
            dve.wait_ge(loaded.sem, 64)
            dve.wait_ge(ada_done.sem, 1)
            for l in range(2):
                for s in range(2):
                    v_link(dve, nc.vector.tensor_tensor(mods[:, l, s, :], PS[:, l, 0:96].rearrange("p (m s) -> p m s", s=2)[:, :, s],
                                                        V("ada_b", 48 * l, 48), ALU.add))
                    for n in range(2):
                        g = V("norm1_g" if n == 0 else "norm2_g", 8 * l, 8)
                        nc.vector.scalar_tensor_tensor(out=amul[:, l, s, n, :], in0=mods[:, l, s, 24 * n + 8:24 * n + 16],
                                                       scalar=1.0, in1=g, op0=ALU.add, op1=ALU.mult)

        hn_sq, hn_sum = signal("head_squares_ready"), signal("head_sums_ready")
        hn_std, hn_done = signal("head_std_ready"), signal("head_normed")
        HR = 4

        def head_norm(items, at):
            sq = [area(at + 512 * i, 512) for i in range(HR)]
            rs = [area(at + 512 * (HR + i), 512) for i in range(HR)]

            def width(it):
                return it[0].shape[-1]

            def act_fn(act):
                for i in range(len(items) + 1):
                    if i < len(items):
                        nc.scalar.activation(sq[i % HR][:, 0:width(items[i])], items[i][0], ACT.Square).then_inc(hn_sq.sem, 1)
                    if i >= 1:
                        j, it = i - 1, items[i - 1]
                        act.wait_ge(hn_sum.sem, hn_sum.at("act", j))
                        if j >= HR:
                            act.wait_ge(hn_done.sem, hn_done.at("act", j - HR))
                        a_link(act, nc.scalar.activation(rs[j % HR][:, 0:width(it)], PS[:, j % 8, 0:width(it)], ACT.Ln,
                                                         bias=V(it[4]), scale=it[3]))
                        nc.scalar.activation(rs[j % HR][:, 0:width(it)], rs[j % HR][:, 0:width(it)], ACT.Exp,
                                             scale=-0.5).then_inc(hn_std.sem, 1)
                hn_sum.advance("act", len(items))
                hn_done.advance("act", len(items))

            def pe_fn(pe):
                for i, it in enumerate(items):
                    pe.wait_ge(hn_sq.sem, hn_sq.at("pe", i))
                    if i >= 8:
                        pe.wait_ge(hn_std.sem, hn_std.at("pe", i - 8))
                    pe.matmul(PS[:, i % 8, 0:width(it)], C(it[2]), sq[i % HR][:, 0:width(it)], start=True, stop=True).then_inc(hn_sum.sem, 1)
                hn_sq.advance("pe", len(items))
                hn_std.advance("pe", len(items))

            def dve_fn(dve):
                for i, (src, dst, _, _, _, gain, extra) in enumerate(items):
                    r = rs[i % HR][:, 0:src.shape[-1]]
                    dve.wait_ge(hn_std.sem, hn_std.at("dve", i))
                    ins = nc.vector.scalar_tensor_tensor(out=dst, in0=src, scalar=gain, in1=r, op0=ALU.mult, op1=ALU.mult)
                    if extra is not None:
                        v_link(dve, ins)
                        ins = nc.vector.tensor_tensor(dst, dst, extra, ALU.mult)
                    ins.then_inc(hn_done.sem, 1)
                hn_std.advance("dve", len(items))

            return pe_fn, act_fn, dve_fn

        rope_rot, rope_used = signal("rotated_ready"), signal("rotated_used")

        def rope(tiles, d, at):
            def pe_fn(pe):
                for i, t in enumerate(tiles):
                    if i >= 4:
                        pe.wait_ge(rope_used.sem, rope_used.at("pe", i - 4))
                    pe.matmul(PS[:, i % 4, :], C(f"rot{d}"), t, start=True, stop=True).then_inc(rope_rot.sem, 1)
                rope_used.advance("pe", len(tiles))

            def dve_fn(dve):
                for i, t in enumerate(tiles):
                    tmp = area(at + 512 * (i % 2), 512)
                    dve.wait_ge(rope_rot.sem, rope_rot.at("dve", i))
                    nc.vector.tensor_tensor(tmp, PS[:, i % 4, :], C(f"sin{d}", 0, 512), ALU.mult)
                    v_link(dve, nc.vector.tensor_tensor(t, t, C(f"cos{d}", 0, 512), ALU.mult))
                    nc.vector.tensor_tensor(t, t, tmp, ALU.add).then_inc(rope_used.sem, 1)
                rope_rot.advance("dve", len(tiles))

            return pe_fn, dve_fn

        at_s, at_nb, at_p = signal("scores_ready"), signal("minus_max_ready"), signal("exp_ready")
        at_n, at_t, at_tc = signal("probs_normed"), signal("probs_turned"), signal("turned_probs_copied")
        at_o, at_oc = signal("head_outputs_ready"), signal("head_outputs_copied")

        def attention(groups, scale, p_at, pt_at):
            units = [(g, j) for g in groups for j in range(4)]
            probs = [area(p_at + 768 * i, 768) for i in range(3)]
            turned = [area(pt_at + 3072 * i, 6, 512) for i in range(2)]
            n = len(units)

            def nk(g):
                return CTX + (g["lat"][1] - g["lat"][0] if g["lat"] else 0)

            def s_all(i, g):
                return PS[:, 2 * (i % 2):2 * (i % 2) + 2, :].rearrange("p a b -> p (a b)")[:, 256:256 + nk(g)]

            def key_tiles(g):
                return list(range(NCT)) + (list(range(g["lat"][0] // P, g["lat"][1] // P)) if g["lat"] else [])

            def col(i, what):
                return small[:, 8 * what + i % 8:8 * what + i % 8 + 1]

            def pe_fn(pe):
                for i in range(n + 2):
                    if i < n:
                        g, j = units[i]
                        if i >= 2:
                            pe.wait_ge(at_p.sem, at_p.at("pe", i - 2))
                        ins = pe.matmul(PS[:, 2 * (i % 2), 256:512], g["q"][j], g["k"][j][:, 0:CTX], start=True, stop=True)
                        if g["lat"]:
                            lo, hi = g["lat"]
                            ins = pe.matmul(PS[:, 2 * (i % 2) + 1, 0:hi - lo], g["q"][j], g["k"][j][:, lo:hi], start=True, stop=True)
                        ins.then_inc(at_s.sem, 1)
                    if i >= 2:
                        u = i - 2
                        g, j = units[u]
                        kts = key_tiles(g)
                        pe.wait_ge(at_n.sem, at_n.at("pe", u))
                        if u >= 1:
                            pe.wait_ge(at_tc.sem, at_tc.at("pe", u - 1))
                        for t in range(len(kts)):
                            ins = pe.transpose(PS[:, 4 + t // 4, (t % 4) * P:(t % 4) * P + P], probs[u % 3][:, t * P:t * P + P], C("ident"))
                        ins.then_inc(at_t.sem, 1)
                        if j == 3:
                            gi = u // 4
                            pe.wait_ge(at_tc.sem, at_tc.at("pe", u))
                            if gi >= 2:
                                pe.wait_ge(at_oc.sem, at_oc.at("pe", gi - 2))
                            for t, kt in enumerate(kts):
                                ins = pe.matmul(PS[0:g["m"], 6 + gi % 2, :], g["v"](kt), turned[gi % 2][:, t, :],
                                                start=(t == 0), stop=(t == len(kts) - 1))
                            ins.then_inc(at_o.sem, 1)
                for s_, c_ in ((at_p, n), (at_n, n), (at_tc, n), (at_oc, len(groups))):
                    s_.advance("pe", c_)

            def dve_fn(dve):
                for i in range(n + 1):
                    if i < n:
                        g, j = units[i]
                        dve.wait_ge(at_s.sem, at_s.at("dve", i))
                        for c_, mask in g["masks"]:
                            s_c = s_all(i, g)[:, c_:c_ + P]
                            ins = nc.vector.tensor_tensor(s_c, s_c, C(mask), ALU.add)
                        if g["masks"]:
                            v_link(dve, ins)
                        v_link(dve, nc.vector.tensor_reduce(col(i, 0), s_all(i, g), AX, ALU.max))
                        if g["sinks"]:
                            v_link(dve, nc.vector.tensor_scalar(col(i, 1), col(i, 0), scale, g["sinks"][j], ALU.mult, ALU.max))
                            ins = nc.vector.tensor_scalar(col(i, 2), col(i, 1), -1.0, None, ALU.mult)
                        else:
                            ins = nc.vector.tensor_scalar(col(i, 2), col(i, 0), -scale, None, ALU.mult)
                        ins.then_inc(at_nb.sem, 1)
                    if i >= 1:
                        u = i - 1
                        g, j = units[u]
                        dve.wait_ge(at_p.sem, at_p.at("dve", u))
                        if g["sinks"]:
                            v_link(dve, nc.vector.tensor_tensor(col(u, 3), col(u, 3), col(u, 4), ALU.add))
                        v_link(dve, nc.vector.reciprocal(col(u, 5), col(u, 3)))
                        nc.vector.tensor_scalar(probs[u % 3][:, 0:nk(g)], probs[u % 3][:, 0:nk(g)], col(u, 5), None,
                                                ALU.mult).then_inc(at_n.sem, 1)
                at_s.advance("dve", n)
                at_p.advance("dve", n)

            def act_fn(act):
                for i in range(n + 2):
                    if i < n:
                        g, j = units[i]
                        act.wait_ge(at_nb.sem, at_nb.at("act", i))
                        if i >= 3:
                            act.wait_ge(at_t.sem, at_t.at("act", i - 3))
                        if g["sinks"]:
                            nc.scalar.activation(col(i, 4), g["sinks"][j], ACT.Exp, bias=col(i, 2))
                        nc.scalar.activation(probs[i % 3][:, 0:nk(g)], s_all(i, g), ACT.Exp, bias=col(i, 2), scale=scale,
                                             accum_out=col(i, 3)).then_inc(at_p.sem, 1)
                    if i >= 2:
                        u = i - 2
                        g, j = units[u]
                        gi = u // 4
                        act.wait_ge(at_t.sem, at_t.at("act", u))
                        if j == 0 and gi >= 2:
                            act.wait_ge(at_o.sem, at_o.at("act", gi - 2))
                        kt = len(key_tiles(g))
                        src = PS[:, 4:6, :].rearrange("p a b -> p (a b)")[:, 0:kt * P].rearrange("p (a b) -> p a b", a=kt)
                        nc.scalar.activation(turned[gi % 2][:, 0:kt, j * P:j * P + P], src, ACT.Copy).then_inc(at_tc.sem, 1)
                        if j == 3:
                            act.wait_ge(at_o.sem, at_o.at("act", gi))
                            g["put"](PS[0:g["m"], 6 + gi % 2, :].rearrange("p (h q) -> p h q", h=4)).then_inc(at_oc.sem, 1)
                at_nb.advance("act", n)
                at_t.advance("act", n)
                at_o.advance("act", len(groups))

            return pe_fn, act_fn, dve_fn

        qa, ka, oa, qb = (area(3072 * i, 4, TOK) for i in range(4))
        kb, gi, gf = area(12288, TOK), area(13056, TOK), area(13824, TOK)
        va = area(14592, 6, 512)
        vb = area(17664, 6, P)

        def to(dst):
            return lambda lo, hi: dst[:, lo:hi]

        def ab_plan():
            t = [ftile(x_h, ALL, "act", copy_act(to(qa[:, m, :]))) for m in range(4)]
            t += [ftile(x_h, ALL, "act", copy_act(to(ka[:, m, :]), P ** -0.5)) for m in range(4)]
            t += [ftile(x_h, ALL, "act", func_act(to(oa[:, m, :]), ACT.Sigmoid)) for m in range(4)]
            t += [ftile(x_h, ALL, "dve", copy_dve(to(qb[:, m, :]))) for m in range(4)]
            t += [ftile(x_h, ALL, "dve", copy_dve(to(d))) for d in (kb, gi, gf)]
            for half in range(2):
                t.append(ttile(x_h, range(NT), 2, "act",
                               copy_act(lambda lo, hi, half=half: va[:, lo // P, 256 * half:256 * half + 256])))
            t.append(ttile(x_h, range(NT), 1, "dve", copy_dve(lambda lo, hi: vb[:, lo // P, :])))
            return t

        def residual(l, gate, m):
            def ev(eng, ps, lo, hi):
                for s, a, b in streams(lo, hi):
                    ins = nc.vector.scalar_tensor_tensor(out=X[:, m, a:b], in0=ps[:, a - lo:b - lo],
                                                         scalar=mods[:, l, s, gate + m:gate + m + 1],
                                                         in1=X[:, m, a:b], op0=ALU.mult, op1=ALU.add)
                return ins
            return ev

        def out_plan(l, segs):
            return [ftile(x_h, segs, "dve", residual(l, 16, m)) for m in range(KD)]

        def split_hidden(h_hi, h, h_lo):
            def post(dve, o, lo, hi):
                dve.wait_ge(evac[o.who].sem, o.freed)
                v_link(dve, high_part(h_hi(lo, hi), h(lo, hi)))
                nc.vector.tensor_tensor(h_lo(lo, hi), h(lo, hi), h_hi(lo, hi).bitcast(F32), ALU.subtract)
            return post

        def mlp_plans(l, segs):
            n = FF1 // P // PARTS[l]
            w = segs[-1][1] - segs[0][0]
            off = segs[0][0]
            h_hi, h, h_lo = area(0, n, w, of=arena_r), area(n * w, n, w), area(n * w, n, w, of=arena_r)

            def relu_sq(m):
                def ev(eng, ps, lo, hi):
                    d = h[:, m, lo - off:hi - off]
                    a_link(eng, nc.scalar.activation(d, ps, ACT.Relu))
                    return nc.scalar.activation(d, d, ACT.Square)
                return ev

            out = []
            for q in range(PARTS[l]):
                out.append([ftile(x_h, segs, "act", relu_sq(m), post=split_hidden(*(
                    lambda lo, hi, m=m, part=part: part[:, m, lo - off:hi - off] for part in (h_hi, h, h_lo)))) for m in range(n)])
                out.append([ftile(lambda k, lo, hi: (h_hi[:, k, lo - off:hi - off], h_lo[:, k, lo - off:hi - off]), segs, "dve",
                                  residual(l, 40, m), kt=n) for m in range(KD)])
            return out

        F_, g_ = gf[0:64, :], gi[0:64, :]
        G_, EM, T1, T2 = (H[0:64, 4 + i, :] for i in range(4))
        gt = small[:, 0:48].rearrange("p (t d h) -> p t d h", t=6, d=2)
        gt_ready, gate_rows, gate_act, gate_abs = (signal(n) for n in ("gates_turned", "gate_rows_ready", "gate_logs_ready", "gate_args_ready"))

        def gates_act(act):
            a_link(act, nc.scalar.activation(F_, F_, ACT.Identity, bias=V("gb_f")[0:64]))
            nc.scalar.activation(g_, g_, ACT.Identity, bias=V("gb_i")[0:64])
            a_link(act, nc.scalar.activation(T1, F_, ACT.Abs))
            a_link(act, nc.scalar.activation(T1, T1, ACT.Exp, scale=-1.0))
            nc.scalar.activation(T1, T1, ACT.Ln, bias=V("one")[0:64]).then_inc(gate_act.sem, 1)
            act.wait_ge(gate_abs.sem, 1)
            nc.scalar.activation(EM, EM, ACT.Exp, scale=-1.0).then_inc(gate_act.sem, 1)
            act.wait_ge(gt_ready.sem, 1)
            nc.scalar.activation(gt, PS[:, 0, 0:384].rearrange("p (t d h) -> p t d h", t=6, d=2)[:, :, :, 0:4], ACT.Copy)

        def gates_dve(dve):
            v_link(dve, nc.vector.memset(T2, 0.0))
            dve.wait_ge(gate_act.sem, 1)
            v_link(dve, nc.vector.scalar_tensor_tensor(out=T1, in0=F_, scalar=0.0, in1=T1, op0=ALU.min, op1=ALU.subtract))

            def scan(dst, src, other, op, start):
                v_link(dve, nc.vector.tensor_tensor_scan(dst[0:32, :], src[0:32, :], other[0:32, :], start, op, op))
                v_link(dve, nc.vector.tensor_tensor_scan(dst[32:64, 0:CTX][:, ::-1], src[32:64, 0:CTX][:, ::-1],
                                                         other[32:64, 0:CTX][:, ::-1], start, op, op))
                v_link(dve, nc.vector.tensor_tensor_scan(dst[32:64, CTX:TOK][:, ::-1], src[32:64, CTX:TOK][:, ::-1],
                                                         other[32:64, CTX:TOK][:, ::-1], dst[32:64, 0:1], op, op))

            scan(F_, T1, T2, ALU.add, 0.0)
            nc.vector.tensor_tensor(g_, g_, F_, ALU.subtract).then_inc(gate_rows.sem, 1)
            dve.wait_ge(gate_rows.sem, 1)
            scan(G_, g_, g_, ALU.max, 0.0)
            nc.vector.tensor_tensor(EM, F_, G_, ALU.add).then_inc(gate_abs.sem, 1)

        def gates_pe(pe):
            pe.wait_ge(gate_rows.sem, 1)
            for t in range(NT):
                ins = pe.transpose(PS[:, 0, 64 * t:64 * t + 64], gi[0:64, P * t:P * t + P], C("ident")[0:64, 0:64])
            ins.then_inc(gt_ready.sem, 1)

        W_ = area(18432, 2, 6, 512)
        PASSES = [(h, seg) for h in range(4) for seg in ((0, CTX), (CTX, TOK))]

        def reach(d, s, lo, hi):
            if s * P < lo:
                return 0, hi - lo, None
            q = s * P - lo
            return (q, hi - lo, q) if d == 0 else (0, q + P, q)

        ml_g, ml_diag, ml_e = signal("row_max_spread"), signal("diagonal_args_ready"), signal("decays_ready")
        ml_s, ml_w = signal("mlstm_scores_ready"), signal("weighted_scores_ready")
        ml_em, ml_nd, ml_abs, ml_h = (signal(n) for n in ("exp_minus_m_spread", "num_den_ready", "abs_den_ready", "mlstm_head_done"))
        DG = [H[:, 6, 0:768], H[:, 7, 0:512]]

        def diag_buf(d, s):
            return H[:, 6 + d, P * s:P * s + P]

        def mlstm_pe(pe):
            for i, (h, (lo, hi)) in enumerate(PASSES):
                w = hi - lo
                if i >= 1:
                    pe.wait_ge(ml_h.sem, i)
                for d, sel in enumerate(("self", "selb")):
                    ins = pe.matmul(PS[:, d, 0:w], C(sel, P * h)[0:64], G_[:, lo:hi], start=True, stop=True)
                ins.then_inc(ml_g.sem, 1)
                ns = hi // P
                for s in range(ns):
                    if ml_s.seen.get("pe", 0) >= 2:
                        pe.wait_ge(ml_w.sem, ml_s.seen["pe"] - 1)
                    pe.matmul(PS[:, 2 + ml_s.seen.get("pe", 0) % 2, 0:w], ka[:, h, P * s:P * s + P], qa[:, h, lo:hi],
                              start=True, stop=True).then_inc(ml_s.sem, 1)
                    ml_s.advance("pe", 1)
                pe.wait_ge(ml_e.sem, ml_e.next("pe"))
                for d, sel in enumerate(("self", "selb")):
                    ins = pe.matmul(PS[:, d, 0:w], C(sel, P * h)[0:64], EM[:, lo:hi], start=True, stop=True)
                ins.then_inc(ml_em.sem, 1)
                pe.wait_ge(ml_w.sem, ml_s.seen["pe"])
                for d in range(2):
                    order = list(range(ns))
                    if d == 1 and lo == 0:
                        order.reverse()
                    for k, s in enumerate(order):
                        a, b, _ = reach(d, s, lo, hi)
                        pe.matmul(PS[:, 4 + 2 * d, a:b], va[:, s, P * h:P * h + P], W_[:, d, s, a:b], start=(k == 0), stop=(k == ns - 1))
                    for k, s in enumerate(order):
                        a, b, _ = reach(d, s, lo, hi)
                        ins = pe.matmul(PS[:, 5 + 2 * d, a:b], C("ones"), W_[:, d, s, a:b], start=(k == 0), stop=(k == ns - 1))
                    ins.then_inc(ml_nd.sem, 1)

        def mlstm_act(act):
            for i, (h, (lo, hi)) in enumerate(PASSES):
                act.wait_ge(ml_g.sem, i + 1)
                act.wait_ge(ml_diag.sem, i + 1)
                if i >= 1:
                    act.wait_ge(ml_nd.sem, 2 * i)
                for s in range(hi // P):
                    for d in range(2):
                        a, b, q = reach(d, s, lo, hi)
                        bias = gt[:, s, d, h:h + 1]
                        if q is not None:
                            ins = nc.scalar.activation(W_[:, d, s, q:q + P], diag_buf(d, s), ACT.Exp, bias=bias)
                            a, b = (q + P, b) if d == 0 else (a, q)
                        if b > a:
                            ins = nc.scalar.activation(W_[:, d, s, a:b], PS[:, d, a:b], ACT.Exp, bias=bias, scale=-1.0)
                ins.then_inc(ml_e.sem, 1)
                for d in range(2):
                    act.wait_ge(ml_nd.sem, 2 * i + d + 1)
                    nc.scalar.activation((rstd, mean)[d][:, 0:hi - lo], PS[:, 5 + 2 * d, 0:hi - lo], ACT.Abs).then_inc(ml_abs.sem, 1)

        def mlstm_dve(dve):
            n_s = 0
            for i, (h, (lo, hi)) in enumerate(PASSES):
                w = hi - lo
                dve.wait_ge(ml_g.sem, i + 1)
                for s in range(lo // P, hi // P):
                    for d, mask in enumerate(("neg_ge", "neg_le")):
                        q = s * P - lo
                        ins = nc.vector.scalar_tensor_tensor(out=diag_buf(d, s), in0=PS[:, d, q:q + P], scalar=-1.0, in1=C(mask),
                                                             op0=ALU.mult, op1=ALU.add)
                ins.then_inc(ml_diag.sem, 1)
                dve.wait_ge(ml_e.sem, i + 1)
                for s in range(hi // P):
                    n_s += 1
                    dve.wait_ge(ml_s.sem, n_s)
                    for d in range(2):
                        a, b, _ = reach(d, s, lo, hi)
                        ins = nc.vector.tensor_tensor(W_[:, d, s, a:b], W_[:, d, s, a:b], PS[:, 2 + (n_s - 1) % 2, a:b], ALU.mult)
                    ins.then_inc(ml_w.sem, 1)
                dve.wait_ge(ml_em.sem, i + 1)
                for d in range(2):
                    r = (rstd, mean)[d][:, 0:w]
                    dve.wait_ge(ml_abs.sem, 2 * i + d + 1)
                    v_link(dve, nc.vector.tensor_tensor(r, r, PS[:, d, 0:w], ALU.max))
                    v_link(dve, nc.vector.reciprocal(r, r))
                    if d == 0:
                        v_link(dve, nc.vector.tensor_tensor(H[:, h, lo:hi], r, PS[:, 4, 0:w], ALU.mult))
                    else:
                        v_link(dve, nc.vector.tensor_tensor(r, r, PS[:, 6, 0:w], ALU.mult))
                        nc.vector.tensor_tensor(H[:, h, lo:hi], H[:, h, lo:hi], r, ALU.add).then_inc(ml_h.sem, 1)

        mlstm_out = head_norm([(H[:, h, a:b], H[:, h, a:b], "ones", 1.0 / P, "eps1", V("mlstm_g", h), oa[:, h, a:b])
                               for h in range(4) for a, b in ALL], 18432)
        qk_norm_b = head_norm([(qb[:, m, a:b], qb[:, m, a:b], "blk64", 1.0 / 64, "eps1", V("swa_q"), None)
                               for m in range(4) for a, b in ALL]
                              + [(kb[:, a:b], kb[:, a:b], "blk64", 1.0 / 64, "eps1", V("swa_k"), None) for a, b in ALL], 18432)
        rope_b = rope([qb[:, m, CTX:TOK] for m in range(4)] + [kb[:, CTX:TOK]], 64, 18432)
        kd = area(0, 2, TOK)
        dup_ready = signal("keys_doubled")

        def dup_pe(pe):
            for n in range(2):
                for j, (a, b) in enumerate(ALL):
                    ins = pe.matmul(PS[:, 2 * n + j, 0:b - a], C(f"dup{n}"), kb[:, a:b], start=True, stop=True)
            ins.then_inc(dup_ready.sem, 1)

        def dup_act(act):
            act.wait_ge(dup_ready.sem, 1)
            for n in range(2):
                for j, (a, b) in enumerate(ALL):
                    nc.scalar.activation(kd[:, n, a:b], PS[:, 2 * n + j, 0:b - a], ACT.Copy)

        def b_groups():
            out = []
            for blk in range(NT):
                if blk < NCT:
                    lat, masks = None, []
                else:
                    a, b = max(blk - 1, NCT), min(blk + 2, NT)
                    lat = (a * P, b * P)
                    masks = [(CTX + (t - a) * P, m) for t, m in ((blk - 1, "neg_ge"), (blk + 1, "neg_le")) if a <= t < b]
                for kv in range(2):
                    heads = [4 * kv + j for j in range(4)]
                    half = [64 * (h % 2) for h in heads]

                    def put(ps, kv=kv, blk=blk):
                        for par in range(2):
                            ins = nc.scalar.activation(H[64 * par:64 * par + 64, 4 + 2 * kv:6 + 2 * kv, blk * P:blk * P + P],
                                                       ps[:, par::2, :], ACT.Copy)
                        return ins

                    out.append(dict(q=[qb[o:o + 64, h // 2, blk * P:blk * P + P] for h, o in zip(heads, half)],
                                    k=[kd[o:o + 64, kv, :] for o in half], v=lambda kt, kv=kv: vb[:, kt, 64 * kv:64 * kv + 64],
                                    lat=lat, masks=masks, sinks=[V("sink", h) for h in heads], put=put, m=64))
            return out

        attn_b = attention(b_groups(), 64 ** -0.5, 3072, 18432)

        qc = area(0, 8, 512)
        kc = area(4096, 2, TOK)
        vc = area(5632, 6, 256)

        def c_plan():
            t = [ftile(x_h, LAT, "act", copy_act(to_lat(qc[:, m, :]))) for m in range(8)]
            t += [ftile(x_h, ALL, "dve", copy_dve(to(kc[:, m, :]))) for m in range(2)]
            t.append(ttile(x_h, range(NT), 2, "act", copy_act(lambda lo, hi: vc[:, lo // P, :])))
            return t

        def to_lat(dst):
            return lambda lo, hi: dst[:, lo - CTX:hi - CTX]

        qk_norm_c = head_norm([(qc[:, m, :], qc[:, m, :], "ones", 1.0 / P, "eps1", V("c_q"), None) for m in range(8)]
                              + [(kc[:, m, a:b], kc[:, m, a:b], "ones", 1.0 / P, "eps1", V("c_k"), None) for m in range(2) for a, b in ALL], 18432)
        rope_c = rope([qc[:, m, :] for m in range(8)] + [kc[:, m, CTX:TOK] for m in range(2)], 128, 18432)

        def c_groups():
            out = []
            for blk in range(NLT):
                for kv in range(2):
                    def put(ps, kv=kv, blk=blk):
                        return nc.scalar.activation(H[:, 4 * kv:4 * kv + 4, CTX + blk * P:CTX + blk * P + P], ps, ACT.Copy)
                    out.append(dict(q=[qc[:, 4 * kv + j, blk * P:blk * P + P] for j in range(4)], k=[kc[:, kv, :]] * 4,
                                    v=lambda kt, kv=kv: vc[:, kt, P * kv:P * kv + P], lat=(CTX, TOK), masks=[], sinks=None, put=put, m=P))
            return out

        attn_c = attention(c_groups(), P ** -0.5, 7168, 9472)

        up_, vp_ = area(0, 2, 512), area(1024, 2, 512)
        qkv = area(2048, 12, 512)
        zp = area(8192, 4, 512)
        be, de = area(10240, 512), area(10752, 512)
        qg, kg = area(11264, 512), area(11776, 512)
        rg = area(12288, 2, 512)
        gl = area(13312, 512)
        vg = area(13824, 4, 256)
        ktok, vtok = area(14848, 4, 512), area(16896, 4, 512)
        SC = 14848
        XL = X[:, :, CTX:TOK]
        Y = H[:, :, CTX:TOK]

        def ffn_plans(l):
            n = FF2 // P // PARTS[2]
            h_hi, h, h_lo = area(0, n, SEQ, of=arena_r), area(n * SEQ, n, SEQ), area(n * SEQ, n, SEQ, of=arena_r)
            out = []
            for q in range(PARTS[2]):
                up = []
                for m in range(n):
                    a = ftile(x_x, LAT, "act", lambda eng, ps, lo, hi, m=m: nc.scalar.activation(h[:, m, :], ps, ACT.Silu))

                    def times(eng, ps, lo, hi, m=m, gate_out=a["outs"][0]):
                        eng.wait_ge(evac["act"].sem, gate_out.freed)
                        return nc.vector.tensor_tensor(h[:, m, :], h[:, m, :], ps, ALU.mult)

                    up += [a, ftile(x_x, LAT, "dve", times, post=split_hidden(*(
                        lambda lo, hi, m=m, part=part: part[:, m, :] for part in (h_hi, h, h_lo))))]

                def half_add(m, first):
                    def ev(eng, ps, lo, hi):
                        if first:
                            v_link(eng, nc.vector.tensor_scalar(X[:, m, lo:hi], X[:, m, lo:hi], ALPHA, None, ALU.mult))
                        return nc.vector.scalar_tensor_tensor(out=X[:, m, lo:hi], in0=ps, scalar=0.5, in1=X[:, m, lo:hi],
                                                              op0=ALU.mult, op1=ALU.add)
                    return ev

                out += [up, [ftile(lambda k, lo, hi: (h_hi[:, k, :], h_lo[:, k, :]), LAT, "dve", half_add(m, q == 0), kt=n)
                             for m in range(KD)]]
            return out

        cv, cv_done = signal("convolved"), signal("silu_of_conv_done")

        def conv_dve(l, t):
            y, x = area(SC + 2048 + 512 * (t % 4), 512), qkv[:, t, :]
            tap = [V("conv", 48 * l + 12 * i + t) for i in range(4)]

            def post(dve, o, lo, hi):
                dve.wait_ge(evac[o.who].sem, o.freed)
                if t >= 4:
                    dve.wait_ge(cv_done.sem, 12 * l + t - 3)
                v_link(dve, nc.vector.tensor_scalar(y, x, tap[3], None, ALU.mult))
                for back in range(1, 4):
                    ins = nc.vector.scalar_tensor_tensor(out=y[:, back:], in0=x[:, 0:512 - back], scalar=tap[3 - back], in1=y[:, back:],
                                                         op0=ALU.mult, op1=ALU.add)
                    if back < 3:
                        v_link(dve, ins)
                ins.then_inc(cv.sem, 1)
            return post

        def conv_act(t):
            def late(act):
                act.wait_ge(cv.sem, cv.next("act"))
                nc.scalar.activation(qkv[:, t, :], area(SC + 2048 + 512 * (t % 4), 512), ACT.Silu).then_inc(cv_done.sem, 1)
            return late

        def in_plan(l):
            dsts = [up_[:, 0, :], up_[:, 1, :], vp_[:, 0, :], vp_[:, 1, :]] + [qkv[:, m, :] for m in range(12)] \
                + [zp[:, m, :] for m in range(4)] + [be, de, qg, kg, rg[:, 0, :], rg[:, 1, :], gl]
            t = []
            for i, d in enumerate(dsts):
                if i < 4:
                    t.append(ftile(x_x, LAT, "act", func_act(to_lat(d), ACT.Gelu_apprx_tanh)))
                elif i < 16:
                    t.append(ftile(x_x, LAT, "act", copy_act(to_lat(d)), post=conv_dve(l, i - 4), late=conv_act(i - 4)))
                elif i < 20 or i in (24, 25):
                    t.append(ftile(x_x, LAT, "act", func_act(to_lat(d), ACT.Silu)))
                else:
                    t.append(ftile(x_x, LAT, "dve", copy_dve(to_lat(d))))
            t.append(ttile(x_x, range(NCT, NT), 2, "act", copy_act(lambda lo, hi: vg[:, lo // P - NCT, :])))
            return t

        def mix_plan():
            def ev_for(m):
                def ev(eng, ps, lo, hi):
                    v_link(eng, nc.vector.tensor_scalar(X[:, m, lo:hi], X[:, m, lo:hi], ALPHA, None, ALU.mult))
                    return nc.vector.tensor_tensor(X[:, m, lo:hi], X[:, m, lo:hi], ps, ALU.add)
                return ev
            return [ftile(x_x, LAT, "dve", ev_for(m)) for m in range(KD)]

        sg_mean, sg_sq, sg_std, sg_v, sg_t, sg_tc, sg_z, sg_w = (signal(n) for n in (
            "sgu_centred", "sgu_squares", "sgu_std", "sgu_v_normed", "sgu_v_turned", "sgu_v_token_major", "sgu_mixed", "sgu_w_masked"))
        wsT = area(SC, 4, P)
        bs_row = area(SC + 512, 512)
        gup = area(SC + 1024, P)
        vt = area(SC + 1536, 4, 256)
        sq2 = area(SC + 2560, 2, 512)

        def sgu_act(act):
            act.wait_ge(sg_mean.sem, sg_mean.next("act"))
            for t in range(2):
                ins = nc.scalar.activation(sq2[:, t, :], vp_[:, t, :], ACT.Square)
            ins.then_inc(sg_sq.sem, 1)
            act.wait_ge(sg_t.sem, sg_t.next("act"))
            a_link(act, nc.scalar.activation(rstd[:], PS[:, 1, :], ACT.Ln, bias=V("eps2"), scale=1.0 / 256))
            nc.scalar.activation(rstd[:], rstd[:], ACT.Exp, scale=-0.5).then_inc(sg_std.sem, 1)
            act.wait_ge(sg_t.sem, sg_t.next("act"))
            nc.scalar.activation(vt[:, 0:2, :], PS[:, 2, :].rearrange("p (a b) -> p a b", a=2), ACT.Copy)
            nc.scalar.activation(vt[:, 2:4, :], PS[:, 3, :].rearrange("p (a b) -> p a b", a=2), ACT.Copy).then_inc(sg_tc.sem, 1)

        def sgu_pe(pe):
            for t in range(2):
                ins = pe.matmul(PS[:, 0, :], C("ones"), vp_[:, t, :], start=(t == 0), stop=(t == 1))
            ins.then_inc(sg_z.sem, 1)
            pe.wait_ge(sg_sq.sem, sg_sq.next("pe"))
            for t in range(2):
                ins = pe.matmul(PS[:, 1, :], C("ones"), sq2[:, t, :], start=(t == 0), stop=(t == 1))
            ins.then_inc(sg_t.sem, 1)
            pe.wait_ge(sg_v.sem, sg_v.next("pe"))
            for n in range(NLT):
                for t in range(2):
                    ins = pe.transpose(PS[:, 2 + n // 2, 256 * (n % 2) + P * t:256 * (n % 2) + P * t + P],
                                       vp_[:, t, P * n:P * n + P], C("ident"))
            ins.then_inc(sg_t.sem, 1)
            pe.wait_ge(sg_tc.sem, sg_tc.next("pe"))
            pe.wait_ge(sg_w.sem, sg_w.next("pe"))
            for h in range(4):
                o = 64 * (h % 2)
                for n in range(NLT):
                    dst = PS[o:o + 64, 4 + h // 2, P * n:P * n + P]
                    pe.matmul(dst, vt[:, n, 64 * h:64 * h + 64], wsT[:, h, :], start=True, stop=False)
                    ins = pe.matmul(dst, C("ones")[0:1, 0:64], bs_row[0:1, P * h:P * h + P], start=False, stop=True)
            ins.then_inc(sg_z.sem, 1)

        def sgu_dve(dve, l):
            dve.wait_ge(small_loaded.sem, 64 + 48 * l)
            nc.vector.tensor_tensor(wsT, wsT, C("m_ge").unsqueeze(1).to_broadcast([P, 4, P]), ALU.mult).then_inc(sg_w.sem, 1)
            dve.wait_ge(sg_z.sem, sg_z.next("dve"))
            v_link(dve, nc.vector.tensor_scalar(mean[:], PS[:, 0, :], 1.0 / 256, None, ALU.mult))
            for t in range(2):
                ins = nc.vector.tensor_tensor(vp_[:, t, :], vp_[:, t, :], mean[:], ALU.subtract)
            ins.then_inc(sg_mean.sem, 1)
            dve.wait_ge(sg_mean.sem, sg_mean.next("dve"))
            dve.wait_ge(sg_std.sem, sg_std.next("dve"))
            for t in range(2):
                v_link(dve, nc.vector.tensor_tensor(vp_[:, t, :], vp_[:, t, :], rstd[:], ALU.mult))
                ins = nc.vector.tensor_scalar(vp_[:, t, :], vp_[:, t, :], V("sgu_g", 2 * l + t), V("sgu_b", 2 * l + t), ALU.mult, ALU.add)
            ins.then_inc(sg_v.sem, 1)
            dve.wait_ge(sg_z.sem, sg_z.next("dve"))
            for t in range(2):
                nc.vector.tensor_tensor(Y[:, t, :], up_[:, t, :], PS[:, 4 + t, :], ALU.mult)

        bc, qd_, kx, kdec = (area(SC + 2048 + 512 * i, 512) for i in range(4))
        kdt = area(SC + 4096, 4, P)
        pTg = area(SC + 4608, 4, 512)
        Sg = area(SC + 6656, 9, 256)
        blocks = area(0, 256)
        gtg = small[:, 48:56]
        (ga_low, ga_arg, ga_log, ga_cum, ga_exp, ga_prod, ga_kt, ga_ktc, ga_s, ga_pt, ga_st, ga_state, ga_o) = (signal(n) for n in (
            "gla_gate_product", "gla_gate_arg", "gla_gate_log", "gla_decay_sums", "gla_decays", "gla_decayed_qk", "gla_k_turned",
            "gla_k_token_major", "gla_scores", "gla_scores_masked", "gla_updates", "gla_states", "gla_outputs"))

        GS = (0, 1, 6, 7)

        def update_bank(c):
            return PS[:, 2 + 2 * (c % 2) + c // 4, 256 * (c // 2 % 2):256 * (c // 2 % 2) + 256]

        def gla_act(act, l):
            act.wait_ge(ga_low.sem, ga_low.next("act"))
            a_link(act, nc.scalar.activation(bc, PS[:, 0, :], ACT.Identity, bias=V("gla_gb", l)))
            a_link(act, nc.scalar.activation(qd_, bc, ACT.Abs))
            a_link(act, nc.scalar.activation(qd_, qd_, ACT.Exp, scale=-1.0))
            nc.scalar.activation(qd_, qd_, ACT.Ln, bias=V("one")).then_inc(ga_log.sem, 1)
            act.wait_ge(ga_cum.sem, ga_cum.next("act"))
            nc.scalar.activation(qd_, bc, ACT.Exp)
            nc.scalar.activation(gtg, bc.rearrange("p (c t) -> p c t", t=64)[:, :, 63], ACT.Exp)
            nc.scalar.activation(kx, bc, ACT.Exp, scale=-1.0)
            nc.scalar.activation(kdec, kdec, ACT.Exp).then_inc(ga_exp.sem, 1)
            act.wait_ge(ga_kt.sem, ga_kt.next("act"))
            nc.scalar.activation(kdt, PS[:, 1, :].rearrange("p (a b) -> p a b", a=4), ACT.Copy).then_inc(ga_ktc.sem, 1)

        def gla_dve(dve, l):
            dve.wait_ge(ga_log.sem, ga_log.next("dve"))
            v_link(dve, nc.vector.scalar_tensor_tensor(out=bc, in0=bc, scalar=0.0, in1=qd_, op0=ALU.min, op1=ALU.subtract))
            v_link(dve, nc.vector.tensor_scalar(kx, bc, 1.0 / 16.0, None, ALU.mult))
            v_link(dve, nc.vector.tensor_tensor_scan(bc, C("rs64", 0, 512), kx, 0.0, ALU.mult, ALU.add))
            b3 = bc.rearrange("p (c t) -> p c t", t=64)
            nc.vector.tensor_tensor(kdec.rearrange("p (c t) -> p c t", t=64), b3[:, :, 63:64].to_broadcast([P, 8, 64]), b3,
                                    ALU.subtract).then_inc(ga_cum.sem, 1)
            dve.wait_ge(ga_exp.sem, ga_exp.next("dve"))
            nc.vector.scalar_tensor_tensor(out=qd_, in0=qg, scalar=32 ** -0.5, in1=qd_, op0=ALU.mult, op1=ALU.mult)
            nc.vector.tensor_tensor(kx, kx, kg, ALU.mult)
            nc.vector.tensor_tensor(kdec, kdec, kg, ALU.mult).then_inc(ga_prod.sem, 1)
            v_link(dve, nc.vector.memset(Sg[:, 0, :], 0.0))
            dve.wait_ge(ga_st.sem, ga_st.next("dve"))
            for c in range(7):
                nc.vector.tensor_scalar(Sg[:, c + 1, :], Sg[:, c, :], gtg[:, c:c + 1], None, ALU.mult)
                v_link(dve, nc.vector.tensor_tensor(blocks, update_bank(c), C("bd_gla", 0, 256), ALU.mult))
                v_link(dve, nc.vector.tensor_tensor(Sg[:, c + 1, :], Sg[:, c + 1, :], blocks, ALU.add))
            for h in range(4):
                dve.wait_ge(ga_s.sem, ga_s.next("dve"))
                nc.vector.tensor_tensor(pTg[:, :, P * h:P * h + P], PS[:, GS[h], :].rearrange("p (n t) -> p n t", n=4),
                                        C("m_gla").unsqueeze(1).to_broadcast([P, 4, P]), ALU.mult).then_inc(ga_pt.sem, 1)
            dve.wait_ge(ga_o.sem, ga_o.next("dve"))
            for p in range(2):
                nc.vector.tensor_copy(Y[:, 6 + p, :], PS[:, 6 + p, :])

        def gla_pe(pe, l):
            pe.wait_ge(small_loaded.sem, 64 + 48 * l)
            pe.matmul(PS[:, 0, :], gup[0:16, :], gl[0:16, :], start=True, stop=True).then_inc(ga_low.sem, 1)
            pe.wait_ge(ga_prod.sem, ga_prod.next("pe"))
            for n in range(NLT):
                ins = pe.transpose(PS[:, 1, P * n:P * n + P], kdec[:, P * n:P * n + P], C("ident"))
            ins.then_inc(ga_kt.sem, 1)
            pe.wait_ge(ga_ktc.sem, ga_ktc.next("pe"))
            for c in range(7):
                o, n = 64 * (c % 2), c // 2
                ins = pe.matmul(update_bank(c), kdt[o:o + 64, n, :], vg[o:o + 64, n, :], start=True, stop=True)
            ins.then_inc(ga_st.sem, 1)
            for h in range(4):
                for n in range(NLT):
                    a, b = 32 * h, P * n
                    ins = pe.matmul(PS[:, GS[h], b:b + P], kx[a:a + 32, b:b + P], qd_[a:a + 32, b:b + P], start=True, stop=True)
                ins.then_inc(ga_s.sem, 1)
            pe.wait_ge(ga_pt.sem, ga_pt.next("pe", 4))
            for n in range(NLT):
                for p in range(2):
                    for j in range(2):
                        h = 2 * p + j
                        pe.matmul(PS[64 * j:64 * j + 64, 6 + p, P * n:P * n + P], vg[:, n, 64 * h:64 * h + 64],
                                  pTg[:, n, P * h:P * h + P], start=True, stop=False, skip_group_check=True)
                    for c in (2 * n, 2 * n + 1):
                        ins = pe.matmul(PS[:, 6 + p, 64 * c:64 * c + 64], Sg[:, c, P * p:P * p + P], qd_[:, 64 * c:64 * c + 64],
                                        start=False, stop=True, skip_group_check=True)
            ins.then_inc(ga_o.sem, 1)

        gla_norm = [head_norm([(Y[:, 6 + p, :], Y[:, 6 + p, :], "blk64", 1.0 / 64, "eps2", V("gla_g", l), rg[:, p, :]) for p in range(2)], SC)
                    for l in range(2)]

        l2_qk = head_norm([(qkv[:, t, :], qkv[:, t, :], "blk64", 1.0, "epsl", 0.125 if t < 4 else 1.0, None) for t in range(8)], SC)
        R4 = area(18944, 512)
        R4T = area(19456, 4, P)
        bk = area(19968, 4, 512)
        wT = area(22016, 4, 512)
        ub = area(6144, 4, 512)
        (gr_exp, gr_rows, gr_r4, gr_t, gr_tc, gr_kv) = (signal(n) for n in (
            "gdn_gate_exps", "gdn_row_args", "gdn_rows", "gdn_rows_turned", "gdn_rows_token_major", "gdn_kv_turned"))

        def rows_act(act, l):
            r = de[0:8]
            s0, s1 = rstd[0:8, :], mean[0:8, :]
            a_link(act, nc.scalar.activation(r, r, ACT.Identity, bias=V("dt_b", l)[0:8]))
            a_link(act, nc.scalar.activation(s0, r, ACT.Abs))
            a_link(act, nc.scalar.activation(s0, s0, ACT.Exp, scale=-1.0))
            nc.scalar.activation(s0, s0, ACT.Ln, bias=V("one")[0:8])
            nc.scalar.activation(small[0:8, 56:57], V("a_log", l)[0:8], ACT.Exp).then_inc(gr_exp.sem, 1)
            act.wait_ge(gr_rows.sem, gr_rows.next("act"))
            nc.scalar.activation(R4[0:8, :], be[0:8, :], ACT.Sigmoid)
            nc.scalar.activation(R4[32:40, :], r, ACT.Copy)
            nc.scalar.activation(R4[64:72, :], s1, ACT.Exp)
            nc.scalar.activation(R4[96:104, :], r, ACT.Exp).then_inc(gr_r4.sem, 1)
            act.wait_ge(gr_t.sem, gr_t.next("act"))
            nc.scalar.activation(R4T, PS[:, 0, :].rearrange("p (a b) -> p a b", a=4), ACT.Copy).then_inc(gr_tc.sem, 1)

        def rows_dve(dve, l):
            r = de[0:8]
            s0, s1 = rstd[0:8, :], mean[0:8, :]
            v_link(dve, nc.vector.memset(R4, 0.0))
            dve.wait_ge(gr_exp.sem, gr_exp.next("dve"))
            v_link(dve, nc.vector.scalar_tensor_tensor(out=s0, in0=r, scalar=0.0, in1=s0, op0=ALU.max, op1=ALU.add))
            v_link(dve, nc.vector.tensor_scalar(s0, s0, small[0:8, 56:57], -1.0, ALU.mult, ALU.mult))
            v_link(dve, nc.vector.tensor_tensor_scan(r, C("rs128", 0, 512)[0:8], s0, 0.0, ALU.mult, ALU.add))
            r3 = r.rearrange("p (c t) -> p c t", t=P)
            nc.vector.tensor_tensor(s1.rearrange("p (c t) -> p c t", t=P), r3[:, :, P - 1:P].to_broadcast([8, 4, P]), r3,
                                    ALU.subtract).then_inc(gr_rows.sem, 1)
            dve.wait_ge(gr_tc.sem, gr_tc.next("dve"))
            v_link(dve, nc.vector.tensor_tensor(R4T[:, :, 96:104], R4T[:, :, 96:104], R4T[:, :, 0:8], ALU.mult))
            for i in range(8):
                n = i % 4

                def heads(t):
                    return t.rearrange("p (h d) -> p h d", h=8)

                def per_head(c):
                    return R4T[:, n, c:c + 8].unsqueeze(2).to_broadcast([P, 8, 64])

                dve.wait_ge(gr_kv.sem, gr_kv.next("dve"))
                src = heads(PS[:, (i + 1) % 8, :])
                if i < 4:
                    nc.vector.tensor_tensor(heads(bk[:, n, :]), src, per_head(96), ALU.mult)
                    nc.vector.tensor_tensor(heads(ktok[:, n, :]), src, per_head(64), ALU.mult)
                else:
                    nc.vector.tensor_tensor(heads(vtok[:, n, :]), src, per_head(0), ALU.mult)

        def rows_pe(pe, l):
            def turn(i):
                n = i % 4
                for p in range(4):
                    ins = pe.transpose(PS[:, (i + 1) % 8, P * p:P * p + P], qkv[:, 4 + 4 * (i // 4) + p, P * n:P * n + P], C("ident"))
                ins.then_inc(gr_kv.sem, 1)

            for i in range(7):
                turn(i)
            pe.wait_ge(gr_r4.sem, gr_r4.next("pe"))
            for n in range(4):
                ins = pe.transpose(PS[:, 0, P * n:P * n + P], R4[:, P * n:P * n + P], C("ident"))
            ins.then_inc(gr_t.sem, 1)
            pe.wait_ge(gr_tc.sem, gr_tc.next("pe"))
            turn(7)

        class Block4:

            def __init__(self, view):
                self.all = view

            def chunk(self, n):
                return self.all[:, n // 2, P * (n % 2):P * (n % 2) + P]

        def pair(view512):
            return Block4(view512.rearrange("p (a b) -> p a b", a=2))

        sets = [[pair(area(11264 + 512 * i, 512)) for i in range(7)],
                [Block4(H[:, 2 * i:2 * i + 2, 0:CTX]) for i in range(4)] + [Block4(X[:, 2 * i:2 * i + 2, 0:CTX]) for i in range(3)]]

        def pt_of(h):
            return pair(area(512 * h, 512)) if h < 4 else pair(H[:, h - 2, CTX:TOK])

        (so_in, so_arg, so_dec, so_L, so_t, so_tc, so_lb, so_y, so_yc, so_x, so_xn, so_out, so_oc) = (signal(n) for n in (
            "solve_inputs", "solve_decay_args", "solve_decays", "solve_L", "solve_L_turned", "solve_LT", "solve_level_masked",
            "solve_y", "solve_y_copied", "solve_products", "solve_inverse_updated", "solve_outputs", "solve_outputs_copied"))
        LEVELS = 7

        def bank(sidx, i):
            return PS[:, 4 * sidx + i, :]

        def half(h):
            return slice(64 * (h % 2), 64 * (h % 2) + 64)

        def solve_pe(pe):
            for hp in range(4):
                for s in range(2):
                    h = 2 * hp + s
                    if hp >= 1:
                        pe.wait_ge(so_oc.sem, so_oc.next("pe"))
                    pe.matmul(bank(s, 0), C("sel", P * h)[0:8], de[0:8, :], start=True, stop=True)
                    for n in range(4):
                        kk = qkv[half(h), 4 + hp, P * n:P * n + P]
                        pe.matmul(bank(s, 1)[:, P * n:P * n + P], kk, kk, start=True, stop=True)
                    for n in range(4):
                        ins = pe.matmul(bank(s, 2)[:, P * n:P * n + P], qkv[half(h), 4 + hp, P * n:P * n + P],
                                        qkv[half(h), hp, P * n:P * n + P], start=True, stop=True)
                    ins.then_inc(so_in.sem, 1)
                for s in range(2):
                    L = sets[s][1]
                    pe.wait_ge(so_L.sem, so_L.next("pe"))
                    for n in range(4):
                        ins = pe.transpose(bank(s, 3)[:, P * n:P * n + P], L.chunk(n), C("ident"))
                    ins.then_inc(so_t.sem, 1)
                for lv in range(1, LEVELS):
                    for s in range(2):
                        _, _, LT, Xi, XT, Yb, Lb = sets[s]
                        Lb = sets[s][6 if lv % 2 else 0]
                        pe.wait_ge(so_lb.sem, so_lb.next("pe"))
                        pe.wait_ge(so_xn.sem, so_xn.next("pe"))
                        for n in range(4):
                            ins = pe.matmul(bank(s, 0)[:, P * n:P * n + P], Lb.chunk(n), Xi.chunk(n), start=True, stop=True)
                        ins.then_inc(so_y.sem, 1)
                    for s in range(2):
                        _, _, LT, Xi, XT, Yb, Lb = sets[s]
                        pe.wait_ge(so_yc.sem, so_yc.next("pe"))
                        for n in range(4):
                            if lv < LEVELS - 1:
                                pe.matmul(bank(s, 1)[:, P * n:P * n + P], XT.chunk(n), Yb.chunk(n), start=True, stop=True)
                            ins = pe.matmul(bank(s, 2)[:, P * n:P * n + P], Yb.chunk(n), XT.chunk(n), start=True, stop=True)
                        ins.then_inc(so_x.sem, 1)
                for s in range(2):
                    h = 2 * hp + s
                    XT = sets[s][4]
                    pe.wait_ge(so_xn.sem, so_xn.next("pe"))
                    for n in range(4):
                        pe.matmul(bank(s, 3)[:, 64 * n:64 * n + 64], XT.chunk(n), vtok[:, n, 64 * h:64 * h + 64], start=True, stop=True)
                        ins = pe.matmul(bank(s, 0)[half(h), P * n:P * n + P], bk[:, n, 64 * h:64 * h + 64], XT.chunk(n), start=True, stop=True)
                    ins.then_inc(so_out.sem, 1)
            pe.wait_ge(so_oc.sem, so_oc.next("pe", 2))

        def solve_act(act):
            for hp in range(4):
                for s in range(2):
                    A, L = sets[s][0], sets[s][1]
                    act.wait_ge(so_arg.sem, so_arg.next("act"))
                    nc.scalar.activation(A.all, A.all, ACT.Exp)
                    nc.scalar.activation(L.all, L.all, ACT.Exp, scale=-1.0).then_inc(so_dec.sem, 1)
                for s in range(2):
                    act.wait_ge(so_t.sem, so_t.next("act"))
                    nc.scalar.activation(sets[s][2].all, bank(s, 3).rearrange("p (a b) -> p a b", a=2), ACT.Copy).then_inc(so_tc.sem, 1)
                for lv in range(1, LEVELS):
                    for s in range(2):
                        act.wait_ge(so_y.sem, so_y.next("act"))
                        nc.scalar.activation(sets[s][5].all, bank(s, 0).rearrange("p (a b) -> p a b", a=2), ACT.Copy).then_inc(so_yc.sem, 1)
                for s in range(2):
                    h = 2 * hp + s
                    act.wait_ge(so_out.sem, so_out.next("act"))
                    nc.scalar.activation(ub[:, :, 64 * h:64 * h + 64], bank(s, 3)[:, 0:256].rearrange("p (n d) -> p n d", n=4), ACT.Copy)
                    nc.scalar.activation(wT[half(h), hp, :], bank(s, 0)[half(h), :], ACT.Copy).then_inc(so_oc.sem, 1)

        def solve_pool(pool, layer):
            for hp in range(4):
                for lv in range(1, LEVELS):
                    for s in range(2):
                        if lv == 1:
                            pool.wait_ge(so_tc.sem, so_tc.next("pool"))
                        if lv == 2:
                            pool.wait_ge(so_xn.sem, so_xn.next("pool"))
                        if lv >= 3:
                            pool.wait_ge(so_y.sem, so_y.next("pool"))
                        LT, Lb = sets[s][2], sets[s][6 if lv % 2 else 0]
                        for n in range(4):
                            ins = nc.gpsimd.tensor_tensor(Lb.chunk(n), LT.chunk(n), C("levt", P * lv), ALU.mult)
                        ins.then_inc(so_lb.sem, 1)
                so_y.advance("pool", 2 * 2)
                so_xn.advance("pool", 2 * 6)

        def solve_dve(dve):
            Splits.order.append(("solve", 0))
            for hp in range(4):
                for s in range(2):
                    h = 2 * hp + s
                    A, L = sets[s][0], sets[s][1]
                    dve.wait_ge(so_in.sem, so_in.next("dve"))
                    for n in range(4):
                        gam = R4T[:, n, 32 + h:33 + h]
                        g = bank(s, 0)[:, P * n:P * n + P]
                        nc.vector.scalar_tensor_tensor(out=A.chunk(n), in0=g, scalar=gam, in1=C("neg_ge"), op0=ALU.subtract, op1=ALU.add)
                        ins = nc.vector.scalar_tensor_tensor(out=L.chunk(n), in0=g, scalar=gam, in1=C("pos_lt"), op0=ALU.subtract, op1=ALU.add)
                    ins.then_inc(so_arg.sem, 1)
                for s in range(2):
                    h = 2 * hp + s
                    A, L = sets[s][0], sets[s][1]
                    dve.wait_ge(so_dec.sem, so_dec.next("dve"))
                    for n in range(4):
                        ins = nc.vector.scalar_tensor_tensor(out=L.chunk(n), in0=bank(s, 1)[:, P * n:P * n + P], scalar=R4T[:, n, h:h + 1],
                                                             in1=L.chunk(n), op0=ALU.mult, op1=ALU.mult)
                    ins.then_inc(so_L.sem, 1)
                    nc.vector.tensor_tensor(pt_of(h).all, A.all, bank(s, 2).rearrange("p (a b) -> p a b", a=2), ALU.mult)
                for s in range(2):
                    _, L, LT, Xi, XT, _, Lb = sets[s]
                    dve.wait_ge(so_tc.sem, so_tc.next("dve"))
                    for n in range(4):
                        nc.vector.tensor_tensor(Xi.chunk(n), L.chunk(n), C("lev"), ALU.mult)
                        ins = nc.vector.tensor_tensor(XT.chunk(n), LT.chunk(n), C("levt"), ALU.mult)
                    v_link(dve, ins)
                    for n in range(4):
                        nc.vector.tensor_tensor(Xi.chunk(n), C("ident"), Xi.chunk(n), ALU.subtract)
                        ins = nc.vector.tensor_tensor(XT.chunk(n), C("ident"), XT.chunk(n), ALU.subtract)
                    ins.then_inc(so_xn.sem, 1)
                for lv in range(1, LEVELS):
                    for s in range(2):
                        _, _, LT, Xi, XT, _, Lb = sets[s]
                        dve.wait_ge(so_x.sem, so_x.next("dve"))
                        ps1, ps2 = (bank(s, i).rearrange("p (a b) -> p a b", a=2) for i in (1, 2))
                        if lv < LEVELS - 1:
                            nc.vector.tensor_tensor(Xi.all, Xi.all, ps1, ALU.subtract)
                            nc.vector.tensor_tensor(XT.all, XT.all, ps2, ALU.subtract).then_inc(so_xn.sem, 1)
                        else:
                            nc.vector.tensor_tensor(XT.all, XT.all, ps2, ALU.subtract).then_inc(so_xn.sem, 1)

        S = area(11264, 4, P)
        uu = area(11776, 512)
        tS = area(12288, 4, P)
        egx = area(12800, 512)
        gtot = small[:, 64:80].rearrange("p (q n) -> p q n", q=4)
        (re_eg0, re_eg, re_qd, re_gt, re_gtx, re_w, re_u, re_s, re_sn, re_o) = (signal(n) for n in (
            "rec_exp_rows", "rec_exp_spread", "rec_q_decayed", "rec_total_spread", "rec_total_exp", "rec_w_product", "rec_u", "rec_update", "rec_state", "rec_outputs"))

        def rec_pe(pe):
            for p in range(4):
                ins = pe.matmul(PS[:, 0, 4 * p:4 * p + 4], C("selp", P * p)[0:8], de[0:8, P - 1::P], start=True, stop=True)
            ins.then_inc(re_gt.sem, 1)
            pe.wait_ge(re_eg0.sem, re_eg0.next("pe"))
            for p in range(4):
                if p >= 2:
                    pe.wait_ge(re_qd.sem, re_qd.next("pe"))
                pe.matmul(PS[:, 1 + p % 2, :], C("selp", P * p)[0:8], egx[0:8, :], start=True, stop=True).then_inc(re_eg.sem, 1)
            pe.wait_ge(re_qd.sem, re_qd.next("pe", 2))
            pe.wait_ge(re_sn.sem, re_sn.next("pe"))
            for n in range(4):
                cols = slice(P * n, P * n + P)
                for p in range(4):
                    ins = pe.matmul(PS[:, 0, P * p:P * p + P], wT[:, p, cols], S[:, p, :], start=True, stop=True)
                ins.then_inc(re_w.sem, 1)
                for p in range(4):
                    ins = pe.matmul(PS[:, 4 + p, cols], S[:, p, :], qkv[:, p, cols], start=True, stop=False, skip_group_check=True)
                pe.wait_ge(re_u.sem, re_u.next("pe"))
                if n < 3:
                    for p in range(4):
                        ins = pe.matmul(PS[:, 3, P * p:P * p + P], ktok[:, n, P * p:P * p + P], uu[:, P * p:P * p + P], start=True, stop=True)
                    ins.then_inc(re_s.sem, 1)
                for h in range(8):
                    ins = pe.matmul(PS[half(h), 4 + h // 2, cols], uu[:, 64 * h:64 * h + 64], pt_of(h).chunk(n), start=False, stop=True,
                                    skip_group_check=True)
                ins.then_inc(re_o.sem, 1)
                if n < 3:
                    pe.wait_ge(re_sn.sem, re_sn.next("pe"))

        def rec_act(act):
            nc.scalar.activation(egx[0:8, :], de[0:8, :], ACT.Exp).then_inc(re_eg0.sem, 1)
            act.wait_ge(re_gt.sem, re_gt.next("act"))
            nc.scalar.activation(gtot, PS[:, 0, 0:16].rearrange("p (q n) -> p q n", q=4), ACT.Exp).then_inc(re_gtx.sem, 1)

        def rec_dve(dve):
            v_link(dve, nc.vector.memset(S, 0.0))
            for p in range(4):
                dve.wait_ge(re_eg.sem, re_eg.next("dve"))
                nc.vector.tensor_tensor(qkv[:, p, :], qkv[:, p, :], PS[:, 1 + p % 2, :], ALU.mult).then_inc(re_qd.sem, 1)
            dve.wait_ge(re_gtx.sem, re_gtx.next("dve"))
            nc.vector.tensor_copy(tS[:, 0, 0:1], S[:, 0, 0:1]).then_inc(re_sn.sem, 1)
            for n in range(4):
                dve.wait_ge(re_w.sem, re_w.next("dve"))
                if n >= 1:
                    dve.wait_ge(re_o.sem, re_o.next("dve"))
                nc.vector.tensor_tensor(uu, ub[:, n, :], PS[:, 0, :], ALU.subtract).then_inc(re_u.sem, 1)
                if n < 3:
                    dve.wait_ge(re_s.sem, re_s.next("dve"))
                    nc.vector.tensor_tensor(S, S, gtot[:, :, n:n + 1].to_broadcast([P, 4, P]), ALU.mult)
                    v_link(dve, nc.vector.tensor_tensor(tS, PS[:, 3, :].rearrange("p (a b) -> p a b", a=4),
                                                        C("blk64").unsqueeze(1).to_broadcast([P, 4, P]), ALU.mult))
                    nc.vector.tensor_tensor(S, S, tS, ALU.add).then_inc(re_sn.sem, 1)
            dve.wait_ge(re_o.sem, re_o.next("dve"))
            for p in range(4):
                nc.vector.tensor_copy(Y[:, 2 + p, :], PS[:, 4 + p, :])

        gdn_norm = [head_norm([(Y[:, 2 + p, :], Y[:, 2 + p, :], "blk64", 1.0 / 64, "eps2", V("gdn_g", l), zp[:, p, :]) for p in range(4)], SC)
                    for l in range(2)]

        def second_loads(l):
            def fn(act):
                if l == 0:
                    act.dma_start(con2[:, 0:N_SECOND], second_d).then_inc(small_loaded.sem, 16)
                act.dma_start(wsT, sguw_d[l]).then_inc(small_loaded.sem, 16)
                act.dma_start(bs_row[0:1, :], sgub_d[l:l + 1]).then_inc(small_loaded.sem, 16)
                act.dma_start(gup[0:16, :], gup_d[l]).then_inc(small_loaded.sem, 16)
            return fn

        stages = []

        def add(pe=None, act=None, dve=None):
            stages.append((pe, act, dve))

        def add_gemm(tiles, before=None, fresh=False):
            n = len(split_inputs) if fresh else 0
            def act_fn(e):
                if before:
                    before(e)
                gemm_evac(e, "act", tiles)
            add(lambda e: gemm_pe(e, tiles, n), act_fn, lambda e: gemm_evac(e, "dve", tiles))

        def add_norm(segs, eps, centred, affine):
            add(lambda e: norm_pe(e, segs, centred), lambda e: norm_act(e, segs, eps, centred, affine), lambda e: norm_dve(e, segs, centred))
            split_tiles_of(X if centred else H, centred, segs)

        add(ada_pe, ada_act, ada_dve)
        add_norm(ALL, "eps1", False, modulate(0, 0))
        add_gemm(ab_plan(), fresh=True)
        add(gates_pe, gates_act, gates_dve)
        add(mlstm_pe, mlstm_act, mlstm_dve)
        add(*mlstm_out)
        add(*qk_norm_b)
        add(rope_b[0], None, rope_b[1])
        add(dup_pe, dup_act, None)
        add(*attn_b)
        add(None, None, split_dve(H, False, ALL))
        split_tiles_of(H, False, ALL)
        add_gemm(out_plan(0, ALL), fresh=True)
        add_norm(ALL, "eps1", False, modulate(0, 1))
        for i, tiles in enumerate(mlp_plans(0, ALL)):
            add_gemm(tiles, fresh=i == 0)
        add_norm(ALL, "eps1", False, modulate(1, 0))
        add_gemm(c_plan(), fresh=True)
        add(*qk_norm_c)
        add(rope_c[0], None, rope_c[1])
        add(*attn_c)
        add(None, None, split_dve(H, False, LAT))
        split_tiles_of(H, False, LAT)
        add_gemm(out_plan(1, LAT), fresh=True)
        add_norm(LAT, "eps1", False, modulate(1, 1))
        for i, tiles in enumerate(mlp_plans(1, LAT)):
            add_gemm(tiles, fresh=i == 0)
        add(None, None, split_dve(X, True, LAT))
        split_tiles_of(X, True, LAT)
        for l in range(2):
            for i, tiles in enumerate(ffn_plans(l)):
                add_gemm(tiles, before=second_loads(l) if i == 0 else None, fresh=i == 0)
            add_norm(LAT, "eps2", True, layer_norm_affine("ln1", l))
            add_gemm(in_plan(l), fresh=True)
            add(sgu_pe, sgu_act, lambda e, l=l: sgu_dve(e, l))
            add(lambda e, l=l: gla_pe(e, l), lambda e, l=l: gla_act(e, l), lambda e, l=l: gla_dve(e, l))
            add(*gla_norm[l])
            add(*l2_qk)
            add(lambda e, l=l: rows_pe(e, l), lambda e, l=l: rows_act(e, l), lambda e, l=l: rows_dve(e, l))
            add(solve_pe, solve_act, solve_dve)
            add(rec_pe, rec_act, rec_dve)
            add(*gdn_norm[l])
            add(None, None, split_dve(H, True, LAT))
            split_tiles_of(H, True, LAT)
            add_gemm(mix_plan(), fresh=True)
            add_norm(LAT, "eps2", True, layer_norm_affine("ln2", l))
            for i, tiles in enumerate(ffn_plans(l)):
                add_gemm(tiles, fresh=i == 0)
            add_norm(LAT, "eps2", True, layer_norm_affine("ln3", l))

        block = ctx.enter_context(nc.Block())

        @block.tensor
        def _(pe):
            for pe_part, _, _ in stages:
                if pe_part:
                    pe_part(pe)
                end_stage(pe, "pe")

        @block.scalar
        def _(act):
            for _, act_part, _ in stages:
                if act_part:
                    act_part(act)
                end_stage(act, "act")

        @block.vector
        def _(dve):
            for _, _, dve_part in stages:
                if dve_part:
                    dve_part(dve)
                end_stage(dve, "dve")

        @block.gpsimd
        def _(pool):
            for kind, n in Splits.order:
                if kind == "slab":
                    slot = n % RING
                    pool.wait_ge(hi_ready.sem, n - RAW_SLABS + 1)
                    nc.gpsimd.tensor_tensor(ring_lo[:, slot, :, :], ring[:, slot, :, :], ring_hi[:, slot, :, :].bitcast(F32),
                                            ALU.subtract).then_inc(lo_ready.sem, 1)
                elif kind == "input":
                    src, x_hi, x_lo = split_inputs[n]
                    pool.wait_ge(xhi_ready.sem, n + 1)
                    nc.gpsimd.tensor_tensor(x_lo, src, x_hi.bitcast(F32), ALU.subtract).then_inc(xlo_ready.sem, 1)
                else:
                    solve_pool(pool, n)

        @block.sync
        def _(sp):
            sp.dma_start(vec[:], vec_d).then_inc(loaded.sem, 16)
            sp.dma_start(con[:], shared_d).then_inc(loaded.sem, 16)
            sp.dma_start(con2[:, 0:N_FIRST], first_d).then_inc(loaded.sem, 16)
            sp.dma_start(X[:], xT_d.rearrange("(k p) t -> p k t", p=P)).then_inc(loaded.sem, 16)
            for n in range(max(Splits.at, -(-Weights.at // SLAB))):
                if n >= RING:
                    used, count = Weights.used[n - RING]
                    sp.wait_ge(used.sem, count)
                sp.dma_start(ring[:, n % RING, :, :].rearrange("p a b -> p (a b)"), w_d[n]).then_inc(slab_loaded[n % RING].sem, 16)
            sp.wait_ge(stage.sem, 3 * len(stages))
            sp.dma_start(out_d.rearrange("(k p) t -> p k t", p=P), X[:, :, CTX:TOK]).then_inc(stored.sem, 16)
            sp.wait_ge(stored.sem, 16)


def kernel(**inputs):
    import concourse.bacc as bacc
    from concourse.bass_utils import run_bass_kernel_spmd as run

    a = {k: np.ascontiguousarray(v) for k, v in inputs.items()}

    def columns(v):
        return v.reshape(-1, P).T

    def rows(v, at):
        out = np.zeros((P, v.shape[0]), np.float32)
        out[at, :] = v.T
        return out

    gb = a["ab_gate_b"][0]
    gate_rows = np.r_[0:4, 32:36]
    packed = dict(
        c=columns(a["c"]), c_ctx=columns(a["c_ctx"]), ada_b=columns(a["ada_b"]), norm1_g=columns(a["norm1_g"]),
        norm2_g=columns(a["norm2_g"]), mlstm_g=columns(a["mlstm_norm_g"]), swa_q=columns(np.tile(a["swa_q_norm_g"][0], 2)),
        swa_k=columns(np.tile(a["swa_k_norm_g"][0], 2)), c_q=columns(a["c_q_norm_g"]), c_k=columns(a["c_k_norm_g"]),
        sink=np.broadcast_to(a["swa_sink"], (P, 8)), gb_i=rows(np.r_[gb[0:4], gb[8:12]][None], gate_rows),
        gb_f=rows(np.r_[gb[4:8], gb[12:16]][None], gate_rows), ln1_g=columns(a["ln1_g_2"]), ln1_b=columns(a["ln1_b_2"]),
        ln2_g=columns(a["ln2_g_2"]), ln2_b=columns(a["ln2_b_2"]), ln3_g=columns(a["ln3_g_2"]), ln3_b=columns(a["ln3_b_2"]),
        sgu_g=columns(a["sgu_ln_g_2"]), sgu_b=columns(a["sgu_ln_b_2"]), conv=columns(a["gdn_conv_w_2"]),
        a_log=rows(a["gdn_a_log_2"], np.arange(8)), dt_b=rows(a["gdn_dt_bias_2"], np.arange(8)),
        gdn_g=np.tile(a["gdn_norm_g_2"], (1, 2)).T, gla_gb=columns(a["gla_gate_b_2"]), gla_g=np.tile(a["gla_norm_g_2"], (1, 2)).T,
        eps1=np.full((P, 1), EPS1), eps2=np.full((P, 1), EPS2), epsl=np.full((P, 1), EPSL), one=np.ones((P, 1)))
    vec = np.concatenate([np.asarray(packed[n], np.float32) for n, _ in VECS], 1)
    assert vec.shape == (P, NVEC)

    def spread(w, pieces):
        out = np.zeros((w.shape[0], P), w.dtype)
        for c, n, at in pieces:
            out[:, at:at + n] = w[:, c:c + n]
        return out

    ab = a["ab_w_in"][0]
    mats = dict(ada0=a["ada_w"][0], ada1=a["ada_w"][1], ab=ab, gi=spread(ab, [(2048, 4, 0), (2056, 4, 32)]),
                gf=spread(ab, [(2052, 4, 0), (2060, 4, 32)]), abo=a["ab_w_out"][0], cw=a["c_w_in"][0], co=a["c_w_out"][0])
    for l in range(2):
        w = a["w_in_2"][l]
        mats.update({f"m1_{l}": a["mlp_w1"][l], f"m2_{l}": a["mlp_w2"][l], f"in{l}": w, f"be{l}": spread(w, [(2560, 8, 0)]),
                     f"de{l}": spread(w, [(2568, 8, 0)]), f"gl{l}": spread(w, [(3344, 16, 0)]), f"out{l}": a["w_out_2"][l],
                     f"f1_{l}": a["ffn1_w1_2"][l], f"f3_{l}": a["ffn1_w3_2"][l], f"f2_{l}": a["ffn1_w2_2"][l],
                     f"g1_{l}": a["ffn2_w1_2"][l], f"g3_{l}": a["ffn2_w3_2"][l], f"g2_{l}": a["ffn2_w2_2"][l]})
    w_all = np.zeros((N_SLABS, P, SLAB * P), np.float32)
    for i, (name, k, c, n) in enumerate(stream()):
        w_all[i // SLAB, :, (i % SLAB) * P:(i % SLAB) * P + P] = mats[name][k * P:k * P + P, c:c + P]

    shared, first, second = consts()
    arrays = dict(
        xT=np.concatenate([a["ctx"][0], a["x"][0]], 0).T, vec=vec, shared=shared, first=first, second=second,
        gup=a["gla_gate_up_2"], sguw=a["sgu_w_2"].transpose(0, 3, 1, 2), sgub=a["sgu_b_2"].reshape(2, 512), weights=w_all)
    nc = bacc.Bacc("TRN2", target_bir_lowering=False, num_devices=1)
    ins, args = {}, []
    for name, arr in arrays.items():
        arr = np.ascontiguousarray(arr)
        ins[name + "_dram"] = arr
        args.append(nc.dram_tensor(name + "_dram", arr.shape, F32, kind="ExternalInput").ap())
    out = nc.dram_tensor("out_dram", (D, SEQ), F32, kind="ExternalOutput").ap()
    program(nc, *args, out)
    got = run(nc, [ins], core_ids=[0]).results[0]["out_dram"]
    return np.ascontiguousarray(got.T)[None]
```

```python
from contextlib import ExitStack

import numpy as np

import concourse.bass as bass
from concourse import mybir

F32 = mybir.dt.float32
F32R = mybir.dt.float32r
ALU = mybir.AluOpType
ACT = mybir.ActivationFunctionType
AX = mybir.AxisListType.X

P = 128
D = 1024
KD = D // P
CTX = 256
SEQ = 512
TOK = CTX + SEQ
NT = TOK // P
NCT = CTX // P
NLT = SEQ // P
FF1 = 4 * D
FF2 = 2816
EPS1, EPS2, EPSL = 1e-6, 1e-5, 1e-6
ALPHA = 4.0 ** 0.25
NEG = -1e30
ALL = [(0, 384), (384, 768)]
LAT = [(256, 768)]
SLAB = 8
RING = 4
PARTS = (4, 2, 2)

VECS = [("c", 8), ("c_ctx", 8), ("ada_b", 96), ("norm1_g", 16), ("norm2_g", 16), ("mlstm_g", 4),
        ("swa_q", 1), ("swa_k", 1), ("c_q", 1), ("c_k", 1), ("sink", 8), ("gb_i", 1), ("gb_f", 1),
        ("ln1_g", 16), ("ln1_b", 16), ("ln2_g", 16), ("ln2_b", 16), ("ln3_g", 16), ("ln3_b", 16),
        ("sgu_g", 4), ("sgu_b", 4), ("conv", 96), ("a_log", 2), ("dt_b", 2), ("gdn_g", 2),
        ("gla_gb", 2), ("gla_g", 2), ("eps1", 1), ("eps2", 1), ("epsl", 1), ("one", 1)]
VOFF = {}
_o = 0
for _n, _w in VECS:
    VOFF[_n] = (_o, _w)
    _o += _w
NVEC = _o

SHARED = [("ident", 128), ("ones", 128), ("blk64", 128), ("neg_ge", 128), ("neg_le", 128)]
FIRST = [("rot64", 128), ("rot128", 128), ("dup0", 128), ("dup1", 128), ("self", 512), ("selb", 512),
         ("cos64", 512), ("sin64", 512), ("cos128", 512), ("sin128", 512)]
SECOND = [("pos_lt", 128), ("m_ge", 128), ("sel", 1024), ("selp", 512), ("m_gla", 128), ("bd_gla", 256),
          ("rs128", 512), ("rs64", 512), ("lev", 896), ("levt", 896)]


def offsets(names):
    at, out = 0, {}
    for name, cols in names:
        out[name] = at
        at += cols
    return out, at


SHARED_AT, N_SHARED = offsets(SHARED)
FIRST_AT, N_FIRST = offsets(FIRST)
SECOND_AT, N_SECOND = offsets(SECOND)


def consts():
    r, c = np.arange(P)[:, None], np.arange(P)[None, :]
    a = {}
    a["ident"] = (r == c)
    a["ones"] = np.ones((P, P))
    a["blk64"] = (r // 64 == c // 64)

    def rot(n):
        h = n // 2
        return np.where((c % n < h) & (r == c + h), -1.0, 0.0) + np.where((c % n >= h) & (r == c - h), 1.0, 0.0)

    a["rot64"], a["rot128"] = rot(64), rot(128)
    a["dup0"], a["dup1"] = (r == c % 64), (r == 64 + c % 64)
    a["neg_ge"] = np.where(c >= r, 0.0, NEG)
    a["neg_le"] = np.where(c <= r, 0.0, NEG)
    a["pos_lt"] = np.where(c < r, 0.0, -NEG)
    a["m_ge"] = (c >= r)
    for name, base, heads in (("self", 0, 4), ("selb", 32, 4), ("sel", 0, 8)):
        a[name] = np.concatenate([np.broadcast_to(r == base + h, (P, P)) for h in range(heads)], 1)
    a["selp"] = np.concatenate([(r == 2 * p + c // 64) for p in range(4)], 1)
    a["m_gla"] = (c >= r) & (c // 64 == r // 64)
    a["bd_gla"] = (r // 32 == np.arange(256)[None, :] // 64)
    t = np.arange(512)[None, :]
    a["rs128"] = np.broadcast_to(t % 128 != 0, (P, 512))
    a["rs64"] = np.broadcast_to(t % 64 != 0, (P, 512))
    lev = [((r // (2 * b) == c // (2 * b)) & (r % (2 * b) >= b) & (c % (2 * b) < b)) for b in (1, 2, 4, 8, 16, 32, 64)]
    a["lev"] = np.concatenate(lev, 1)
    a["levt"] = np.concatenate([m.T for m in lev], 1)
    a["cos64"], a["sin64"] = rope_tables(64)
    a["cos128"], a["sin128"] = rope_tables(128)
    return [np.concatenate([np.asarray(a[n], np.float32) for n, _ in group], 1) for group in (SHARED, FIRST, SECOND)]


def rope_tables(head_dim):
    t = np.arange(SEQ)
    row, col = (t // 64).astype(np.float32), (t % 64).astype(np.float32)
    pairs = head_dim // 4
    inv = (np.float32(10000.0) ** (-np.arange(pairs, dtype=np.float32) / np.float32(pairs))).astype(np.float32)
    ang = np.concatenate([inv[:, None] * row[None], inv[:, None] * col[None]], 0)
    reps = P // ang.shape[0]
    return np.tile(np.cos(ang), (reps, 1)).astype(np.float32), np.tile(np.sin(ang), (reps, 1)).astype(np.float32)


def ftiles(w, cols, kt=KD):
    return [(w, k, c, P) for c in range(cols[0], cols[1], P) for k in range(kt)]


def down_tiles(w, rows):
    return [(w, k, c, P) for c in range(0, D, P) for k in range(rows[0], rows[1])]


def mlp_stream(up, down, ff, parts):
    s, n = [], ff // P // parts
    for q in range(parts):
        for m in range(q * n, q * n + n):
            for w in up:
                s += ftiles(w, (m * P, m * P + P))
        s += down_tiles(down, (q * n, q * n + n))
    return s


def ttiles(w, cols, kt=KD):
    return [(w, k, c, P) for k in range(kt) for c in range(cols[0], cols[1], P)]


def stream():
    s = []
    for l in range(2):
        for c in range(0, 6144, 512):
            s += ttiles(f"ada{l}", (c, c + 512))
    s += ftiles("ab", (0, 1024)) + ftiles("ab", (1536, 2048)) + ftiles("ab", (2064, 2576)) + ftiles("ab", (2576, 2704))
    s += ftiles("gi", (0, P)) + ftiles("gf", (0, P))
    s += ttiles("ab", (1024, 1280)) + ttiles("ab", (1280, 1536)) + ttiles("ab", (2704, 2832))
    s += ftiles("abo", (0, D)) + mlp_stream(["m1_0"], "m2_0", FF1, PARTS[0])
    s += ftiles("cw", (0, 1280)) + ttiles("cw", (1280, 1536)) + ftiles("co", (0, D))
    s += mlp_stream(["m1_1"], "m2_1", FF1, PARTS[1])
    for l in range(2):
        for f in ("f", None, "g"):
            if f is None:
                w = f"in{l}"
                s += ftiles(w, (0, 512)) + ftiles(w, (512, 2048)) + ftiles(w, (2048, 2560))
                s += ftiles(f"be{l}", (0, P)) + ftiles(f"de{l}", (0, P))
                s += ftiles(w, (2576, 2832)) + ftiles(w, (3088, 3344)) + ftiles(f"gl{l}", (0, P))
                s += ttiles(w, (2832, 3088)) + ftiles(f"out{l}", (0, D))
            else:
                s += mlp_stream([f"{f}1_{l}", f"{f}3_{l}"], f"{f}2_{l}", FF2, PARTS[2])
    return s


N_SLABS = -(-len(stream()) // SLAB)
RAW_SLABS = 2 * 6144 * D // (P * P) // SLAB


class Signal:

    def __init__(self, sem):
        self.sem = sem
        self.seen = {}

    def at(self, who, k):
        return self.seen.get(who, 0) + k + 1

    def advance(self, who, n):
        self.seen[who] = self.seen.get(who, 0) + n

    def next(self, who, step=1):
        self.seen[who] = self.seen.get(who, 0) + step
        return self.seen[who]


class Out:

    def __init__(self, bank, ready, who, freed, reuse):
        self.bank, self.ready, self.who, self.freed, self.reuse = bank, ready, who, freed, reuse


class Banks:

    def __init__(self):
        self.n, self.done, self.user = 0, {"act": 0, "dve": 0}, [None] * 8
        self.first = 0

    def take(self, who):
        bank = self.first + self.n % (8 - self.first)
        self.n += 1
        self.done[who] += 1
        out = Out(bank, self.n, who, self.done[who], self.user[bank])
        self.user[bank] = (who, self.done[who])
        return out


def program(nc, xT_d, vec_d, shared_d, first_d, second_d, gup_d, sguw_d, sgub_d, w_d, out_d):
    with ExitStack() as ctx:
        def sb(name, cols):
            return ctx.enter_context(nc.sbuf_tensor(name, [P, cols], F32))

        def signal(name):
            return Signal(ctx.enter_context(nc.semaphore(name)))

        def with_rounded(name, shape):
            at = -(-nc.sbuf_base // 32) * 32
            return (ctx.enter_context(nc.sbuf_tensor(name, shape, F32)),
                    nc.alloc_sbuf_tensor_at(name + "_r", shape, F32R, offset=at))

        X = ctx.enter_context(nc.sbuf_tensor("X", [P, KD, TOK], F32))
        H, H_r = with_rounded("H", [P, KD, TOK])
        ring, ring_lo = with_rounded("ring", [P, RING, SLAB, P])
        ring_hi = ctx.enter_context(nc.sbuf_tensor("ring_hi", [P, RING, SLAB, P], F32R))
        ARENA = 24576
        arena, arena_r = with_rounded("arena", [P, ARENA])
        vec = sb("vec", NVEC)
        con = sb("con", N_SHARED)
        con2 = sb("con2", max(N_FIRST, N_SECOND))
        mods = ctx.enter_context(nc.sbuf_tensor("mods", [P, 2, 2, 48], F32))
        amul = ctx.enter_context(nc.sbuf_tensor("amul", [P, 2, 2, 2, 8], F32))
        cs = ctx.enter_context(nc.sbuf_tensor("cs", [P, 8, 2], F32))
        small = sb("small", 160)
        PS = ctx.enter_context(nc.psum_tensor("PS", [P, 8, 512], F32))

        def V(name, i=0, n=1):
            return vec[:, VOFF[name][0] + i:VOFF[name][0] + i + n]

        def C(name, i=0, n=P):
            if name in SHARED_AT:
                return con[:, SHARED_AT[name] + i:SHARED_AT[name] + i + n]
            at = FIRST_AT[name] if name in FIRST_AT else SECOND_AT[name]
            return con2[:, at + i:at + i + n]

        def area(at, *dims, of=arena):
            n = int(np.prod(dims))
            assert at + n <= ARENA, (at, n)
            a = of[:, at:at + n]
            if len(dims) == 2:
                return a.rearrange("p (a b) -> p a b", a=dims[0])
            if len(dims) == 3:
                return a.rearrange("p (a b c) -> p a b c", a=dims[0], b=dims[1])
            return a

        vec_loaded = signal("vectors_loaded")
        loaded = signal("inputs_loaded")
        rope_loaded = signal("rope_loaded")
        small_loaded = signal("sgu_loaded")
        slab_loaded = [signal(f"slab_loaded{i}") for i in range(RING)]
        slab_used = signal("slab_used")
        hi_ready = signal("slab_high_parts_ready")
        lo_ready = signal("slab_low_parts_ready")
        mm_done = signal("product_ready")
        evac = {"act": signal("evacuated_by_act"), "dve": signal("evacuated_by_dve")}
        stage = signal("stage_done")
        stored = signal("stored")
        act_step = signal("act_step")
        dve_step = signal("dve_step")
        silu_c = signal("silu_c_ready")
        ada_done = signal("ada_products_ready")
        sq_ready = signal("squares_ready")
        sum_ready = signal("sums_ready")
        std_ready = signal("std_ready")
        norm_ready = signal("normed_ready")
        mean_used = signal("mean_used")
        affine_done = signal("norm_scaled")
        xhi_ready = signal("input_high_parts_ready")
        xlo_ready = signal("input_low_parts_ready")
        hidden_ready = signal("hidden_low_parts_ready")
        tile_sq, tile_sq_used = signal("tile_squares_ready"), signal("tile_squares_used")

        def a_link(act, ins):
            ins.then_inc(act_step.sem, 1)
            act.wait_ge(act_step.sem, act_step.next("act"))

        def v_link(dve, ins):
            ins.then_inc(dve_step.sem, 1)
            dve.wait_ge(dve_step.sem, dve_step.next("dve"))

        def end_stage(eng, who):
            eng.drain().then_inc(stage.sem, 1)
            eng.wait_ge(stage.sem, stage.next(who, 3))

        class Weights:
            at = 0
            used = []

        def used_up(ins):
            ins.then_inc(slab_used.sem, 1)
            Weights.used.append((slab_used, slab_used.next("pe")))

        def high_part(out, src):
            return nc.vector.tensor_copy(out, src)

        def raw_tiles(pe, n):
            slab, pos = divmod(Weights.at, SLAB)
            assert pos + n <= SLAB
            if pos == 0:
                pe.wait_ge(slab_loaded[slab % RING].sem, 16 * (slab // RING + 1))
            Weights.at += n
            return ring[:, slab % RING, pos:pos + n, :], Weights.at % SLAB == 0

        def split_tiles(pe, n):
            slab, pos = divmod(Weights.at, SLAB)
            assert pos + n <= SLAB
            if pos == 0:
                pe.wait_ge(lo_ready.sem, slab - RAW_SLABS + 1)
            Weights.at += n
            return ring_hi[:, slab % RING, pos:pos + n, :], ring_lo[:, slab % RING, pos:pos + n, :], Weights.at % SLAB == 0

        class Splits:
            at = RAW_SLABS
            order = []
            inputs = 0

        def split_up_to(dve, slab):
            while Splits.at < min(slab, N_SLABS):
                n = Splits.at
                dve.wait_ge(slab_loaded[n % RING].sem, 16 * (n // RING + 1))
                high_part(ring_hi[:, n % RING, :, :], ring[:, n % RING, :, :]).then_inc(hi_ready.sem, 1)
                Splits.order.append(("slab", n))
                Splits.at += 1

        def row_sums_pe(pe, t):
            for i, (o, (lo, hi)) in enumerate(zip(t["outs"], t["segs"])):
                flags = dict(start=(t["m"] == 0), stop=(t["m"] == KD - 1))
                if t["sums"] == "mean":
                    pe.wait_ge(evac["dve"].sem, o.freed)
                    pe.matmul(PS[:, 1, 0:hi - lo], C("ones"), X[:, t["m"], lo:hi], **flags)
                else:
                    pe.wait_ge(tile_sq.sem, tile_sq.next("pe"))
                    pe.matmul(PS[:, i, 0:hi - lo], C("ones"), sq_buf(t, i)[:, 0:hi - lo], **flags).then_inc(tile_sq_used.sem, 1)

        def sq_buf(t, i):
            return area(16384 + 512 * ((t["m"] * len(t["segs"]) + i) % 4), 512)

        def squares_act(act, t):
            for i, (o, (lo, hi)) in enumerate(zip(t["outs"], t["segs"])):
                j = t["m"] * len(t["segs"]) + i
                act.wait_ge(evac["dve"].sem, o.freed)
                if j >= 4:
                    act.wait_ge(tile_sq_used.sem, tile_sq_used.at("act", j - 4))
                nc.scalar.activation(sq_buf(t, i)[:, 0:hi - lo], X[:, t["m"], lo:hi], ACT.Square).then_inc(tile_sq.sem, 1)
            if t["m"] == KD - 1:
                tile_sq_used.advance("act", KD * len(t["segs"]))

        def gemm_pe(pe, tiles):
            for i, t in enumerate(tiles + [{}, {}]):
                if i >= 2 and "sums" in tiles[i - 2]:
                    row_sums_pe(pe, tiles[i - 2])
                if i >= len(tiles):
                    continue
                for o in t["outs"]:
                    if o.reuse:
                        pe.wait_ge(evac[o.reuse[0]].sem, o.reuse[1])
                kt = t["kt"]
                for k in range(kt):
                    if "input_ready" in t:
                        pe.wait_ge(t["input_ready"][0].sem, t["input_ready"][1][k])
                    w_hi, w_lo, last_of_slab = split_tiles(pe, t["n"])
                    for o, (lo, hi) in zip(t["outs"], t["segs"]):
                        x_hi, x_lo = t["rhs"](k, lo, hi)
                        for j, (w, x) in enumerate(((w_hi, x_hi), (w_hi, x_lo), (w_lo, x_hi))):
                            flags = dict(start=(k == 0 and j == 0), stop=(k == kt - 1 and j == 2))
                            if t["mode"] == "F":
                                ins = pe.matmul(PS[:, o.bank, 0:hi - lo], w[:, 0, :], x, **flags)
                            else:
                                ins = pe.matmul(PS[:, o.bank, 0:t["n"] * P], x, w.rearrange("p a b -> p (a b)"), **flags)
                        if k == kt - 1:
                            ins.then_inc(mm_done.sem, 1)
                    if last_of_slab:
                        if k == kt - 1:
                            Weights.used.append((mm_done, t["outs"][-1].ready))
                        else:
                            used_up(ins)

        def gemm_evac(eng, who, tiles):
            for i, t in enumerate(tiles + [dict(late=None), dict(late=None)]):
                if who == "act" and i >= 2 and tiles[i - 2]["late"]:
                    tiles[i - 2]["late"](eng)
                if i >= len(tiles):
                    continue
                if who == "act" and t.get("sums") == "squares":
                    squares_act(eng, t)
                if who == "dve":
                    split_up_to(eng, t["last_slab"] + 3)
                for o, (lo, hi) in zip(t["outs"], t["segs"]):
                    if o.who == who:
                        eng.wait_ge(mm_done.sem, o.ready)
                        width = hi - lo if t["mode"] == "F" else t["n"] * P
                        t["ev"](eng, PS[:, o.bank, 0:width], lo, hi).then_inc(evac[who].sem, 1)
                    if who == "dve" and t["post"]:
                        t["post"](eng, o, lo, hi)

        banks = Banks()

        class Planned:
            at = RAW_SLABS * SLAB

        def planned(n):
            Planned.at += n
            return (Planned.at - 1) // SLAB

        def ftile(rhs, segs, who, ev, kt=KD, post=None, late=None):
            return dict(mode="F", n=1, kt=kt, segs=segs, rhs=rhs, ev=ev, post=post, late=late, outs=[banks.take(who) for _ in segs],
                        last_slab=planned(kt))

        def ttile(rhs, toks, n, who, ev):
            return dict(mode="T", n=n, kt=KD, segs=[(P * t, P * t + P) for t in toks], rhs=rhs, ev=ev, post=None, late=None,
                        outs=[banks.take(who) for _ in toks], last_slab=planned(KD * n))

        XHI = area(18432, KD, TOK, of=arena_r)
        XHI2 = area(20480, KD, SEQ, of=arena_r)

        def x_h(k, lo, hi):
            return XHI[:, k, lo:hi], H_r[:, k, lo:hi]

        def x_x(k, lo, hi):
            return XHI2[:, k, lo - CTX:hi - CTX], H_r[:, k, lo:hi]

        def xhi(second, k, lo, hi):
            return XHI2[:, k, lo - CTX:hi - CTX] if second else XHI[:, k, lo:hi]

        split_inputs = []

        class Fresh:
            need = []

        def split_tiles_of(src, second, segs, by_rows):
            tiles = [(k, lo, hi) for lo, hi in segs for k in range(KD)]
            if by_rows:
                tiles.sort(key=lambda x: x[0])
            Fresh.need = [0] * KD
            for k, lo, hi in tiles:
                split_inputs.append((src[:, k, lo:hi], xhi(second, k, lo, hi), H_r[:, k, lo:hi]))
                Fresh.need[k] = len(split_inputs)

        def split_dve(src, second, segs):
            def fn(dve):
                for k in range(KD):
                    for lo, hi in segs:
                        high_part(xhi(second, k, lo, hi), src[:, k, lo:hi]).then_inc(xhi_ready.sem, 1)
                        Splits.order.append(("input", Splits.inputs))
                        Splits.inputs += 1
            return fn

        def copy_act(dst, scale=1.0):
            def ev(eng, ps, lo, hi):
                return nc.scalar.activation(dst(lo, hi), ps, ACT.Copy, scale=scale)
            return ev

        def func_act(dst, func):
            def ev(eng, ps, lo, hi):
                return nc.scalar.activation(dst(lo, hi), ps, func)
            return ev

        def copy_dve(dst):
            def ev(eng, ps, lo, hi):
                return nc.vector.tensor_copy(dst(lo, hi), ps)
            return ev

        def streams(lo, hi):
            return [(s, max(lo, a), min(hi, b)) for s, a, b in ((1, 0, CTX), (0, CTX, TOK)) if max(lo, a) < min(hi, b)]

        rstd = sb("rstd", 512)
        mean = sb("mean", 512)

        def root(i, summed):
            return mean if i == 1 and summed else rstd

        def norm_act(act, segs, eps, centred, affine, summed):
            def log(i):
                lo, hi = segs[i]
                sums = PS[:, i if summed else 0, 0:hi - lo]
                return nc.scalar.activation(root(i, summed)[:, 0:hi - lo], sums, ACT.Ln, bias=V(eps), scale=1.0 / D)

            def power(i):
                r = root(i, summed)[:, 0:segs[i][1] - segs[i][0]]
                nc.scalar.activation(r, r, ACT.Exp, scale=-0.5).then_inc(std_ready.sem, 1)

            if summed:
                for i in range(len(segs)):
                    ins = log(i)
                a_link(act, ins)
                for i in range(len(segs)):
                    power(i)
            for i, (lo, hi) in enumerate(segs):
                if not summed:
                    for k in range(KD):
                        if centred:
                            act.wait_ge(mean_used.sem, mean_used.next("act"))
                        nc.scalar.activation(tmp_sq[:, k, lo:hi], (H if centred else X)[:, k, lo:hi], ACT.Square).then_inc(sq_ready.sem, 1)
                    nc.scalar.activation(small[:, 159:160], V("one"), ACT.Ln)
                    act.wait_ge(sum_ready.sem, sum_ready.next("act"))
                    a_link(act, log(i))
                    power(i)
                for k in range(KD):
                    act.wait_ge(norm_ready.sem, norm_ready.next("act"))
                    affine(act, k, lo, hi).then_inc(affine_done.sem, 1)

        def norm_pe(pe, segs, centred):
            for lo, hi in segs:
                for k in range(KD):
                    pe.wait_ge(sq_ready.sem, sq_ready.next("pe"))
                    ins = pe.matmul(PS[:, 0, 0:hi - lo], C("ones"), tmp_sq[:, k, lo:hi], start=(k == 0), stop=(k == KD - 1))
                ins.then_inc(sum_ready.sem, 1)

        def norm_dve(dve, segs, centred, summed):
            for i, (lo, hi) in enumerate(segs):
                src = X
                if centred:
                    v_link(dve, nc.vector.tensor_scalar(mean[:, 0:hi - lo], PS[:, 1, 0:hi - lo], 1.0 / D, None, ALU.mult))
                    for k in range(KD):
                        nc.vector.tensor_tensor(H[:, k, lo:hi], X[:, k, lo:hi], mean[:, 0:hi - lo], ALU.subtract).then_inc(mean_used.sem, 1)
                    src = H
                dve.wait_ge(std_ready.sem, std_ready.next("dve"))
                for k in range(KD):
                    nc.vector.tensor_tensor(H[:, k, lo:hi], src[:, k, lo:hi], root(i, summed)[:, 0:hi - lo],
                                            ALU.mult).then_inc(norm_ready.sem, 1)
                for k in range(KD):
                    dve.wait_ge(affine_done.sem, affine_done.next("dve"))
                    high_part(xhi(centred, k, lo, hi), (X if centred else H)[:, k, lo:hi]).then_inc(xhi_ready.sem, 1)
                    Splits.order.append(("input", Splits.inputs))
                    Splits.inputs += 1

        tmp_sq = area(0, KD, TOK)

        def modulate(l, n):
            def affine(act, k, lo, hi):
                for s, a, b in streams(lo, hi):
                    ins = nc.scalar.activation(H[:, k, a:b], H[:, k, a:b], ACT.Identity,
                                               bias=mods[:, l, s, 24 * n + k:24 * n + k + 1], scale=amul[:, l, s, n, k:k + 1])
                return ins
            return affine

        def layer_norm_affine(name, l):
            def affine(act, k, lo, hi):
                return nc.scalar.activation(X[:, k, lo:hi], H[:, k, lo:hi], ACT.Identity, bias=V(name + "_b", 8 * l + k),
                                            scale=V(name + "_g", 8 * l + k))
            return affine

        ada_out, ada_row = signal("ada_rows_ready"), signal("ada_rows_copied")
        ada_rows = area(0, 2, 6144)

        def ada_act(act):
            act.dma_start(con[:], shared_d).then_inc(loaded.sem, 16)
            act.dma_start(con2[:, 0:N_FIRST], first_d).then_inc(loaded.sem, 16)
            act.dma_start(X[:], xT_d.rearrange("(k p) t -> p k t", p=P)).then_inc(loaded.sem, 16)
            act.wait_ge(vec_loaded.sem, 16)
            nc.scalar.activation(cs[:, :, 0], V("c", 0, 8), ACT.Silu)
            nc.scalar.activation(cs[:, :, 1], V("c_ctx", 0, 8), ACT.Silu).then_inc(silu_c.sem, 1)
            for i in range(24):
                act.wait_ge(ada_out.sem, i + 1)
                nc.scalar.activation(ada_rows[0:2, i // 12, 512 * (i % 12):512 * (i % 12) + 512], PS[0:2, 2 + i % 6, :],
                                     ACT.Copy).then_inc(ada_row.sem, 1)

        def ada_pe(pe):
            pe.wait_ge(silu_c.sem, 1)
            for i in range(24):
                if i >= 6:
                    pe.wait_ge(ada_row.sem, i - 5)
                for k in range(KD):
                    w, last_of_slab = raw_tiles(pe, 4)
                    ins = pe.matmul(PS[0:2, 2 + i % 6, :], cs[:, k, :], w.rearrange("p a b -> p (a b)"), start=(k == 0), stop=(k == KD - 1))
                    if last_of_slab:
                        if k == KD - 1:
                            ins.then_inc(ada_out.sem, 1)
                            Weights.used.append((ada_out, i + 1))
                        else:
                            used_up(ins)
            pe.wait_ge(loaded.sem, 48)
            for l in range(2):
                pe.wait_ge(ada_row.sem, 12 * l + 12)
                for m in range(48):
                    ins = pe.transpose(PS[:, l, 2 * m:2 * m + 2], ada_rows[0:2, l, P * m:P * m + P], C("ident")[0:2, 0:2])
            ins.then_inc(ada_done.sem, 1)

        def ada_dve(dve):
            dve.wait_ge(vec_loaded.sem, 16)
            dve.wait_ge(loaded.sem, 48)
            dve.wait_ge(ada_done.sem, 1)
            for l in range(2):
                for s in range(2):
                    v_link(dve, nc.vector.tensor_tensor(mods[:, l, s, :], PS[:, l, 0:96].rearrange("p (m s) -> p m s", s=2)[:, :, s],
                                                        V("ada_b", 48 * l, 48), ALU.add))
                    for n in range(2):
                        g = V("norm1_g" if n == 0 else "norm2_g", 8 * l, 8)
                        nc.vector.scalar_tensor_tensor(out=amul[:, l, s, n, :], in0=mods[:, l, s, 24 * n + 8:24 * n + 16],
                                                       scalar=1.0, in1=g, op0=ALU.add, op1=ALU.mult)

        hn_sq, hn_sum = signal("head_squares_ready"), signal("head_sums_ready")
        hn_std, hn_done = signal("head_std_ready"), signal("head_normed")
        HSQ, HRS = 4, 8

        def head_norm(items, at):
            sq = [area(at + 512 * i, 512) for i in range(HSQ)]
            rs = [area(at + 512 * (HSQ + i), 512) for i in range(HRS)]
            per = -(-len(items) // -(-len(items) // HRS))

            def width(it):
                return it[0].shape[-1]

            def act_fn(act):
                for g in range(0, len(items), per):
                    group = range(g, min(g + per, len(items)))
                    for i in group:
                        if i >= HSQ:
                            act.wait_ge(hn_sum.sem, hn_sum.at("act", i - HSQ))
                        nc.scalar.activation(sq[i % HSQ][:, 0:width(items[i])], items[i][0], ACT.Square).then_inc(hn_sq.sem, 1)
                    for i in group:
                        act.wait_ge(hn_sum.sem, hn_sum.at("act", i))
                        if i >= HRS:
                            act.wait_ge(hn_done.sem, hn_done.at("act", i - HRS))
                        it = items[i]
                        ins = nc.scalar.activation(rs[i % HRS][:, 0:width(it)], PS[:, i % 8, 0:width(it)], ACT.Ln, bias=V(it[4]), scale=it[3])
                    a_link(act, ins)
                    for i in group:
                        r = rs[i % HRS][:, 0:width(items[i])]
                        nc.scalar.activation(r, r, ACT.Exp, scale=-0.5).then_inc(hn_std.sem, 1)
                hn_sum.advance("act", len(items))
                hn_done.advance("act", len(items))

            def pe_fn(pe):
                for i, it in enumerate(items):
                    pe.wait_ge(hn_sq.sem, hn_sq.at("pe", i))
                    if i >= 8:
                        pe.wait_ge(hn_std.sem, hn_std.at("pe", i - 8))
                    pe.matmul(PS[:, i % 8, 0:width(it)], C(it[2]), sq[i % HSQ][:, 0:width(it)], start=True, stop=True).then_inc(hn_sum.sem, 1)
                hn_sq.advance("pe", len(items))
                hn_std.advance("pe", len(items))

            def dve_fn(dve):
                for i, (src, dst, _, _, _, gain, extra) in enumerate(items):
                    r = rs[i % HRS][:, 0:src.shape[-1]]
                    dve.wait_ge(hn_std.sem, hn_std.at("dve", i))
                    ins = nc.vector.scalar_tensor_tensor(out=dst, in0=src, scalar=gain, in1=r, op0=ALU.mult, op1=ALU.mult)
                    if extra is not None:
                        v_link(dve, ins)
                        ins = nc.vector.tensor_tensor(dst, dst, extra, ALU.mult)
                    ins.then_inc(hn_done.sem, 1)
                hn_std.advance("dve", len(items))

            return pe_fn, act_fn, dve_fn

        rope_rot, rope_used = signal("rotated_ready"), signal("rotated_used")

        def rope(tiles, d, at):
            def pe_fn(pe):
                for i, t in enumerate(tiles):
                    if i >= 4:
                        pe.wait_ge(rope_used.sem, rope_used.at("pe", i - 4))
                    pe.matmul(PS[:, i % 4, :], C(f"rot{d}"), t, start=True, stop=True).then_inc(rope_rot.sem, 1)
                rope_used.advance("pe", len(tiles))

            def dve_fn(dve):
                for i, t in enumerate(tiles):
                    tmp = area(at + 512 * (i % 2), 512)
                    dve.wait_ge(rope_rot.sem, rope_rot.at("dve", i))
                    nc.vector.tensor_tensor(tmp, PS[:, i % 4, :], C(f"sin{d}", 0, 512), ALU.mult)
                    v_link(dve, nc.vector.tensor_tensor(t, t, C(f"cos{d}", 0, 512), ALU.mult))
                    nc.vector.tensor_tensor(t, t, tmp, ALU.add).then_inc(rope_used.sem, 1)
                rope_rot.advance("dve", len(tiles))

            return pe_fn, dve_fn

        at_s, at_nb, at_p = signal("scores_ready"), signal("minus_max_ready"), signal("exp_ready")
        at_n, at_t, at_tc = signal("probs_normed"), signal("probs_turned"), signal("turned_probs_copied")
        at_o, at_oc = signal("head_outputs_ready"), signal("head_outputs_copied")

        def attention(groups, scale, p_at, pt_at):
            units = [(g, j) for g in groups for j in range(4)]
            probs = [area(p_at + 768 * i, 768) for i in range(3)]
            turned = [area(pt_at + 3072 * i, 6, 512) for i in range(2)]
            n = len(units)

            def nk(g):
                return CTX + (g["lat"][1] - g["lat"][0] if g["lat"] else 0)

            def s_all(i, g):
                return PS[:, 2 * (i % 2):2 * (i % 2) + 2, :].rearrange("p a b -> p (a b)")[:, 256:256 + nk(g)]

            def key_tiles(g):
                return list(range(NCT)) + (list(range(g["lat"][0] // P, g["lat"][1] // P)) if g["lat"] else [])

            def col(i, what):
                return small[:, 8 * what + i % 8:8 * what + i % 8 + 1]

            def pe_fn(pe):
                for i in range(n + 3):
                    if i < n:
                        g, j = units[i]
                        if i >= 2:
                            pe.wait_ge(at_p.sem, at_p.at("pe", i - 2))
                        ins = pe.matmul(PS[:, 2 * (i % 2), 256:512], g["q"][j], g["k"][j][:, 0:CTX], start=True, stop=True)
                        if g["lat"]:
                            lo, hi = g["lat"]
                            ins = pe.matmul(PS[:, 2 * (i % 2) + 1, 0:hi - lo], g["q"][j], g["k"][j][:, lo:hi], start=True, stop=True)
                        ins.then_inc(at_s.sem, 1)
                    if i >= 3 and (i - 3) % 4 == 3:
                        gi, g = (i - 3) // 4, units[i - 3][0]
                        kts = key_tiles(g)
                        pe.wait_ge(at_tc.sem, at_tc.at("pe", i - 3))
                        if gi >= 2:
                            pe.wait_ge(at_oc.sem, at_oc.at("pe", gi - 2))
                        for t, kt in enumerate(kts):
                            ins = pe.matmul(PS[0:g["m"], 6 + gi % 2, :], g["v"](kt), turned[gi % 2][:, t, :],
                                            start=(t == 0), stop=(t == len(kts) - 1))
                        ins.then_inc(at_o.sem, 1)
                    if 2 <= i < n + 2:
                        u = i - 2
                        g, j = units[u]
                        kts = key_tiles(g)
                        pe.wait_ge(at_n.sem, at_n.at("pe", u))
                        if u >= 1:
                            pe.wait_ge(at_tc.sem, at_tc.at("pe", u - 1))
                        for t in range(len(kts)):
                            ins = pe.transpose(PS[:, 4 + t // 4, (t % 4) * P:(t % 4) * P + P], probs[u % 3][:, t * P:t * P + P], C("ident"))
                        ins.then_inc(at_t.sem, 1)
                for s_, c_ in ((at_p, n), (at_n, n), (at_tc, n), (at_oc, len(groups))):
                    s_.advance("pe", c_)

            def dve_fn(dve):
                for i in range(n + 1):
                    if i < n:
                        g, j = units[i]
                        dve.wait_ge(at_s.sem, at_s.at("dve", i))
                        for c_, mask in g["masks"]:
                            s_c = s_all(i, g)[:, c_:c_ + P]
                            ins = nc.vector.tensor_tensor(s_c, s_c, C(mask), ALU.add)
                        if g["masks"]:
                            v_link(dve, ins)
                        v_link(dve, nc.vector.tensor_reduce(col(i, 0), s_all(i, g), AX, ALU.max))
                        if g["sinks"]:
                            v_link(dve, nc.vector.tensor_scalar(col(i, 1), col(i, 0), scale, g["sinks"][j], ALU.mult, ALU.max))
                            ins = nc.vector.tensor_scalar(col(i, 2), col(i, 1), -1.0, None, ALU.mult)
                        else:
                            ins = nc.vector.tensor_scalar(col(i, 2), col(i, 0), -scale, None, ALU.mult)
                        ins.then_inc(at_nb.sem, 1)
                    if i >= 1:
                        u = i - 1
                        g, j = units[u]
                        dve.wait_ge(at_p.sem, at_p.at("dve", u))
                        if g["sinks"]:
                            v_link(dve, nc.vector.tensor_tensor(col(u, 3), col(u, 3), col(u, 4), ALU.add))
                        v_link(dve, nc.vector.reciprocal(col(u, 5), col(u, 3)))
                        nc.vector.tensor_scalar(probs[u % 3][:, 0:nk(g)], probs[u % 3][:, 0:nk(g)], col(u, 5), None,
                                                ALU.mult).then_inc(at_n.sem, 1)
                at_s.advance("dve", n)
                at_p.advance("dve", n)

            def act_fn(act):
                for i in range(n + 4):
                    if i < n:
                        g, j = units[i]
                        act.wait_ge(at_nb.sem, at_nb.at("act", i))
                        if i >= 3:
                            act.wait_ge(at_t.sem, at_t.at("act", i - 3))
                        if g["sinks"]:
                            nc.scalar.activation(col(i, 4), g["sinks"][j], ACT.Exp, bias=col(i, 2))
                        nc.scalar.activation(probs[i % 3][:, 0:nk(g)], s_all(i, g), ACT.Exp, bias=col(i, 2), scale=scale,
                                             accum_out=col(i, 3)).then_inc(at_p.sem, 1)
                    if 2 <= i < n + 2:
                        u = i - 2
                        g, j = units[u]
                        gi = u // 4
                        act.wait_ge(at_t.sem, at_t.at("act", u))
                        if j == 0 and gi >= 2:
                            act.wait_ge(at_o.sem, at_o.at("act", gi - 2))
                        kt = len(key_tiles(g))
                        src = PS[:, 4:6, :].rearrange("p a b -> p (a b)")[:, 0:kt * P].rearrange("p (a b) -> p a b", a=kt)
                        nc.scalar.activation(turned[gi % 2][:, 0:kt, j * P:j * P + P], src, ACT.Copy).then_inc(at_tc.sem, 1)
                    if i >= 4 and (i - 4) % 4 == 3:
                        gi, g = (i - 4) // 4, units[i - 4][0]
                        act.wait_ge(at_o.sem, at_o.at("act", gi))
                        g["put"](PS[0:g["m"], 6 + gi % 2, :].rearrange("p (h q) -> p h q", h=4)).then_inc(at_oc.sem, 1)
                at_nb.advance("act", n)
                at_t.advance("act", n)
                at_o.advance("act", len(groups))

            return pe_fn, act_fn, dve_fn

        qa, ka, oa, qb = (area(3072 * i, 4, TOK) for i in range(4))
        kb, gi, gf = area(12288, TOK), area(13056, TOK), area(13824, TOK)
        va = area(14592, 6, 512)
        vb = area(17664, 6, P)

        def to(dst):
            return lambda lo, hi: dst[:, lo:hi]

        def ab_plan():
            t = [ftile(x_h, ALL, "act", copy_act(to(qa[:, m, :]))) for m in range(4)]
            t += [ftile(x_h, ALL, "act", copy_act(to(ka[:, m, :]), P ** -0.5)) for m in range(4)]
            t += [ftile(x_h, ALL, "act", func_act(to(oa[:, m, :]), ACT.Sigmoid)) for m in range(4)]
            t += [ftile(x_h, ALL, "dve", copy_dve(to(qb[:, m, :]))) for m in range(4)]
            t += [ftile(x_h, ALL, "dve", copy_dve(to(d))) for d in (kb, gi, gf)]
            for half in range(2):
                t.append(ttile(x_h, range(NT), 2, "act",
                               copy_act(lambda lo, hi, half=half: va[:, lo // P, 256 * half:256 * half + 256])))
            t.append(ttile(x_h, range(NT), 1, "dve", copy_dve(lambda lo, hi: vb[:, lo // P, :])))
            return t

        def residual(l, gate, m):
            def ev(eng, ps, lo, hi):
                for s, a, b in streams(lo, hi):
                    ins = nc.vector.scalar_tensor_tensor(out=X[:, m, a:b], in0=ps[:, a - lo:b - lo],
                                                         scalar=mods[:, l, s, gate + m:gate + m + 1],
                                                         in1=X[:, m, a:b], op0=ALU.mult, op1=ALU.add)
                return ins
            return ev

        def out_plan(l, segs):
            banks.first = 2
            tiles = with_sums([ftile(x_h, segs, "dve", residual(l, 16, m)) for m in range(KD)], "squares")
            banks.first = 0
            return tiles

        def split_hidden(h_hi, h, h_lo):
            def post(dve, o, lo, hi):
                dve.wait_ge(evac[o.who].sem, o.freed)
                v_link(dve, high_part(h_hi(lo, hi), h(lo, hi)))
                nc.vector.tensor_tensor(h_lo(lo, hi), h(lo, hi), h_hi(lo, hi).bitcast(F32), ALU.subtract).then_inc(hidden_ready.sem, 1)
            return post

        class Hidden:
            at = 0

        def down_tiles(tiles, n_segs, n):
            tiles[0]["input_ready"] = (hidden_ready, [Hidden.at + n_segs * (k + 1) for k in range(n)])
            Hidden.at += n_segs * n
            return tiles

        def with_sums(tiles, kind):
            for m, t in enumerate(tiles):
                t["sums"], t["m"] = kind, m
            return tiles

        def mlp_plans(l, segs):
            n = FF1 // P // PARTS[l]
            w = segs[-1][1] - segs[0][0]
            off = segs[0][0]
            h_hi, h, h_lo = area(0, n, w, of=arena_r), area(n * w, n, w), area(n * w, n, w, of=arena_r)

            def relu_sq(m):
                def ev(eng, ps, lo, hi):
                    d = h[:, m, lo - off:hi - off]
                    a_link(eng, nc.scalar.activation(d, ps, ACT.Relu))
                    return nc.scalar.activation(d, d, ACT.Square)
                return ev

            out = []
            banks.first = 2
            for q in range(PARTS[l]):
                out += ([ftile(x_h, segs, "act", relu_sq(m), post=split_hidden(*(
                    lambda lo, hi, m=m, part=part: part[:, m, lo - off:hi - off] for part in (h_hi, h, h_lo)))) for m in range(n)])
                down = ([ftile(lambda k, lo, hi: (h_hi[:, k, lo - off:hi - off], h_lo[:, k, lo - off:hi - off]), segs, "dve",
                               residual(l, 40, m), kt=n) for m in range(KD)])
                out += down_tiles(with_sums(down, "squares") if l == 0 and q == PARTS[l] - 1 else down, len(segs), n)
            banks.first = 0
            return out

        F_, g_ = gf[0:64, :], gi[0:64, :]
        G_, EM, T1, T2 = (H[0:64, 4 + i, :] for i in range(4))
        gt = small[:, 0:48].rearrange("p (t d h) -> p t d h", t=6, d=2)
        gt_ready, gate_rows, gate_act, gate_abs = (signal(n) for n in ("gates_turned", "gate_rows_ready", "gate_logs_ready", "gate_args_ready"))

        def gates_act(act):
            a_link(act, nc.scalar.activation(F_, F_, ACT.Identity, bias=V("gb_f")[0:64]))
            nc.scalar.activation(g_, g_, ACT.Identity, bias=V("gb_i")[0:64])
            a_link(act, nc.scalar.activation(T1, F_, ACT.Abs))
            a_link(act, nc.scalar.activation(T1, T1, ACT.Exp, scale=-1.0))
            nc.scalar.activation(T1, T1, ACT.Ln, bias=V("one")[0:64]).then_inc(gate_act.sem, 1)
            act.wait_ge(gate_abs.sem, 1)
            nc.scalar.activation(EM, EM, ACT.Exp, scale=-1.0).then_inc(gate_act.sem, 1)
            act.wait_ge(gt_ready.sem, 1)
            nc.scalar.activation(gt, PS[:, 0, 0:384].rearrange("p (t d h) -> p t d h", t=6, d=2)[:, :, :, 0:4], ACT.Copy)

        def gates_dve(dve):
            v_link(dve, nc.vector.memset(T2, 0.0))
            dve.wait_ge(gate_act.sem, 1)
            v_link(dve, nc.vector.scalar_tensor_tensor(out=T1, in0=F_, scalar=0.0, in1=T1, op0=ALU.min, op1=ALU.subtract))

            def scan(dst, src, other, op, start):
                v_link(dve, nc.vector.tensor_tensor_scan(dst[0:32, :], src[0:32, :], other[0:32, :], start, op, op))
                v_link(dve, nc.vector.tensor_tensor_scan(dst[32:64, 0:CTX][:, ::-1], src[32:64, 0:CTX][:, ::-1],
                                                         other[32:64, 0:CTX][:, ::-1], start, op, op))
                v_link(dve, nc.vector.tensor_tensor_scan(dst[32:64, CTX:TOK][:, ::-1], src[32:64, CTX:TOK][:, ::-1],
                                                         other[32:64, CTX:TOK][:, ::-1], dst[32:64, 0:1], op, op))

            scan(F_, T1, T2, ALU.add, 0.0)
            nc.vector.tensor_tensor(g_, g_, F_, ALU.subtract).then_inc(gate_rows.sem, 1)
            dve.wait_ge(gate_rows.sem, 1)
            scan(G_, g_, g_, ALU.max, 0.0)
            nc.vector.tensor_tensor(EM, F_, G_, ALU.add).then_inc(gate_abs.sem, 1)

        def gates_pe(pe):
            pe.wait_ge(gate_rows.sem, 1)
            for t in range(NT):
                ins = pe.transpose(PS[:, 0, 64 * t:64 * t + 64], gi[0:64, P * t:P * t + P], C("ident")[0:64, 0:64])
            ins.then_inc(gt_ready.sem, 1)

        W_ = area(18432, 2, 6, 512)
        PASSES = [(h, seg) for h in range(4) for seg in ((0, CTX), (CTX, TOK))]

        def reach(d, s, lo, hi):
            if s * P < lo:
                return 0, hi - lo, None
            q = s * P - lo
            return (q, hi - lo, q) if d == 0 else (0, q + P, q)

        ml_g, ml_diag, ml_e = signal("row_max_spread"), signal("diagonal_args_ready"), signal("decays_ready")
        ml_s, ml_w = signal("mlstm_scores_ready"), signal("weighted_scores_ready")
        ml_em, ml_nd, ml_abs, ml_h = (signal(n) for n in ("exp_minus_m_spread", "num_den_ready", "abs_den_ready", "mlstm_head_done"))
        DG = [H[:, 6, 0:768], H[:, 7, 0:512]]

        def diag_buf(d, s):
            return H[:, 6 + d, P * s:P * s + P]

        ml_max = signal("mlstm_floor_applied")

        def mlstm_pe(pe):
            for i, (h, (lo, hi)) in enumerate(PASSES):
                w, ns, base = hi - lo, hi // P, ml_s.seen.get("pe", 0)

                def scores(s):
                    if base + s >= 2:
                        pe.wait_ge(ml_w.sem, base + s - 1)
                    pe.matmul(PS[:, 2 + (base + s) % 2, 0:w], ka[:, h, P * s:P * s + P], qa[:, h, lo:hi],
                              start=True, stop=True).then_inc(ml_s.sem, 1)

                def products(d, order, s):
                    a, b, _ = reach(d, s, lo, hi)
                    flags = dict(start=(s == order[0]), stop=(s == order[-1]))
                    pe.matmul(PS[:, 4 + 2 * d, a:b], va[:, s, P * h:P * h + P], W_[:, d, s, a:b], **flags)
                    return pe.matmul(PS[:, 5 + 2 * d, a:b], C("ones"), W_[:, d, s, a:b], **flags)

                for s in range(2):
                    scores(s)
                if i >= 1:
                    pe.wait_ge(ml_max.sem, i)
                for d, sel in enumerate(("self", "selb")):
                    ins = pe.matmul(PS[:, d, 0:w], C(sel, P * h)[0:64], G_[:, lo:hi], start=True, stop=True)
                ins.then_inc(ml_g.sem, 1)
                if i >= 1:
                    pe.wait_ge(ml_h.sem, i)
                for s in range(ns):
                    pe.wait_ge(ml_w.sem, base + s + 1)
                    if s + 2 < ns:
                        scores(s + 2)
                    ins = products(0, range(ns), s)
                ins.then_inc(ml_nd.sem, 1)
                pe.wait_ge(ml_e.sem, ml_e.next("pe", ns))
                for d, sel in enumerate(("self", "selb")):
                    ins = pe.matmul(PS[:, d, 0:w], C(sel, P * h)[0:64], EM[:, lo:hi], start=True, stop=True)
                ins.then_inc(ml_em.sem, 1)
                order = list(range(ns))
                if lo == 0:
                    order.reverse()
                for s in order:
                    ins = products(1, order, s)
                ins.then_inc(ml_nd.sem, 1)
                ml_s.advance("pe", ns)

        def mlstm_act(act):
            for i, (h, (lo, hi)) in enumerate(PASSES):
                act.wait_ge(ml_g.sem, i + 1)
                act.wait_ge(ml_diag.sem, i + 1)
                if i >= 1:
                    act.wait_ge(ml_nd.sem, 2 * i)
                for s in range(hi // P):
                    for d in range(2):
                        a, b, q = reach(d, s, lo, hi)
                        bias = gt[:, s, d, h:h + 1]
                        if q is not None:
                            ins = nc.scalar.activation(W_[:, d, s, q:q + P], diag_buf(d, s), ACT.Exp, bias=bias)
                            a, b = (q + P, b) if d == 0 else (a, q)
                        if b > a:
                            ins = nc.scalar.activation(W_[:, d, s, a:b], PS[:, d, a:b], ACT.Exp, bias=bias, scale=-1.0)
                    ins.then_inc(ml_e.sem, 1)
                for d in range(2):
                    act.wait_ge(ml_nd.sem, 2 * i + d + 1)
                    nc.scalar.activation((rstd, mean)[d][:, 0:hi - lo], PS[:, 5 + 2 * d, 0:hi - lo], ACT.Abs).then_inc(ml_abs.sem, 1)

        def mlstm_dve(dve):
            def diagonals(i):
                dve.wait_ge(ml_g.sem, i + 1)
                lo, hi = PASSES[i][1]
                for s in range(lo // P, hi // P):
                    for d, mask in enumerate(("neg_ge", "neg_le")):
                        q = s * P - lo
                        ins = nc.vector.scalar_tensor_tensor(out=diag_buf(d, s), in0=PS[:, d, q:q + P], scalar=-1.0, in1=C(mask),
                                                             op0=ALU.mult, op1=ALU.add)
                ins.then_inc(ml_diag.sem, 1)

            n_s = 0
            diagonals(0)
            for i, (h, (lo, hi)) in enumerate(PASSES):
                w = hi - lo
                for s in range(hi // P):
                    n_s += 1
                    dve.wait_ge(ml_e.sem, n_s)
                    dve.wait_ge(ml_s.sem, n_s)
                    for d in range(2):
                        a, b, _ = reach(d, s, lo, hi)
                        ins = nc.vector.tensor_tensor(W_[:, d, s, a:b], W_[:, d, s, a:b], PS[:, 2 + (n_s - 1) % 2, a:b], ALU.mult)
                    ins.then_inc(ml_w.sem, 1)
                dve.wait_ge(ml_em.sem, i + 1)
                r = [rstd[:, 0:w], mean[:, 0:w]]
                for d in range(2):
                    dve.wait_ge(ml_abs.sem, 2 * i + d + 1)
                    ins = nc.vector.tensor_tensor(r[d], r[d], PS[:, d, 0:w], ALU.max)
                ins.then_inc(ml_max.sem, 1)
                dve.wait_ge(ml_max.sem, i + 1)
                ins = nc.vector.reciprocal(r[0], r[0])
                if i + 1 < len(PASSES):
                    v_link(dve, ins)
                    diagonals(i + 1)
                v_link(dve, nc.vector.reciprocal(r[1], r[1]))
                nc.vector.tensor_tensor(H[:, h, lo:hi], r[0], PS[:, 4, 0:w], ALU.mult)
                v_link(dve, nc.vector.tensor_tensor(r[1], r[1], PS[:, 6, 0:w], ALU.mult))
                nc.vector.tensor_tensor(H[:, h, lo:hi], H[:, h, lo:hi], r[1], ALU.add).then_inc(ml_h.sem, 1)

        mlstm_out = head_norm([(H[:, h, a:b], H[:, h, a:b], "ones", 1.0 / P, "eps1", V("mlstm_g", h), oa[:, h, a:b])
                               for h in range(4) for a, b in ALL], 18432)
        qk_norm_b = head_norm([(qb[:, m, a:b], qb[:, m, a:b], "blk64", 1.0 / 64, "eps1", V("swa_q"), None)
                               for m in range(4) for a, b in ALL]
                              + [(kb[:, a:b], kb[:, a:b], "blk64", 1.0 / 64, "eps1", V("swa_k"), None) for a, b in ALL], 18432)
        rope_b = rope([qb[:, m, CTX:TOK] for m in range(4)] + [kb[:, CTX:TOK]], 64, 18432)
        kd = area(0, 2, TOK)
        dup_ready = signal("keys_doubled")

        def dup_pe(pe):
            for n in range(2):
                for j, (a, b) in enumerate(ALL):
                    ins = pe.matmul(PS[:, 2 * n + j, 0:b - a], C(f"dup{n}"), kb[:, a:b], start=True, stop=True)
            ins.then_inc(dup_ready.sem, 1)

        def dup_act(act):
            act.wait_ge(dup_ready.sem, 1)
            for n in range(2):
                for j, (a, b) in enumerate(ALL):
                    nc.scalar.activation(kd[:, n, a:b], PS[:, 2 * n + j, 0:b - a], ACT.Copy)

        def b_groups():
            out = []
            for blk in range(NT):
                if blk < NCT:
                    lat, masks = None, []
                else:
                    a, b = max(blk - 1, NCT), min(blk + 2, NT)
                    lat = (a * P, b * P)
                    masks = [(CTX + (t - a) * P, m) for t, m in ((blk - 1, "neg_ge"), (blk + 1, "neg_le")) if a <= t < b]
                for kv in range(2):
                    heads = [4 * kv + j for j in range(4)]
                    half = [64 * (h % 2) for h in heads]

                    def put(ps, kv=kv, blk=blk):
                        for par in range(2):
                            ins = nc.scalar.activation(H[64 * par:64 * par + 64, 4 + 2 * kv:6 + 2 * kv, blk * P:blk * P + P],
                                                       ps[:, par::2, :], ACT.Copy)
                        return ins

                    out.append(dict(q=[qb[o:o + 64, h // 2, blk * P:blk * P + P] for h, o in zip(heads, half)],
                                    k=[kd[o:o + 64, kv, :] for o in half], v=lambda kt, kv=kv: vb[:, kt, 64 * kv:64 * kv + 64],
                                    lat=lat, masks=masks, sinks=[V("sink", h) for h in heads], put=put, m=64))
            return out

        attn_b = attention(b_groups(), 64 ** -0.5, 3072, 18432)

        qc = area(0, 8, 512)
        kc = area(4096, 2, TOK)
        vc = area(5632, 6, 256)

        def c_plan():
            t = [ftile(x_h, LAT, "act", copy_act(to_lat(qc[:, m, :]))) for m in range(8)]
            t += [ftile(x_h, ALL, "dve", copy_dve(to(kc[:, m, :]))) for m in range(2)]
            t.append(ttile(x_h, range(NT), 2, "act", copy_act(lambda lo, hi: vc[:, lo // P, :])))
            return t

        def to_lat(dst):
            return lambda lo, hi: dst[:, lo - CTX:hi - CTX]

        qk_norm_c = head_norm([(qc[:, m, :], qc[:, m, :], "ones", 1.0 / P, "eps1", V("c_q"), None) for m in range(8)]
                              + [(kc[:, m, a:b], kc[:, m, a:b], "ones", 1.0 / P, "eps1", V("c_k"), None) for m in range(2) for a, b in ALL], 18432)
        rope_c = rope([qc[:, m, :] for m in range(8)] + [kc[:, m, CTX:TOK] for m in range(2)], 128, 18432)

        def c_groups():
            out = []
            for blk in range(NLT):
                for kv in range(2):
                    def put(ps, kv=kv, blk=blk):
                        return nc.scalar.activation(H[:, 4 * kv:4 * kv + 4, CTX + blk * P:CTX + blk * P + P], ps, ACT.Copy)
                    out.append(dict(q=[qc[:, 4 * kv + j, blk * P:blk * P + P] for j in range(4)], k=[kc[:, kv, :]] * 4,
                                    v=lambda kt, kv=kv: vc[:, kt, P * kv:P * kv + P], lat=(CTX, TOK), masks=[], sinks=None, put=put, m=P))
            return out

        attn_c = attention(c_groups(), P ** -0.5, 7168, 9472)

        up_, vp_ = area(0, 2, 512), area(1024, 2, 512)
        qkv = area(2048, 12, 512)
        zp = area(8192, 4, 512)
        be, de = area(10240, 512), area(10752, 512)
        qg, kg = area(11264, 512), area(11776, 512)
        rg = area(12288, 2, 512)
        gl = area(13312, 512)
        vg = area(13824, 4, 256)
        ktok, vtok = area(14848, 4, 512), area(16896, 4, 512)
        SC = 14848
        XL = X[:, :, CTX:TOK]
        Y = H[:, :, CTX:TOK]

        def ffn_plans(l):
            n = FF2 // P // PARTS[2]
            h_hi, h, h_lo = area(0, n, SEQ, of=arena_r), area(n * SEQ, n, SEQ), area(n * SEQ, n, SEQ, of=arena_r)
            out = []
            banks.first = 2
            for q in range(PARTS[2]):
                up = []
                for m in range(n):
                    a = ftile(x_x, LAT, "act", lambda eng, ps, lo, hi, m=m: nc.scalar.activation(h[:, m, :], ps, ACT.Silu))

                    def times(eng, ps, lo, hi, m=m, gate_out=a["outs"][0]):
                        eng.wait_ge(evac["act"].sem, gate_out.freed)
                        return nc.vector.tensor_tensor(h[:, m, :], h[:, m, :], ps, ALU.mult)

                    up += [a, ftile(x_x, LAT, "dve", times, post=split_hidden(*(
                        lambda lo, hi, m=m, part=part: part[:, m, :] for part in (h_hi, h, h_lo))))]

                def half_add(m, first):
                    def ev(eng, ps, lo, hi):
                        if first:
                            v_link(eng, nc.vector.tensor_scalar(X[:, m, lo:hi], X[:, m, lo:hi], ALPHA, None, ALU.mult))
                        return nc.vector.scalar_tensor_tensor(out=X[:, m, lo:hi], in0=ps, scalar=0.5, in1=X[:, m, lo:hi],
                                                              op0=ALU.mult, op1=ALU.add)
                    return ev

                down = [ftile(lambda k, lo, hi: (h_hi[:, k, :], h_lo[:, k, :]), LAT, "dve", half_add(m, q == 0), kt=n)
                        for m in range(KD)]
                out += up + down_tiles(with_sums(down, "mean") if q == PARTS[2] - 1 else down, 1, n)
            banks.first = 0
            return out

        cv, cv_done = signal("convolved"), signal("silu_of_conv_done")

        def conv_dve(l, t):
            y, x = area(SC + 2048 + 512 * (t % 4), 512), qkv[:, t, :]
            tap = [V("conv", 48 * l + 12 * i + t) for i in range(4)]

            def post(dve, o, lo, hi):
                dve.wait_ge(evac[o.who].sem, o.freed)
                if t >= 4:
                    dve.wait_ge(cv_done.sem, 12 * l + t - 3)
                v_link(dve, nc.vector.tensor_scalar(y, x, tap[3], None, ALU.mult))
                for back in range(1, 4):
                    ins = nc.vector.scalar_tensor_tensor(out=y[:, back:], in0=x[:, 0:512 - back], scalar=tap[3 - back], in1=y[:, back:],
                                                         op0=ALU.mult, op1=ALU.add)
                    if back < 3:
                        v_link(dve, ins)
                ins.then_inc(cv.sem, 1)
            return post

        def conv_act(t):
            def late(act):
                act.wait_ge(cv.sem, cv.next("act"))
                nc.scalar.activation(qkv[:, t, :], area(SC + 2048 + 512 * (t % 4), 512), ACT.Silu).then_inc(cv_done.sem, 1)
            return late

        def in_plan(l):
            dsts = [up_[:, 0, :], up_[:, 1, :], vp_[:, 0, :], vp_[:, 1, :]] + [qkv[:, m, :] for m in range(12)] \
                + [zp[:, m, :] for m in range(4)] + [be, de, qg, kg, rg[:, 0, :], rg[:, 1, :], gl]
            t = []
            for i, d in enumerate(dsts):
                if i < 4:
                    t.append(ftile(x_x, LAT, "act", func_act(to_lat(d), ACT.Gelu_apprx_tanh)))
                elif i < 16:
                    t.append(ftile(x_x, LAT, "act", copy_act(to_lat(d)), post=conv_dve(l, i - 4), late=conv_act(i - 4)))
                elif i < 20 or i in (24, 25):
                    t.append(ftile(x_x, LAT, "act", func_act(to_lat(d), ACT.Silu)))
                else:
                    t.append(ftile(x_x, LAT, "dve", copy_dve(to_lat(d))))
            t.append(ttile(x_x, range(NCT, NT), 2, "act", copy_act(lambda lo, hi: vg[:, lo // P - NCT, :])))
            return t

        def mix_plan():
            def ev_for(m):
                def ev(eng, ps, lo, hi):
                    v_link(eng, nc.vector.tensor_scalar(X[:, m, lo:hi], X[:, m, lo:hi], ALPHA, None, ALU.mult))
                    return nc.vector.tensor_tensor(X[:, m, lo:hi], X[:, m, lo:hi], ps, ALU.add)
                return ev
            banks.first = 2
            tiles = with_sums([ftile(x_x, LAT, "dve", ev_for(m)) for m in range(KD)], "mean")
            banks.first = 0
            return tiles

        sg_mean, sg_sq, sg_std, sg_v, sg_t, sg_tc, sg_z, sg_w = (signal(n) for n in (
            "sgu_centred", "sgu_squares", "sgu_std", "sgu_v_normed", "sgu_v_turned", "sgu_v_token_major", "sgu_mixed", "sgu_w_masked"))
        wsT = area(SC, 4, P)
        bs_row = area(SC + 512, 512)
        gup = area(SC + 1024, P)
        vt = area(SC + 1536, 4, 256)
        sq2 = area(SC + 2560, 2, 512)

        def sgu_act(act):
            act.wait_ge(sg_mean.sem, sg_mean.next("act"))
            for t in range(2):
                ins = nc.scalar.activation(sq2[:, t, :], vp_[:, t, :], ACT.Square)
            ins.then_inc(sg_sq.sem, 1)
            act.wait_ge(sg_t.sem, sg_t.next("act"))
            a_link(act, nc.scalar.activation(rstd[:], PS[:, 1, :], ACT.Ln, bias=V("eps2"), scale=1.0 / 256))
            nc.scalar.activation(rstd[:], rstd[:], ACT.Exp, scale=-0.5).then_inc(sg_std.sem, 1)
            act.wait_ge(sg_t.sem, sg_t.next("act"))
            nc.scalar.activation(vt[:, 0:2, :], PS[:, 2, :].rearrange("p (a b) -> p a b", a=2), ACT.Copy)
            nc.scalar.activation(vt[:, 2:4, :], PS[:, 3, :].rearrange("p (a b) -> p a b", a=2), ACT.Copy).then_inc(sg_tc.sem, 1)

        def sgu_pe(pe):
            for t in range(2):
                ins = pe.matmul(PS[:, 0, :], C("ones"), vp_[:, t, :], start=(t == 0), stop=(t == 1))
            ins.then_inc(sg_z.sem, 1)
            pe.wait_ge(sg_sq.sem, sg_sq.next("pe"))
            for t in range(2):
                ins = pe.matmul(PS[:, 1, :], C("ones"), sq2[:, t, :], start=(t == 0), stop=(t == 1))
            ins.then_inc(sg_t.sem, 1)
            pe.wait_ge(sg_v.sem, sg_v.next("pe"))
            for n in range(NLT):
                for t in range(2):
                    ins = pe.transpose(PS[:, 2 + n // 2, 256 * (n % 2) + P * t:256 * (n % 2) + P * t + P],
                                       vp_[:, t, P * n:P * n + P], C("ident"))
            ins.then_inc(sg_t.sem, 1)
            pe.wait_ge(sg_tc.sem, sg_tc.next("pe"))
            pe.wait_ge(sg_w.sem, sg_w.next("pe"))
            for h in range(4):
                o = 64 * (h % 2)
                for n in range(NLT):
                    dst = PS[o:o + 64, 4 + h // 2, P * n:P * n + P]
                    pe.matmul(dst, vt[:, n, 64 * h:64 * h + 64], wsT[:, h, :], start=True, stop=False)
                    ins = pe.matmul(dst, C("ones")[0:1, 0:64], bs_row[0:1, P * h:P * h + P], start=False, stop=True)
            ins.then_inc(sg_z.sem, 1)

        def sgu_dve(dve, l):
            dve.wait_ge(small_loaded.sem, 64 + 48 * l)
            nc.vector.tensor_tensor(wsT, wsT, C("m_ge").unsqueeze(1).to_broadcast([P, 4, P]), ALU.mult).then_inc(sg_w.sem, 1)
            dve.wait_ge(sg_z.sem, sg_z.next("dve"))
            v_link(dve, nc.vector.tensor_scalar(mean[:], PS[:, 0, :], 1.0 / 256, None, ALU.mult))
            for t in range(2):
                ins = nc.vector.tensor_tensor(vp_[:, t, :], vp_[:, t, :], mean[:], ALU.subtract)
            ins.then_inc(sg_mean.sem, 1)
            dve.wait_ge(sg_mean.sem, sg_mean.next("dve"))
            dve.wait_ge(sg_std.sem, sg_std.next("dve"))
            for t in range(2):
                v_link(dve, nc.vector.tensor_tensor(vp_[:, t, :], vp_[:, t, :], rstd[:], ALU.mult))
                ins = nc.vector.tensor_scalar(vp_[:, t, :], vp_[:, t, :], V("sgu_g", 2 * l + t), V("sgu_b", 2 * l + t), ALU.mult, ALU.add)
            ins.then_inc(sg_v.sem, 1)
            dve.wait_ge(sg_z.sem, sg_z.next("dve"))
            for t in range(2):
                nc.vector.tensor_tensor(Y[:, t, :], up_[:, t, :], PS[:, 4 + t, :], ALU.mult)

        bc, qd_, kx, kdec = (area(SC + 2048 + 512 * i, 512) for i in range(4))
        kdt = area(SC + 4096, 4, P)
        pTg = area(SC + 4608, 4, 512)
        Sg = area(SC + 6656, 9, 256)
        blocks = area(0, 256)
        gtg = small[:, 48:56]
        (ga_low, ga_arg, ga_log, ga_cum, ga_exp, ga_prod, ga_kt, ga_ktc, ga_s, ga_pt, ga_st, ga_state, ga_o) = (signal(n) for n in (
            "gla_gate_product", "gla_gate_arg", "gla_gate_log", "gla_decay_sums", "gla_decays", "gla_decayed_qk", "gla_k_turned",
            "gla_k_token_major", "gla_scores", "gla_scores_masked", "gla_updates", "gla_states", "gla_outputs"))

        GS = (0, 1, 6, 7)

        def update_bank(c):
            return PS[:, 2 + 2 * (c % 2) + c // 4, 256 * (c // 2 % 2):256 * (c // 2 % 2) + 256]

        def gla_act(act, l):
            act.wait_ge(ga_low.sem, ga_low.next("act"))
            a_link(act, nc.scalar.activation(bc, PS[:, 0, :], ACT.Identity, bias=V("gla_gb", l)))
            a_link(act, nc.scalar.activation(qd_, bc, ACT.Abs))
            a_link(act, nc.scalar.activation(qd_, qd_, ACT.Exp, scale=-1.0))
            nc.scalar.activation(qd_, qd_, ACT.Ln, bias=V("one")).then_inc(ga_log.sem, 1)
            act.wait_ge(ga_cum.sem, ga_cum.next("act"))
            nc.scalar.activation(qd_, bc, ACT.Exp)
            nc.scalar.activation(gtg, bc.rearrange("p (c t) -> p c t", t=64)[:, :, 63], ACT.Exp)
            nc.scalar.activation(kx, bc, ACT.Exp, scale=-1.0)
            nc.scalar.activation(kdec, kdec, ACT.Exp).then_inc(ga_exp.sem, 1)
            act.wait_ge(ga_kt.sem, ga_kt.next("act"))
            nc.scalar.activation(kdt, PS[:, 1, :].rearrange("p (a b) -> p a b", a=4), ACT.Copy).then_inc(ga_ktc.sem, 1)

        def gla_dve(dve, l):
            dve.wait_ge(ga_log.sem, ga_log.next("dve"))
            v_link(dve, nc.vector.scalar_tensor_tensor(out=bc, in0=bc, scalar=0.0, in1=qd_, op0=ALU.min, op1=ALU.subtract))
            v_link(dve, nc.vector.tensor_scalar(kx, bc, 1.0 / 16.0, None, ALU.mult))
            v_link(dve, nc.vector.tensor_tensor_scan(bc, C("rs64", 0, 512), kx, 0.0, ALU.mult, ALU.add))
            b3 = bc.rearrange("p (c t) -> p c t", t=64)
            nc.vector.tensor_tensor(kdec.rearrange("p (c t) -> p c t", t=64), b3[:, :, 63:64].to_broadcast([P, 8, 64]), b3,
                                    ALU.subtract).then_inc(ga_cum.sem, 1)
            dve.wait_ge(ga_exp.sem, ga_exp.next("dve"))
            nc.vector.scalar_tensor_tensor(out=qd_, in0=qg, scalar=32 ** -0.5, in1=qd_, op0=ALU.mult, op1=ALU.mult)
            nc.vector.tensor_tensor(kx, kx, kg, ALU.mult)
            nc.vector.tensor_tensor(kdec, kdec, kg, ALU.mult).then_inc(ga_prod.sem, 1)
            v_link(dve, nc.vector.memset(Sg[:, 0, :], 0.0))
            dve.wait_ge(ga_st.sem, ga_st.next("dve"))
            for c in range(7):
                nc.vector.tensor_scalar(Sg[:, c + 1, :], Sg[:, c, :], gtg[:, c:c + 1], None, ALU.mult)
                v_link(dve, nc.vector.tensor_tensor(blocks, update_bank(c), C("bd_gla", 0, 256), ALU.mult))
                v_link(dve, nc.vector.tensor_tensor(Sg[:, c + 1, :], Sg[:, c + 1, :], blocks, ALU.add))
            for h in range(4):
                dve.wait_ge(ga_s.sem, ga_s.next("dve"))
                nc.vector.tensor_tensor(pTg[:, :, P * h:P * h + P], PS[:, GS[h], :].rearrange("p (n t) -> p n t", n=4),
                                        C("m_gla").unsqueeze(1).to_broadcast([P, 4, P]), ALU.mult).then_inc(ga_pt.sem, 1)
            dve.wait_ge(ga_o.sem, ga_o.next("dve"))
            for p in range(2):
                nc.vector.tensor_copy(Y[:, 6 + p, :], PS[:, 6 + p, :])

        def gla_pe(pe, l):
            pe.wait_ge(small_loaded.sem, 64 + 48 * l)
            pe.matmul(PS[:, 0, :], gup[0:16, :], gl[0:16, :], start=True, stop=True).then_inc(ga_low.sem, 1)
            pe.wait_ge(ga_prod.sem, ga_prod.next("pe"))
            for n in range(NLT):
                ins = pe.transpose(PS[:, 1, P * n:P * n + P], kdec[:, P * n:P * n + P], C("ident"))
            ins.then_inc(ga_kt.sem, 1)
            pe.wait_ge(ga_ktc.sem, ga_ktc.next("pe"))
            for c in range(7):
                o, n = 64 * (c % 2), c // 2
                ins = pe.matmul(update_bank(c), kdt[o:o + 64, n, :], vg[o:o + 64, n, :], start=True, stop=True)
            ins.then_inc(ga_st.sem, 1)
            for h in range(4):
                for n in range(NLT):
                    a, b = 32 * h, P * n
                    ins = pe.matmul(PS[:, GS[h], b:b + P], kx[a:a + 32, b:b + P], qd_[a:a + 32, b:b + P], start=True, stop=True)
                ins.then_inc(ga_s.sem, 1)
            pe.wait_ge(ga_pt.sem, ga_pt.next("pe", 4))
            for n in range(NLT):
                for p in range(2):
                    for j in range(2):
                        h = 2 * p + j
                        pe.matmul(PS[64 * j:64 * j + 64, 6 + p, P * n:P * n + P], vg[:, n, 64 * h:64 * h + 64],
                                  pTg[:, n, P * h:P * h + P], start=True, stop=False, skip_group_check=True)
                    for c in (2 * n, 2 * n + 1):
                        ins = pe.matmul(PS[:, 6 + p, 64 * c:64 * c + 64], Sg[:, c, P * p:P * p + P], qd_[:, 64 * c:64 * c + 64],
                                        start=False, stop=True, skip_group_check=True)
            ins.then_inc(ga_o.sem, 1)

        gla_norm = [head_norm([(Y[:, 6 + p, :], Y[:, 6 + p, :], "blk64", 1.0 / 64, "eps2", V("gla_g", l), rg[:, p, :]) for p in range(2)], SC)
                    for l in range(2)]

        l2_qk = head_norm([(qkv[:, t, :], qkv[:, t, :], "blk64", 1.0, "epsl", 0.125 if t < 4 else 1.0, None) for t in range(8)], SC)
        R4 = area(18944, 512)
        R4T = area(19456, 4, P)
        bk = area(19968, 4, 512)
        wT = area(22016, 4, 512)
        ub = area(6144, 4, 512)
        (gr_exp, gr_rows, gr_r4, gr_t, gr_tc, gr_kv) = (signal(n) for n in (
            "gdn_gate_exps", "gdn_row_args", "gdn_rows", "gdn_rows_turned", "gdn_rows_token_major", "gdn_kv_turned"))

        def rows_act(act, l):
            r = de[0:8]
            s0, s1 = rstd[0:8, :], mean[0:8, :]
            a_link(act, nc.scalar.activation(r, r, ACT.Identity, bias=V("dt_b", l)[0:8]))
            a_link(act, nc.scalar.activation(s0, r, ACT.Abs))
            a_link(act, nc.scalar.activation(s0, s0, ACT.Exp, scale=-1.0))
            nc.scalar.activation(s0, s0, ACT.Ln, bias=V("one")[0:8])
            nc.scalar.activation(small[0:8, 56:57], V("a_log", l)[0:8], ACT.Exp).then_inc(gr_exp.sem, 1)
            act.wait_ge(gr_rows.sem, gr_rows.next("act"))
            nc.scalar.activation(R4[0:8, :], be[0:8, :], ACT.Sigmoid)
            nc.scalar.activation(R4[32:40, :], r, ACT.Copy)
            nc.scalar.activation(R4[64:72, :], s1, ACT.Exp)
            nc.scalar.activation(R4[96:104, :], r, ACT.Exp).then_inc(gr_r4.sem, 1)
            act.wait_ge(gr_t.sem, gr_t.next("act"))
            nc.scalar.activation(R4T, PS[:, 0, :].rearrange("p (a b) -> p a b", a=4), ACT.Copy).then_inc(gr_tc.sem, 1)

        def rows_dve(dve, l):
            r = de[0:8]
            s0, s1 = rstd[0:8, :], mean[0:8, :]
            v_link(dve, nc.vector.memset(R4, 0.0))
            dve.wait_ge(gr_exp.sem, gr_exp.next("dve"))
            v_link(dve, nc.vector.scalar_tensor_tensor(out=s0, in0=r, scalar=0.0, in1=s0, op0=ALU.max, op1=ALU.add))
            v_link(dve, nc.vector.tensor_scalar(s0, s0, small[0:8, 56:57], -1.0, ALU.mult, ALU.mult))
            v_link(dve, nc.vector.tensor_tensor_scan(r, C("rs128", 0, 512)[0:8], s0, 0.0, ALU.mult, ALU.add))
            r3 = r.rearrange("p (c t) -> p c t", t=P)
            nc.vector.tensor_tensor(s1.rearrange("p (c t) -> p c t", t=P), r3[:, :, P - 1:P].to_broadcast([8, 4, P]), r3,
                                    ALU.subtract).then_inc(gr_rows.sem, 1)
            dve.wait_ge(gr_tc.sem, gr_tc.next("dve"))
            v_link(dve, nc.vector.tensor_tensor(R4T[:, :, 96:104], R4T[:, :, 96:104], R4T[:, :, 0:8], ALU.mult))
            for i in range(8):
                n = i % 4

                def heads(t):
                    return t.rearrange("p (h d) -> p h d", h=8)

                def per_head(c):
                    return R4T[:, n, c:c + 8].unsqueeze(2).to_broadcast([P, 8, 64])

                dve.wait_ge(gr_kv.sem, gr_kv.next("dve"))
                src = heads(PS[:, (i + 1) % 8, :])
                if i < 4:
                    nc.vector.tensor_tensor(heads(bk[:, n, :]), src, per_head(96), ALU.mult)
                    nc.vector.tensor_tensor(heads(ktok[:, n, :]), src, per_head(64), ALU.mult)
                else:
                    nc.vector.tensor_tensor(heads(vtok[:, n, :]), src, per_head(0), ALU.mult)

        def rows_pe(pe, l):
            def turn(i):
                n = i % 4
                for p in range(4):
                    ins = pe.transpose(PS[:, (i + 1) % 8, P * p:P * p + P], qkv[:, 4 + 4 * (i // 4) + p, P * n:P * n + P], C("ident"))
                ins.then_inc(gr_kv.sem, 1)

            for i in range(7):
                turn(i)
            pe.wait_ge(gr_r4.sem, gr_r4.next("pe"))
            for n in range(4):
                ins = pe.transpose(PS[:, 0, P * n:P * n + P], R4[:, P * n:P * n + P], C("ident"))
            ins.then_inc(gr_t.sem, 1)
            pe.wait_ge(gr_tc.sem, gr_tc.next("pe"))
            turn(7)

        class Block4:

            def __init__(self, view):
                self.all = view

            def chunk(self, n):
                return self.all[:, n // 2, P * (n % 2):P * (n % 2) + P]

            @property
            def blocks(self):
                return self.all.rearrange("p a (b c) -> p a b c", c=P)

        def each(name, i=0):
            return C(name, i).unsqueeze(1).unsqueeze(1).to_broadcast([P, 2, 2, P])

        def pair(view512):
            return Block4(view512.rearrange("p (a b) -> p a b", a=2))

        sets = [[pair(area(11264 + 512 * i, 512)) for i in range(7)],
                [Block4(H[:, 2 * i:2 * i + 2, 0:CTX]) for i in range(4)] + [Block4(X[:, 2 * i:2 * i + 2, 0:CTX]) for i in range(3)]]

        def pt_of(h):
            return pair(area(512 * h, 512)) if h < 4 else pair(H[:, h - 2, CTX:TOK])

        (so_in, so_arg, so_dec, so_L, so_t, so_tc, so_lb, so_y, so_yc, so_x, so_xn, so_out, so_oc) = (signal(n) for n in (
            "solve_inputs", "solve_decay_args", "solve_decays", "solve_L", "solve_L_turned", "solve_LT", "solve_level_masked",
            "solve_y", "solve_y_copied", "solve_products", "solve_inverse_updated", "solve_outputs", "solve_outputs_copied"))
        LEVELS = 7

        def bank(sidx, i):
            return PS[:, 4 * sidx + i, :]

        def half(h):
            return slice(64 * (h % 2), 64 * (h % 2) + 64)

        def solve_pe(pe):
            def squares(hp, s):
                for n in range(4):
                    kk = qkv[half(2 * hp + s), 4 + hp, P * n:P * n + P]
                    pe.matmul(bank(s, 1)[:, P * n:P * n + P], kk, kk, start=True, stop=True)
                for n in range(4):
                    pe.matmul(bank(s, 2)[:, P * n:P * n + P], qkv[half(2 * hp + s), 4 + hp, P * n:P * n + P],
                              qkv[half(2 * hp + s), hp, P * n:P * n + P], start=True, stop=True)

            for hp in range(4):
                for s in range(2):
                    if hp == 0:
                        squares(hp, s)
                    else:
                        pe.wait_ge(so_oc.sem, so_oc.next("pe"))
                    pe.matmul(bank(s, 0), C("sel", P * (2 * hp + s))[0:8], de[0:8, :], start=True, stop=True).then_inc(so_in.sem, 1)
                for s in range(2):
                    L = sets[s][1]
                    pe.wait_ge(so_L.sem, so_L.next("pe"))
                    for n in range(4):
                        ins = pe.transpose(bank(s, 3)[:, P * n:P * n + P], L.chunk(n), C("ident"))
                    ins.then_inc(so_t.sem, 1)
                for lv in range(1, LEVELS):
                    for s in range(2):
                        _, _, LT, Xi, XT, Yb, Lb = sets[s]
                        Lb = sets[s][6 if lv % 2 else 0]
                        pe.wait_ge(so_lb.sem, so_lb.next("pe"))
                        pe.wait_ge(so_xn.sem, so_xn.next("pe"))
                        for n in range(4):
                            ins = pe.matmul(bank(s, 0)[:, P * n:P * n + P], Lb.chunk(n), Xi.chunk(n), start=True, stop=True)
                        ins.then_inc(so_y.sem, 1)
                    for s in range(2):
                        _, _, LT, Xi, XT, Yb, Lb = sets[s]
                        pe.wait_ge(so_yc.sem, so_yc.next("pe"))
                        for n in range(4):
                            if lv < LEVELS - 1:
                                pe.matmul(bank(s, 1)[:, P * n:P * n + P], XT.chunk(n), Yb.chunk(n), start=True, stop=True)
                            ins = pe.matmul(bank(s, 2)[:, P * n:P * n + P], Yb.chunk(n), XT.chunk(n), start=True, stop=True)
                        ins.then_inc(so_x.sem, 1)
                for s in range(2):
                    h = 2 * hp + s
                    XT = sets[s][4]
                    pe.wait_ge(so_xn.sem, so_xn.next("pe"))
                    for n in range(4):
                        pe.matmul(bank(s, 3)[:, 64 * n:64 * n + 64], XT.chunk(n), vtok[:, n, 64 * h:64 * h + 64], start=True, stop=True)
                        ins = pe.matmul(bank(s, 0)[half(h), P * n:P * n + P], bk[:, n, 64 * h:64 * h + 64], XT.chunk(n), start=True, stop=True)
                    ins.then_inc(so_out.sem, 1)
                    if hp < 3:
                        squares(hp + 1, s)
            pe.wait_ge(so_oc.sem, so_oc.next("pe", 2))

        def solve_act(act):
            for hp in range(4):
                for s in range(2):
                    A, L = sets[s][0], sets[s][1]
                    act.wait_ge(so_arg.sem, so_arg.next("act"))
                    nc.scalar.activation(A.all, A.all, ACT.Exp)
                    nc.scalar.activation(L.all, L.all, ACT.Exp, scale=-1.0).then_inc(so_dec.sem, 1)
                for s in range(2):
                    act.wait_ge(so_t.sem, so_t.next("act"))
                    nc.scalar.activation(sets[s][2].all, bank(s, 3).rearrange("p (a b) -> p a b", a=2), ACT.Copy).then_inc(so_tc.sem, 1)
                for lv in range(1, LEVELS):
                    for s in range(2):
                        act.wait_ge(so_y.sem, so_y.next("act"))
                        nc.scalar.activation(sets[s][5].all, bank(s, 0).rearrange("p (a b) -> p a b", a=2), ACT.Copy).then_inc(so_yc.sem, 1)
                for s in range(2):
                    h = 2 * hp + s
                    act.wait_ge(so_out.sem, so_out.next("act"))
                    nc.scalar.activation(ub[:, :, 64 * h:64 * h + 64], bank(s, 3)[:, 0:256].rearrange("p (n d) -> p n d", n=4), ACT.Copy)
                    nc.scalar.activation(wT[half(h), hp, :], bank(s, 0)[half(h), :], ACT.Copy).then_inc(so_oc.sem, 1)

        def solve_pool(pool, layer):
            for hp in range(4):
                for lv in range(1, LEVELS):
                    for s in range(2):
                        if lv == 1:
                            pool.wait_ge(so_tc.sem, so_tc.next("pool"))
                        if lv == 2:
                            pool.wait_ge(so_xn.sem, so_xn.next("pool"))
                        if lv >= 3:
                            pool.wait_ge(so_y.sem, so_y.next("pool"))
                        LT, Lb = sets[s][2], sets[s][6 if lv % 2 else 0]
                        nc.gpsimd.tensor_tensor(Lb.blocks, LT.blocks, each("levt", P * lv), ALU.mult).then_inc(so_lb.sem, 1)
                so_y.advance("pool", 2 * 2)
                so_xn.advance("pool", 2 * 6)

        def solve_dve(dve):
            Splits.order.append(("solve", 0))
            for hp in range(4):
                for s in range(2):
                    h = 2 * hp + s
                    A, L = sets[s][0], sets[s][1]
                    dve.wait_ge(so_in.sem, so_in.next("dve"))
                    for n in range(4):
                        gam = R4T[:, n, 32 + h:33 + h]
                        g = bank(s, 0)[:, P * n:P * n + P]
                        nc.vector.scalar_tensor_tensor(out=A.chunk(n), in0=g, scalar=gam, in1=C("neg_ge"), op0=ALU.subtract, op1=ALU.add)
                        ins = nc.vector.scalar_tensor_tensor(out=L.chunk(n), in0=g, scalar=gam, in1=C("pos_lt"), op0=ALU.subtract, op1=ALU.add)
                    ins.then_inc(so_arg.sem, 1)
                for s in range(2):
                    h = 2 * hp + s
                    A, L = sets[s][0], sets[s][1]
                    dve.wait_ge(so_dec.sem, so_dec.next("dve"))
                    for n in range(4):
                        ins = nc.vector.scalar_tensor_tensor(out=L.chunk(n), in0=bank(s, 1)[:, P * n:P * n + P], scalar=R4T[:, n, h:h + 1],
                                                             in1=L.chunk(n), op0=ALU.mult, op1=ALU.mult)
                    ins.then_inc(so_L.sem, 1)
                    nc.vector.tensor_tensor(pt_of(h).all, A.all, bank(s, 2).rearrange("p (a b) -> p a b", a=2), ALU.mult)
                for s in range(2):
                    _, L, LT, Xi, XT, _, Lb = sets[s]
                    dve.wait_ge(so_tc.sem, so_tc.next("dve"))
                    nc.vector.tensor_tensor(Xi.blocks, L.blocks, each("lev"), ALU.mult)
                    v_link(dve, nc.vector.tensor_tensor(XT.blocks, LT.blocks, each("levt"), ALU.mult))
                    nc.vector.tensor_tensor(Xi.blocks, each("ident"), Xi.blocks, ALU.subtract)
                    nc.vector.tensor_tensor(XT.blocks, each("ident"), XT.blocks, ALU.subtract).then_inc(so_xn.sem, 1)
                for lv in range(1, LEVELS):
                    for s in range(2):
                        _, _, LT, Xi, XT, _, Lb = sets[s]
                        dve.wait_ge(so_x.sem, so_x.next("dve"))
                        ps1, ps2 = (bank(s, i).rearrange("p (a b) -> p a b", a=2) for i in (1, 2))
                        if lv < LEVELS - 1:
                            nc.vector.tensor_tensor(Xi.all, Xi.all, ps1, ALU.subtract)
                            nc.vector.tensor_tensor(XT.all, XT.all, ps2, ALU.subtract).then_inc(so_xn.sem, 1)
                        else:
                            nc.vector.tensor_tensor(XT.all, XT.all, ps2, ALU.subtract).then_inc(so_xn.sem, 1)

        S = area(11264, 4, P)
        uu = area(11776, 512)
        tS = area(12288, 4, P)
        egx = area(12800, 512)
        gtot = small[:, 64:80].rearrange("p (q n) -> p q n", q=4)
        (re_eg0, re_eg, re_qd, re_gt, re_gtx, re_w, re_u, re_s, re_sn, re_o) = (signal(n) for n in (
            "rec_exp_rows", "rec_exp_spread", "rec_q_decayed", "rec_total_spread", "rec_total_exp", "rec_w_product", "rec_u", "rec_update", "rec_state", "rec_outputs"))

        def rec_pe(pe):
            for p in range(4):
                ins = pe.matmul(PS[:, 0, 4 * p:4 * p + 4], C("selp", P * p)[0:8], de[0:8, P - 1::P], start=True, stop=True)
            ins.then_inc(re_gt.sem, 1)
            pe.wait_ge(re_eg0.sem, re_eg0.next("pe"))
            for p in range(4):
                if p >= 2:
                    pe.wait_ge(re_qd.sem, re_qd.next("pe"))
                pe.matmul(PS[:, 1 + p % 2, :], C("selp", P * p)[0:8], egx[0:8, :], start=True, stop=True).then_inc(re_eg.sem, 1)
            pe.wait_ge(re_qd.sem, re_qd.next("pe", 2))
            pe.wait_ge(re_sn.sem, re_sn.next("pe"))
            for n in range(4):
                cols = slice(P * n, P * n + P)
                for p in range(4):
                    ins = pe.matmul(PS[:, 0, P * p:P * p + P], wT[:, p, cols], S[:, p, :], start=True, stop=True)
                ins.then_inc(re_w.sem, 1)
                for p in range(4):
                    ins = pe.matmul(PS[:, 4 + p, cols], S[:, p, :], qkv[:, p, cols], start=True, stop=False, skip_group_check=True)
                pe.wait_ge(re_u.sem, re_u.next("pe"))
                if n < 3:
                    for p in range(4):
                        ins = pe.matmul(PS[:, 3, P * p:P * p + P], ktok[:, n, P * p:P * p + P], uu[:, P * p:P * p + P], start=True, stop=True)
                    ins.then_inc(re_s.sem, 1)
                for h in range(8):
                    ins = pe.matmul(PS[half(h), 4 + h // 2, cols], uu[:, 64 * h:64 * h + 64], pt_of(h).chunk(n), start=False, stop=True,
                                    skip_group_check=True)
                ins.then_inc(re_o.sem, 1)
                if n < 3:
                    pe.wait_ge(re_sn.sem, re_sn.next("pe"))

        def rec_act(act):
            nc.scalar.activation(egx[0:8, :], de[0:8, :], ACT.Exp).then_inc(re_eg0.sem, 1)
            act.wait_ge(re_gt.sem, re_gt.next("act"))
            nc.scalar.activation(gtot, PS[:, 0, 0:16].rearrange("p (q n) -> p q n", q=4), ACT.Exp).then_inc(re_gtx.sem, 1)

        def rec_dve(dve):
            v_link(dve, nc.vector.memset(S, 0.0))
            for p in range(4):
                dve.wait_ge(re_eg.sem, re_eg.next("dve"))
                nc.vector.tensor_tensor(qkv[:, p, :], qkv[:, p, :], PS[:, 1 + p % 2, :], ALU.mult).then_inc(re_qd.sem, 1)
            dve.wait_ge(re_gtx.sem, re_gtx.next("dve"))
            nc.vector.tensor_copy(tS[:, 0, 0:1], S[:, 0, 0:1]).then_inc(re_sn.sem, 1)
            for n in range(4):
                dve.wait_ge(re_w.sem, re_w.next("dve"))
                if n >= 1:
                    dve.wait_ge(re_o.sem, re_o.next("dve"))
                nc.vector.tensor_tensor(uu, ub[:, n, :], PS[:, 0, :], ALU.subtract).then_inc(re_u.sem, 1)
                if n < 3:
                    dve.wait_ge(re_s.sem, re_s.next("dve"))
                    nc.vector.tensor_tensor(S, S, gtot[:, :, n:n + 1].to_broadcast([P, 4, P]), ALU.mult)
                    v_link(dve, nc.vector.tensor_tensor(tS, PS[:, 3, :].rearrange("p (a b) -> p a b", a=4),
                                                        C("blk64").unsqueeze(1).to_broadcast([P, 4, P]), ALU.mult))
                    nc.vector.tensor_tensor(S, S, tS, ALU.add).then_inc(re_sn.sem, 1)
            dve.wait_ge(re_o.sem, re_o.next("dve"))
            for p in range(4):
                nc.vector.tensor_copy(Y[:, 2 + p, :], PS[:, 4 + p, :])

        gdn_norm = [head_norm([(Y[:, 2 + p, :], Y[:, 2 + p, :], "blk64", 1.0 / 64, "eps2", V("gdn_g", l), zp[:, p, :]) for p in range(4)], SC)
                    for l in range(2)]

        def second_loads(l):
            def fn(act):
                if l == 0:
                    act.dma_start(con2[:, 0:N_SECOND], second_d).then_inc(small_loaded.sem, 16)
                act.dma_start(wsT, sguw_d[l]).then_inc(small_loaded.sem, 16)
                act.dma_start(bs_row[0:1, :], sgub_d[l:l + 1]).then_inc(small_loaded.sem, 16)
                act.dma_start(gup[0:16, :], gup_d[l]).then_inc(small_loaded.sem, 16)
            return fn

        stages = []

        def add(pe=None, act=None, dve=None):
            stages.append((pe, act, dve))

        def add_gemm(tiles, before=None):
            tiles[0]["input_ready"] = (xlo_ready, Fresh.need)
            def act_fn(e):
                if before:
                    before(e)
                gemm_evac(e, "act", tiles)
            add(lambda e: gemm_pe(e, tiles), act_fn, lambda e: gemm_evac(e, "dve", tiles))

        def add_norm(segs, eps, centred, affine, summed=True, before=None):
            summed = summed and not centred

            def dve_fn(e):
                if before:
                    before(e)
                norm_dve(e, segs, centred, summed)
            add(None if summed else lambda e: norm_pe(e, segs, centred),
                lambda e: norm_act(e, segs, eps, centred, affine, summed), dve_fn)
            split_tiles_of(X if centred else H, centred, segs, by_rows=False)

        add(ada_pe, ada_act, ada_dve)
        add_norm(ALL, "eps1", False, modulate(0, 0), summed=False, before=lambda e: split_up_to(e, RAW_SLABS + 3))
        add_gemm(ab_plan())
        add(gates_pe, gates_act, gates_dve)
        add(mlstm_pe, mlstm_act, mlstm_dve)
        add(*mlstm_out)
        add(*qk_norm_b)
        add(rope_b[0], None, rope_b[1])
        add(dup_pe, dup_act, None)
        add(*attn_b)
        add(None, None, split_dve(H, False, ALL))
        split_tiles_of(H, False, ALL, by_rows=True)
        add_gemm(out_plan(0, ALL))
        add_norm(ALL, "eps1", False, modulate(0, 1))
        add_gemm(mlp_plans(0, ALL))
        add_norm(ALL, "eps1", False, modulate(1, 0))
        add_gemm(c_plan())
        add(*qk_norm_c)
        add(rope_c[0], None, rope_c[1])
        add(*attn_c)
        add(None, None, split_dve(H, False, LAT))
        split_tiles_of(H, False, LAT, by_rows=True)
        add_gemm(out_plan(1, LAT))
        add_norm(LAT, "eps1", False, modulate(1, 1))
        add_gemm(mlp_plans(1, LAT))
        add(None, None, split_dve(X, True, LAT))
        split_tiles_of(X, True, LAT, by_rows=True)
        for l in range(2):
            add_gemm(ffn_plans(l), before=second_loads(l))
            add_norm(LAT, "eps2", True, layer_norm_affine("ln1", l))
            add_gemm(in_plan(l))
            add(sgu_pe, sgu_act, lambda e, l=l: sgu_dve(e, l))
            add(lambda e, l=l: gla_pe(e, l), lambda e, l=l: gla_act(e, l), lambda e, l=l: gla_dve(e, l))
            add(*gla_norm[l])
            add(*l2_qk)
            add(lambda e, l=l: rows_pe(e, l), lambda e, l=l: rows_act(e, l), lambda e, l=l: rows_dve(e, l))
            add(solve_pe, solve_act, solve_dve)
            add(rec_pe, rec_act, rec_dve)
            add(*gdn_norm[l])
            add(None, None, split_dve(H, True, LAT))
            split_tiles_of(H, True, LAT, by_rows=True)
            add_gemm(mix_plan())
            add_norm(LAT, "eps2", True, layer_norm_affine("ln2", l))
            add_gemm(ffn_plans(l))
            add_norm(LAT, "eps2", True, layer_norm_affine("ln3", l))

        block = ctx.enter_context(nc.Block())

        @block.tensor
        def _(pe):
            for pe_part, _, _ in stages:
                if pe_part:
                    pe_part(pe)
                end_stage(pe, "pe")

        @block.scalar
        def _(act):
            for _, act_part, _ in stages:
                if act_part:
                    act_part(act)
                end_stage(act, "act")

        @block.vector
        def _(dve):
            for _, _, dve_part in stages:
                if dve_part:
                    dve_part(dve)
                end_stage(dve, "dve")

        @block.gpsimd
        def _(pool):
            for kind, n in Splits.order:
                if kind == "slab":
                    slot = n % RING
                    pool.wait_ge(hi_ready.sem, n - RAW_SLABS + 1)
                    nc.gpsimd.tensor_tensor(ring_lo[:, slot, :, :], ring[:, slot, :, :], ring_hi[:, slot, :, :].bitcast(F32),
                                            ALU.subtract).then_inc(lo_ready.sem, 1)
                elif kind == "input":
                    src, x_hi, x_lo = split_inputs[n]
                    pool.wait_ge(xhi_ready.sem, n + 1)
                    nc.gpsimd.tensor_tensor(x_lo, src, x_hi.bitcast(F32), ALU.subtract).then_inc(xlo_ready.sem, 1)
                else:
                    solve_pool(pool, n)

        @block.sync
        def _(sp):
            sp.dma_start(vec[:], vec_d).then_inc(vec_loaded.sem, 16)
            for n in range(max(Splits.at, -(-Weights.at // SLAB))):
                if n >= RING:
                    used, count = Weights.used[n - RING]
                    sp.wait_ge(used.sem, count)
                sp.dma_start(ring[:, n % RING, :, :].rearrange("p a b -> p (a b)"), w_d[n]).then_inc(slab_loaded[n % RING].sem, 16)
            sp.wait_ge(stage.sem, 3 * len(stages))
            sp.dma_start(out_d.rearrange("(k p) t -> p k t", p=P), X[:, :, CTX:TOK]).then_inc(stored.sem, 16)
            sp.wait_ge(stored.sem, 16)


def kernel(**inputs):
    import concourse.bacc as bacc
    from concourse.bass_utils import run_bass_kernel_spmd as run

    a = {k: np.ascontiguousarray(v) for k, v in inputs.items()}

    def columns(v):
        return v.reshape(-1, P).T

    def rows(v, at):
        out = np.zeros((P, v.shape[0]), np.float32)
        out[at, :] = v.T
        return out

    gb = a["ab_gate_b"][0]
    gate_rows = np.r_[0:4, 32:36]
    packed = dict(
        c=columns(a["c"]), c_ctx=columns(a["c_ctx"]), ada_b=columns(a["ada_b"]), norm1_g=columns(a["norm1_g"]),
        norm2_g=columns(a["norm2_g"]), mlstm_g=columns(a["mlstm_norm_g"]), swa_q=columns(np.tile(a["swa_q_norm_g"][0], 2)),
        swa_k=columns(np.tile(a["swa_k_norm_g"][0], 2)), c_q=columns(a["c_q_norm_g"]), c_k=columns(a["c_k_norm_g"]),
        sink=np.broadcast_to(a["swa_sink"], (P, 8)), gb_i=rows(np.r_[gb[0:4], gb[8:12]][None], gate_rows),
        gb_f=rows(np.r_[gb[4:8], gb[12:16]][None], gate_rows), ln1_g=columns(a["ln1_g_2"]), ln1_b=columns(a["ln1_b_2"]),
        ln2_g=columns(a["ln2_g_2"]), ln2_b=columns(a["ln2_b_2"]), ln3_g=columns(a["ln3_g_2"]), ln3_b=columns(a["ln3_b_2"]),
        sgu_g=columns(a["sgu_ln_g_2"]), sgu_b=columns(a["sgu_ln_b_2"]), conv=columns(a["gdn_conv_w_2"]),
        a_log=rows(a["gdn_a_log_2"], np.arange(8)), dt_b=rows(a["gdn_dt_bias_2"], np.arange(8)),
        gdn_g=np.tile(a["gdn_norm_g_2"], (1, 2)).T, gla_gb=columns(a["gla_gate_b_2"]), gla_g=np.tile(a["gla_norm_g_2"], (1, 2)).T,
        eps1=np.full((P, 1), EPS1), eps2=np.full((P, 1), EPS2), epsl=np.full((P, 1), EPSL), one=np.ones((P, 1)))
    vec = np.concatenate([np.asarray(packed[n], np.float32) for n, _ in VECS], 1)
    assert vec.shape == (P, NVEC)

    def spread(w, pieces):
        out = np.zeros((w.shape[0], P), w.dtype)
        for c, n, at in pieces:
            out[:, at:at + n] = w[:, c:c + n]
        return out

    ab = a["ab_w_in"][0]
    mats = dict(ada0=a["ada_w"][0], ada1=a["ada_w"][1], ab=ab, gi=spread(ab, [(2048, 4, 0), (2056, 4, 32)]),
                gf=spread(ab, [(2052, 4, 0), (2060, 4, 32)]), abo=a["ab_w_out"][0], cw=a["c_w_in"][0], co=a["c_w_out"][0])
    for l in range(2):
        w = a["w_in_2"][l]
        mats.update({f"m1_{l}": a["mlp_w1"][l], f"m2_{l}": a["mlp_w2"][l], f"in{l}": w, f"be{l}": spread(w, [(2560, 8, 0)]),
                     f"de{l}": spread(w, [(2568, 8, 0)]), f"gl{l}": spread(w, [(3344, 16, 0)]), f"out{l}": a["w_out_2"][l],
                     f"f1_{l}": a["ffn1_w1_2"][l], f"f3_{l}": a["ffn1_w3_2"][l], f"f2_{l}": a["ffn1_w2_2"][l],
                     f"g1_{l}": a["ffn2_w1_2"][l], f"g3_{l}": a["ffn2_w3_2"][l], f"g2_{l}": a["ffn2_w2_2"][l]})
    w_all = np.zeros((N_SLABS, P, SLAB * P), np.float32)
    for i, (name, k, c, n) in enumerate(stream()):
        w_all[i // SLAB, :, (i % SLAB) * P:(i % SLAB) * P + P] = mats[name][k * P:k * P + P, c:c + P]

    shared, first, second = consts()
    arrays = dict(
        xT=np.concatenate([a["ctx"][0], a["x"][0]], 0).T, vec=vec, shared=shared, first=first, second=second,
        gup=a["gla_gate_up_2"], sguw=a["sgu_w_2"].transpose(0, 3, 1, 2), sgub=a["sgu_b_2"].reshape(2, 512), weights=w_all)
    nc = bacc.Bacc("TRN2", target_bir_lowering=False, num_devices=1)
    ins, args = {}, []
    for name, arr in arrays.items():
        arr = np.ascontiguousarray(arr)
        ins[name + "_dram"] = arr
        args.append(nc.dram_tensor(name + "_dram", arr.shape, F32, kind="ExternalInput").ap())
    out = nc.dram_tensor("out_dram", (D, SEQ), F32, kind="ExternalOutput").ap()
    program(nc, *args, out)
    got = run(nc, [ins], core_ids=[0]).results[0]["out_dram"]
    return np.ascontiguousarray(got.T)[None]
```
